# Optimizing a Trainium2 kernel written in Bass

```python
import numpy as np
import jax, jax.numpy as jnp
from jax import lax

D_MODEL = 1024
BATCH = 1
SEQ = 512
DEPTH = 1

CHUNK = 64
HEAD_DIM = 64
N_HEADS_SB = 8
N_HEADS_CA = 8
D_SB = N_HEADS_SB * HEAD_DIM
D_CA = N_HEADS_CA * HEAD_DIM
D_MIX = D_SB + D_CA
QUERY_BLOCK = 128
LEFT_CHUNKS = 8
BAND = (LEFT_CHUNKS + 1) * CHUNK
REL_CLIP = 128
N_GROUPS = 4
EXPERTS_PER_GROUP = 8
TOP_K = 2
D_EXPERT = 256
LN_EPS = 1e-5
DEEPNORM_ALPHA = (2.0 * DEPTH) ** 0.25
DEEPNORM_BETA = (8.0 * DEPTH) ** -0.25

kernel_name = "hybrid_stickbreak_chunkrel_hmoe_deepnorm"

def layer_norm(x, g, b):
    xf = x.astype(jnp.float32)
    mu = jnp.mean(xf, axis=-1, keepdims=True)
    var = jnp.mean(jnp.square(xf - mu), axis=-1, keepdims=True)
    return ((xf - mu) * lax.rsqrt(var + LN_EPS)).astype(x.dtype) * g + b

def stick_breaking_attention(q, k, v):
    seq = q.shape[2]
    scale = HEAD_DIM ** -0.5
    outs = []
    for start in range(0, seq, QUERY_BLOCK):
        end = start + QUERY_BLOCK
        qb = q[:, :, start:end]
        kp = k[:, :, :end]
        vp = v[:, :, :end]
        z = jnp.einsum('bhqd,bhkd->bhqk', qb, kp).astype(jnp.float32) * scale
        t_pos = start + jnp.arange(QUERY_BLOCK)[:, None]
        s_pos = jnp.arange(end)[None, :]
        causal = s_pos < t_pos
        log_fail = jnp.where(causal, jax.nn.log_sigmoid(-z), 0.0)
        between = lax.cumsum(log_fail, axis=3, reverse=True) - log_fail
        w = jnp.where(causal, jnp.exp(jax.nn.log_sigmoid(z) + between), 0.0)
        outs.append(jnp.einsum('bhqk,bhkd->bhqd', w.astype(v.dtype), vp))
    return jnp.concatenate(outs, axis=2)

def chunked_rel_attention(q, k, v, rel_bias):
    b, h, s, dh = q.shape
    nc = s // CHUNK
    scale = HEAD_DIM ** -0.5
    qc = q.reshape(b, h, nc, CHUNK, dh)

    def band(t):
        t = t.reshape(b, h, nc, CHUNK, dh)
        tp = jnp.pad(t, ((0, 0), (0, 0), (LEFT_CHUNKS, 0), (0, 0), (0, 0)))
        return jnp.concatenate([tp[:, :, i:i + nc] for i in range(LEFT_CHUNKS + 1)], axis=3)

    kb, vb = band(k), band(v)
    scores = jnp.einsum('bhcqd,bhckd->bhcqk', qc, kb).astype(jnp.float32) * scale
    rel = np.arange(CHUNK)[:, None] + LEFT_CHUNKS * CHUNK - np.arange(BAND)[None, :]
    rel_idx = np.clip(rel, -REL_CLIP, REL_CLIP) + REL_CLIP
    bias = rel_bias[:, rel_idx].astype(jnp.float32)
    chunk_ok = (np.arange(nc)[:, None] - LEFT_CHUNKS + np.arange(LEFT_CHUNKS + 1)[None, :]) >= 0
    key_ok = np.repeat(chunk_ok, CHUNK, axis=1)
    scores = scores + bias[None, :, None]
    scores = jnp.where(key_ok[None, None, :, None, :], scores, -1e30)
    p = jax.nn.softmax(scores, axis=-1)
    out = jnp.einsum('bhcqk,bhckd->bhcqd', p.astype(v.dtype), vb)
    return out.reshape(b, h, s, dh)

def hybrid_mixer(x, w_in, w_out, rel_bias):
    b, s, _ = x.shape
    proj = x @ w_in
    cuts = list(np.cumsum([D_SB, D_SB, D_SB, D_CA, D_CA]))
    qa, ka, va, qc, kc, vc = jnp.split(proj, cuts, axis=-1)

    def heads(t, n):
        return t.reshape(b, s, n, HEAD_DIM).transpose(0, 2, 1, 3)

    def merge(t):
        return t.transpose(0, 2, 1, 3).reshape(b, s, -1)

    ya = stick_breaking_attention(heads(qa, N_HEADS_SB), heads(ka, N_HEADS_SB), heads(va, N_HEADS_SB))
    yc = chunked_rel_attention(heads(qc, N_HEADS_CA), heads(kc, N_HEADS_CA), heads(vc, N_HEADS_CA), rel_bias)
    y = jnp.concatenate([merge(ya), merge(yc)], axis=-1)
    return y @ w_out

def hierarchical_moe(x, w_group, b_group, w_expert, b_expert, w_gate, w_up, w_down):
    g_logits = (x @ w_group).astype(jnp.float32) + b_group
    g_prob = jax.nn.softmax(g_logits, axis=-1)
    g_gate, g_idx = lax.top_k(g_prob, 1)
    e_logits_all = jnp.einsum('bsd,gde->bsge', x, w_expert).astype(jnp.float32) + b_expert
    e_logits = jnp.take_along_axis(e_logits_all, g_idx[..., None], axis=2)[:, :, 0]
    e_prob = jax.nn.softmax(e_logits, axis=-1)
    e_gate, e_idx = lax.top_k(e_prob, TOP_K)
    e_gate = e_gate / jnp.sum(e_gate, axis=-1, keepdims=True)
    combine = jnp.sum(jax.nn.one_hot(e_idx, EXPERTS_PER_GROUP, dtype=jnp.float32)
                      * e_gate[..., None], axis=2) * g_gate
    group_mask = jax.nn.one_hot(g_idx[..., 0], N_GROUPS, dtype=jnp.float32)
    y = jnp.zeros_like(x)
    for g in range(N_GROUPS):
        cw = (combine * group_mask[..., g:g + 1]).astype(x.dtype)
        hid = jax.nn.silu(jnp.einsum('bsd,edf->bsef', x, w_gate[g])) * jnp.einsum('bsd,edf->bsef', x, w_up[g])
        y = y + jnp.einsum('bsef,efd->bsd', hid * cw[..., None], w_down[g])
    return y

def setup_inputs(seed: int = 0) -> dict:
    key = jax.random.key(seed)
    ks = jax.random.split(key, 16)
    f32 = jnp.float32
    d = D_MODEL
    x = jax.random.normal(ks[0], (BATCH, SEQ, d), f32)
    w_in = jax.random.normal(ks[1], (DEPTH, d, 3 * D_SB + 3 * D_CA), f32) * d ** -0.5
    col_scale = jnp.concatenate([
        jnp.ones((2 * D_SB,), f32), jnp.full((D_SB,), DEEPNORM_BETA, f32),
        jnp.ones((2 * D_CA,), f32), jnp.full((D_CA,), DEEPNORM_BETA, f32)])
    w_in = w_in * col_scale
    w_out = jax.random.normal(ks[2], (DEPTH, D_MIX, d), f32) * D_MIX ** -0.5 * DEEPNORM_BETA
    rel_bias = jax.random.normal(ks[3], (DEPTH, N_HEADS_CA, 2 * REL_CLIP + 1), f32) * 0.1
    ln1_g = 1.0 + 0.01 * jax.random.normal(ks[4], (DEPTH, d), f32)
    ln1_b = 0.01 * jax.random.normal(ks[5], (DEPTH, d), f32)
    w_group = jax.random.normal(ks[6], (DEPTH, d, N_GROUPS), f32) * d ** -0.5
    b_group = 0.01 * jax.random.normal(ks[7], (DEPTH, N_GROUPS), f32)
    w_expert = jax.random.normal(ks[8], (DEPTH, N_GROUPS, d, EXPERTS_PER_GROUP), f32) * d ** -0.5
    b_expert = 0.01 * jax.random.normal(ks[9], (DEPTH, N_GROUPS, EXPERTS_PER_GROUP), f32)
    eshape = (DEPTH, N_GROUPS, EXPERTS_PER_GROUP)
    w_gate = jax.random.normal(ks[10], eshape + (d, D_EXPERT), f32) * d ** -0.5
    w_up = jax.random.normal(ks[11], eshape + (d, D_EXPERT), f32) * d ** -0.5 * DEEPNORM_BETA
    w_down = jax.random.normal(ks[12], eshape + (D_EXPERT, d), f32) * D_EXPERT ** -0.5 * DEEPNORM_BETA
    ln2_g = 1.0 + 0.01 * jax.random.normal(ks[13], (DEPTH, d), f32)
    ln2_b = 0.01 * jax.random.normal(ks[14], (DEPTH, d), f32)
    return {"x": x, "w_in": w_in, "w_out": w_out, "rel_bias": rel_bias,
            "ln1_g": ln1_g, "ln1_b": ln1_b, "w_group": w_group, "b_group": b_group,
            "w_expert": w_expert, "b_expert": b_expert, "w_gate": w_gate, "w_up": w_up,
            "w_down": w_down, "ln2_g": ln2_g, "ln2_b": ln2_b}

def reference(x, w_in, w_out, rel_bias, ln1_g, ln1_b, w_group, b_group, w_expert, b_expert,
              w_gate, w_up, w_down, ln2_g, ln2_b):
    for l in range(DEPTH):
        mix = hybrid_mixer(x, w_in[l], w_out[l], rel_bias[l])
        x = layer_norm(DEEPNORM_ALPHA * x + mix, ln1_g[l], ln1_b[l])
        ffn = hierarchical_moe(x, w_group[l], b_group[l], w_expert[l], b_expert[l],
                               w_gate[l], w_up[l], w_down[l])
        x = layer_norm(DEEPNORM_ALPHA * x + ffn, ln2_g[l], ln2_b[l])
    return x


_drawn_inputs = setup_inputs


def setup_inputs(seed=0):
    import zlib

    import numpy as np

    out = dict(_drawn_inputs(seed))
    spreads = {}
    factors = {'rel_bias': 8.0,
     'ln1_g': 4.53,
     'ln1_b': 4.153,
     'b_group': 8.0,
     'b_expert': 8.0,
     'ln2_g': 5.481,
     'ln2_b': 5.744}
    for name, (base, spread) in spreads.items():
        noise = np.random.default_rng([zlib.crc32(name.encode()), seed]).standard_normal(out[name].shape)
        drawn = base * np.exp(spread * noise) if base else spread * noise
        out[name] = __import__('jax').numpy.asarray(drawn.astype(out[name].dtype))
    for name, factor in factors.items():
        out[name] = (out[name] * factor).astype(out[name].dtype)
    return out
```

```python
from contextlib import ExitStack

import concourse.bass as bass
from concourse import mybir

F32 = mybir.dt.float32
F32R = mybir.dt.float32r
BF16 = mybir.dt.bfloat16
I32 = mybir.dt.int32
ALU = mybir.AluOpType
ACT = mybir.ActivationFunctionType
AX = mybir.AxisListType

P = 128
NEG = -1e30
BIG = 64.0
FAR = 1 << 20
LN_EPS = 1e-5
ds = bass.ds


def build(nc, x, w_in, w_out, rel_bias, ln1_g, ln1_b, w_group, b_group, w_expert, b_expert,
          w_gate, w_up, w_down, ln2_g, ln2_b, out):
    DEPTH, D, _ = w_in.shape
    S = x.shape[1]
    T = S // P
    KD = D // P
    DH = 64
    D_SB = D // 2
    PAIRS_SB = D_SB // P
    PAIRS = D // P
    HEADS_CA = rel_bias.shape[1]
    REL = rel_bias.shape[2]
    CLIP = REL // 2
    G = w_group.shape[2]
    EG = w_expert.shape[3]
    E = G * EG
    F = w_gate.shape[4]
    FB = F // P
    ALPHA = (2.0 * DEPTH) ** 0.25
    SCALE = DH ** -0.5
    SLOTS = 64
    RING = 6
    EXPERT_ROUNDS = E // RING
    assert DEPTH == 1 and T == 4 and KD == 8 and E == 32 and FB == 2 and PAIRS_SB == 4

    CHUNKS_V = KD
    FIRST_QK = CHUNKS_V
    FIRST_OUT = FIRST_QK + 2 * PAIRS
    CHUNKS = FIRST_OUT + KD
    UNITS = T
    W = [(b + 1) * P for b in range(T)]

    h_dram = nc.dram_tensor("h_rows", [S, D], F32).ap()
    y_dram = nc.dram_tensor("expert_rows", [2 * S, D], F32).ap()
    table = nc.dram_tensor("rank_table", [S * E, 2], I32).ap()
    LINE = S + P - 1
    line_dram = nc.dram_tensor("bias_lines", [HEADS_CA, P, LINE], F32).ap()

    with ExitStack() as ctx:
        base = (nc.sbuf_base + 63) // 64 * 64
        top = [base]

        def at(name, shape, dt, offset):
            return nc.alloc_sbuf_tensor_at(name, shape, dt, offset=offset)

        def size(shape, dt):
            n = 2 if dt == BF16 else 4
            for d in shape[1:]:
                n *= d
            return (n + 31) // 32 * 32

        def sb(name, shape, dt=F32):
            t = at(name, shape, dt, top[0])
            top[0] += size(shape, dt)
            return t

        def sem(name):
            return ctx.enter_context(nc.semaphore(name))

        hx = sb("hx", [P, T, D])
        gain = sb("gain", [P, D])
        shift = sb("shift", [P, D])
        w_route = sb("w_route", [P, KD, G + E])
        b_route = sb("b_route", [P, G + E])
        ident = sb("ident", [P, P])
        eps = sb("eps", [P, 1])
        stats = sb("stats", [P, T, 2, 6])
        moments = sb("moments", [P, T, 2])
        rstd = sb("rstd", [P, T, 2])
        y_rows = sb("y_rows", [P, 2, D])
        xeT = sb("xeT", [P, 2, KD, SLOTS])
        silu_g = sb("silu_g", [P, 2, FB, SLOTS])
        hid = sb("hid", [P, 2, FB, SLOTS])
        idx_all = sb("idx_all", [SLOTS, E, 2], I32)
        idx_get = sb("idx_get", [SLOTS, 2, 2], I32)
        idx_put = sb("idx_put", [SLOTS, 2, 2], I32)
        iota_i = sb("iota_i", [P, E], I32)
        iota_f = sb("iota_f", [P, E])
        iota_big = sb("iota_big", [P, EG])
        before = sb("before", [P, P], BF16)
        ones = sb("ones", [P, P], BF16)
        pair_ids = sb("pair_ids", [P, 2, T, 2], I32)
        logit = sb("logit", [P, T, G + E])
        gmax = sb("gmax", [P, T])
        gdif = sb("gdif", [P, T, G])
        gexp = sb("gexp", [P, T, G])
        gsum = sb("gsum", [P, T])
        gprob = sb("gprob", [P, T])
        same = sb("same", [P, T, EG])
        cand = sb("cand", [P, T, EG])
        gidx = sb("gidx", [P, T])
        gone = sb("gone", [P, T, G])
        picked = sb("picked", [P, T, G, EG])
        elog = sb("elog", [P, T, EG])
        emax = sb("emax", [P, 2, T])
        eidx = sb("eidx", [P, 2, T])
        eone = sb("eone", [P, T, EG])
        edif = sb("edif", [P, T])
        eexp = sb("eexp", [P, T])
        esum = sb("esum", [P, T])
        einv = sb("einv", [P, T])
        gate = sb("gate", [P, 2, T])
        expert = sb("expert", [P, 2, T])
        chosen = sb("chosen", [P, 2, T, E])
        chosen_b = sb("chosen_b", [P, T, E], BF16)
        ranked = sb("ranked", [P, 2, T, E])
        rank = sb("rank", [P, 2, T])
        row_i = sb("row_i", [P, 2, T], I32)
        count_i = sb("count_i", [P, 1], I32)
        count_f = sb("count_f", [P, 1])
        passes_i = sb("passes_i", [P, 1], I32)
        near = sb("near", [P, 2, 2])
        nnear = sb("nnear", [P, 2, 2])
        psumd = sb("psumd", [P, 2, 2])
        pinv = sb("pinv", [P, 2, 2])
        arena = (top[0] + 63) // 64 * 64

        top[0] = arena
        xT_hi = sb("xT_hi", [P, KD, S], F32R)
        xT_lo = sb("xT_lo", [P, KD, S], F32R)
        values = sb("values", [P, T, D])
        bias = sb("bias", [P, HEADS_CA, S])
        Z = sb("Z", [P, 2, 2, S])
        L = sb("L", [P, 2, 2, S])
        R = sb("R", [P, 2, 2, S])
        wT = sb("wT", [P, 2, S])
        qT = sb("qT", [P, S])
        kT = sb("kT", [P, S])
        y_pair = sb("y_pair", [P, T, P])
        raw = sb("raw", [P, 2, D])
        w_hi = sb("w_hi", [P, 2, D], F32R)
        w_lo = sb("w_lo", [P, 2, D], F32R)
        mask_off = top[0]
        yT_hi = sb("yT_hi", [P, KD, S], F32R)
        yT_lo = sb("yT_lo", [P, KD, S], F32R)
        arena_end = top[0]
        causal = sb("causal", [P, S])
        line = at("line", [HEADS_CA, LINE], F32, mask_off)
        rb = at("rb", [HEADS_CA, REL], F32, mask_off + 4096)
        far_rows = at("far_rows", [P, S * E * 2 // P], I32, mask_off + 8192)
        assert top[0] <= nc.sbuf_usable_end, (top[0], nc.sbuf_usable_end)

        SLOT = (2 * KD * F + FB * D) * 4
        gate_w, up_w, down_w = [], [], []
        for r in range(RING):
            o = arena + r * SLOT
            gate_w.append(at(f"gate_w{r}", [P, KD, F], F32, o))
            up_w.append(at(f"up_w{r}", [P, KD, F], F32, o + KD * F * 4))
            down_w.append(at(f"down_w{r}", [P, FB, D], F32, o + 2 * KD * F * 4))
        xe_off = arena + RING * SLOT
        xe = at("xe", [SLOTS, 2, D], F32, xe_off)
        assert xe_off + 2 * D * 4 <= arena_end
        hT = at("hT", [P, KD, S], F32, arena_end - KD * S * 4)
        first_y = at("first_y", [P, T, D], F32, arena)
        second_y = at("second_y", [P, T, D], F32, arena + T * D * 4)

        bank = ctx.enter_context(nc.psum_tensor("bank", [P, 8, 512], F32))
        SC = bank[:, 0:2, :]
        TR = [bank[:, 2, :], bank[:, 3, :]]
        PQ, PK = bank[:, 4, :], bank[:, 5, :]
        PV = bank[:, 6, 0:P]
        YT = bank[:, 7, :]
        XE = bank[:, 6, :].rearrange("p (c s) -> p c s", c=KD)
        GU = [bank[:, 4 + i, 0:2 * FB * SLOTS].rearrange("p (j s) -> p j s", s=SLOTS) for i in range(2)]
        DN = [bank[0:SLOTS, 2 * i:2 * i + 2, :] for i in range(2)]

        s_x = [sem(f"s_x{t}") for t in range(T)]
        s_ident = sem("s_ident")
        s_const = sem("s_const")
        s_mask = sem("s_mask")
        s_rb = sem("s_rb"); s_line = sem("s_line"); s_line_out = sem("s_line_out"); s_bias = sem("s_bias")
        s_bmask = sem("s_bmask")
        s_xT = sem("s_xT"); s_xTh = sem("s_xTh"); s_xTl = sem("s_xTl")
        s_raw = [sem("s_raw0"), sem("s_raw1")]
        s_hi = sem("s_hi"); s_lo = sem("s_lo"); s_vused = sem("s_vused"); s_oused = sem("s_oused")
        s_vout_d = sem("s_vout_d"); s_vout_a = sem("s_vout_a")
        s_pq = sem("s_pq"); s_pk = sem("s_pk"); s_q = sem("s_q"); s_k = sem("s_k")
        s_sc = sem("s_sc")
        s_z = sem("s_z")
        s_abs = sem("s_abs"); s_exp = sem("s_exp"); s_ln = sem("s_ln"); s_relu = sem("s_relu")
        s_scan = sem("s_scan"); s_wlog = sem("s_wlog")
        s_p = sem("s_p")
        s_mx = sem("s_mx"); s_nmx = sem("s_nmx"); s_inv = sem("s_inv")
        s_tr = [sem("s_tr0"), sem("s_tr1")]
        s_wT = [sem("s_wT0"), sem("s_wT1")]
        s_pv = [sem("s_pv0"), sem("s_pv1")]
        s_y = sem("s_y"); s_yt = sem("s_yt"); s_yTh = sem("s_yTh"); s_yTl = sem("s_yTl")
        s_mix = sem("s_mix")
        s_vec = sem("s_vec"); s_vec2 = sem("s_vec2")
        s_res = sem("s_res"); s_stat = sem("s_stat"); s_mom = sem("s_mom"); s_sqrt = sem("s_sqrt")
        s_rstd = sem("s_rstd"); s_nrm = sem("s_nrm"); s_gain = sem("s_gain"); s_h = sem("s_h")
        s_hst = sem("s_hst"); s_hT = sem("s_hT"); s_hTe = sem("s_hTe"); s_logit = sem("s_logit")
        s_rw = sem("s_rw")
        s_far = sem("s_far"); s_blank = sem("s_blank")
        s_route = sem("s_route"); s_gexp = sem("s_gexp"); s_eexp = sem("s_eexp")
        s_onehot = sem("s_onehot"); s_rank = sem("s_rank"); s_rows = sem("s_rows"); s_passes = sem("s_passes")
        s_table = sem("s_table"); s_idx = sem("s_idx")
        s_xe0 = sem("s_xe0")
        s_w = [sem(f"s_w{r}") for r in range(RING)]
        s_gidx = sem("s_gidx"); s_pidx = sem("s_pidx")
        s_get = [sem("s_get0"), sem("s_get1")]
        s_xeT = sem("s_xeT"); s_xeTs = sem("s_xeTs")
        s_gu = sem("s_gu"); s_silu = sem("s_silu"); s_hid = sem("s_hid")
        s_dn = sem("s_dn"); s_ya = sem("s_ya"); s_yd = sem("s_yd")
        s_put = sem("s_put"); s_all = sem("s_all")
        s_first = [sem(f"s_first{t}") for t in range(T)]
        s_scaled = sem("s_scaled")
        s_res2 = sem("s_res2"); s_out = sem("s_out")
        s_oidx = sem("s_oidx")

        x_v = x.rearrange("a (t p) d -> p (a t) d", p=P)
        out_v = out.rearrange("a (t p) d -> p (a t) d", p=P)
        h_v = h_dram.rearrange("(t p) d -> p t d", p=P)
        w_in_v = w_in[0].rearrange("(c p) n -> p c n", p=P)
        w_out_v = w_out[0].rearrange("(c p) n -> p c n", p=P)
        w_gate_v = w_gate.rearrange("l g e (p c) f -> p (l g e) (c f)", p=P)
        w_up_v = w_up.rearrange("l g e (p c) f -> p (l g e) (c f)", p=P)
        w_down_v = w_down.rearrange("l g e (b p) d -> p (l g e) b d", p=P)
        table_v = table.rearrange("(r e) c -> r e c", e=E)
        y_v = y_dram.rearrange("(k t p) d -> p k t d", k=2, p=P)

        def everywhere(row, n):
            return bass.AP(row.tensor, row.offset, [[0, P], [1, n]])

        def unit(i, o):
            return UNITS * i + o

        ORDER = list(range(T - 1, -1, -1))
        CREDIT_TR, CREDIT_WT, CREDIT_PV, CREDIT_Y = 2, 1, 1, 1
        CREDIT_WLOG, CREDIT_SCAN, CREDIT_Z = 2, 2, 1

        block = ctx.enter_context(nc.Block())

        @block.sync
        def _(sp):
            for t in range(T):
                sp.dma_start(hx[:, t, :], x_v[:, t, :]).then_inc(s_x[t], 16)

            def chunk_free(n):
                if not isinstance(n, int) or n >= 2:
                    sp.wait_ge(s_hi, n - 1)
                    sp.wait_ge(s_lo, n - 1)

            for n in range(CHUNKS_V):
                chunk_free(n)
                src = bass.AP(w_in_v.tensor, w_in_v[:, n, 2 * D_SB:2 * D_SB + 1].offset,
                              [[3 * D, P], [3 * D_SB, 2], [1, D_SB]])
                sp.dma_start(raw[:, n % 2, :].rearrange("p (g j) -> p g j", g=2), src).then_inc(s_raw[n % 2], 16)
                if n == 1:
                    sp.dma_start(rb[:, :], rel_bias[0]).then_inc(s_rb, 16)
                if n == 4:
                    sp.wait_ge(s_line, 2)
                    sp.dma_start(line_dram, line[:, :].unsqueeze(1).broadcast_to([HEADS_CA, P, LINE])).then_inc(s_line_out, 16)
                    sp.wait_ge(s_far, 1)
                    sp.dma_start(table.rearrange("(p r) c -> p (r c)", p=P), far_rows[:, :]).then_inc(s_blank, 16)
                if n == 6:
                    sp.wait_ge(s_line_out, 16)
                    sp.dma_start(bias[:, :, :], bass.AP(line_dram.tensor, P - 1, [[LINE - 1, P], [P * LINE, HEADS_CA], [1, S]])
                                 ).then_inc(s_bias, 16)
            for first_col, first_pair, pairs in ((0, 0, PAIRS_SB), (3 * D_SB, PAIRS_SB, PAIRS - PAIRS_SB)):
                with sp.Fori(0, pairs) as i:
                    for j in range(2):
                        chunk_free(FIRST_QK + 2 * first_pair + j + 2 * i)
                        sp.nop(nofuse=True)
                        src = w_in_v[:, :, ds(first_col + j * D_SB + P * i, P)]
                        sp.dma_start(raw[:, j, :].rearrange("p (c m) -> p c m", c=KD), src).then_inc(s_raw[j], 16)
                if first_pair == 0:
                    sp.dma_start(gain[:, :], everywhere(ln1_g[0], D)).then_inc(s_vec, 16)
                    sp.dma_start(shift[:, :], everywhere(ln1_b[0], D)).then_inc(s_vec, 16)
                    sp.dma_start(b_route[:, 0:G], everywhere(b_group[0], G)).then_inc(s_rw, 16)
                    sp.dma_start(b_route[:, G:], everywhere(b_expert[0], E)).then_inc(s_rw, 16)
                    with nc.allow_non_contiguous_dma(reason="router weights, once, short rows"):
                        sp.dma_start(w_route[:, :, 0:G], w_group[0].rearrange("(p c) g -> p c g", p=P)
                                     ).then_inc(s_rw, 16)
                        for g in range(G):
                            sp.dma_start(w_route[:, :, G + g * EG:G + (g + 1) * EG],
                                         w_expert[0, g].rearrange("(p c) e -> p c e", p=P)).then_inc(s_rw, 16)
            for n in range(FIRST_OUT, CHUNKS):
                chunk_free(n)
                sp.dma_start(raw[:, n % 2, :], w_out_v[:, n - FIRST_OUT, :]).then_inc(s_raw[n % 2], 16)

            def expert_weights(r, e):
                one = slice(e, e + 1) if isinstance(e, int) else ds(e, 1)
                sp.dma_start(gate_w[r][:, :, :].rearrange("p c f -> p (c f)"),
                             w_gate_v[:, one, :].rearrange("p e n -> p (e n)")).then_inc(s_w[r], 16)
                sp.dma_start(up_w[r][:, :, :].rearrange("p c f -> p (c f)"),
                             w_up_v[:, one, :].rearrange("p e n -> p (e n)")).then_inc(s_w[r], 16)
                sp.dma_start(down_w[r][:, :, :],
                             w_down_v[:, one, :, :].rearrange("p e b d -> p (e b) d")).then_inc(s_w[r], 16)

            sp.wait_ge(s_pk, PAIRS)
            sp.wait_ge(s_pv[1], PAIRS * UNITS + CREDIT_PV)
            sp.wait_ge(s_y, PAIRS * UNITS + CREDIT_Y)
            for r in range(4):
                expert_weights(r, r)
            sp.wait_ge(s_mix, 1)
            expert_weights(4, 4)
            for t in range(T):
                sp.wait_ge(s_h, t + 1)
                sp.dma_start(h_v[:, t, :], hx[:, t, :]).then_inc(s_hst, 16)
            sp.wait_ge(s_logit, 1)
            expert_weights(5, 5)
            sp.dma_start(gain[:, :], everywhere(ln2_g[0], D)).then_inc(s_vec2, 16)
            sp.dma_start(shift[:, :], everywhere(ln2_b[0], D)).then_inc(s_vec2, 16)
            sp.wait_ge(s_table, 16 * 2 * T)
            sp.dma_start(idx_all[:, :, :].rearrange("r e c -> r (e c)"),
                         table_v[0:SLOTS].rearrange("r e c -> r (e c)")).then_inc(s_idx, 16)
            with sp.Fori(1, EXPERT_ROUNDS) as rd:
                for r in range(RING):
                    sp.wait_ge(s_dn, rd * RING + (r - RING + 1))
                    sp.nop(nofuse=True)
                    expert_weights(r, rd * RING + r)
            for e in range(RING * EXPERT_ROUNDS, E):
                sp.wait_ge(s_dn, e - RING + 1)
                expert_weights(e % RING, e)

            sp.wait_ge(s_passes, 1)
            n_passes = sp.value_load(passes_i[0:1, 0:1], min_val=0, max_val=S // SLOTS)
            with sp.If(n_passes > 1):
                with sp.Fori(1, n_passes) as ps:
                    with sp.Fori(0, E) as e:
                        sp.wait_ge(s_dn, E * ps + e)
                        sp.nop(nofuse=True)
                        expert_weights(0, e)
            with sp.Else():
                sp.nop(nofuse=True)

            sp.wait_ge(s_all, 1)
            for t in range(T):
                sp.dma_start(first_y[:, t, :], y_v[:, 0, t, :]).then_inc(s_first[t], 16)
                sp.dma_start(second_y[:, t, :], y_v[:, 1, t, :]).then_inc(s_first[t], 16)
            for t in range(T):
                sp.wait_ge(s_h, T + t + 1)
                sp.dma_start(out_v[:, t, :], hx[:, t, :]).then_inc(s_out, 16)
            sp.wait_ge(s_out, 16 * T)

        @block.gpsimd
        def _(pool):
            pool.memset(ident[:, :], 0.0).then_inc(s_ident, 1)
            pool.wait_ge(s_ident, 1)
            pool.affine_select(out=ident[:, :], in_=ident[:, :], compare_op=ALU.not_equal, fill=1.0, base=0,
                               pattern=[[-1, P]], channel_multiplier=1).then_inc(s_ident, 1)
            pool.memset(far_rows[:, :], FAR).then_inc(s_far, 1)
            pool.memset(causal[:, :], 0.0).then_inc(s_mask, 1)
            pool.wait_ge(s_mask, 1)
            pool.affine_select(out=causal[:, (T - 1) * P:], in_=causal[:, (T - 1) * P:], compare_op=ALU.is_gt,
                               fill=NEG, base=0, pattern=[[-1, P]], channel_multiplier=1).then_inc(s_mask, 1)
            pool.memset(ones[:, :], 1.0).then_inc(s_const, 1)
            pool.iota(iota_i[:, :], pattern=[[1, E]], base=0, channel_multiplier=0).then_inc(s_const, 1)
            pool.iota(pair_ids[:, :, :, 0], pattern=[[0, 2], [P, T]], base=0, channel_multiplier=1).then_inc(s_const, 1)
            pool.iota(pair_ids[:, :, :, 1], pattern=[[S, 2], [P, T]], base=0, channel_multiplier=1).then_inc(s_const, 1)
            pool.memset(eps[:, :], LN_EPS).then_inc(s_const, 1)
            pool.wait_ge(s_const, 5)
            pool.affine_select(out=before[:, :], in_=ones[:, :], compare_op=ALU.is_gt, fill=0.0, base=0,
                               pattern=[[1, P]], channel_multiplier=-1).then_inc(s_const, 1)

            def low_part(n, slot):
                pool.wait_ge(s_hi, n + 1)
                nc.gpsimd.tensor_tensor(w_lo[:, slot, :], raw[:, slot, :], w_hi[:, slot, :].bitcast(F32),
                                        ALU.subtract).then_inc(s_lo, 1)

            for n in range(FIRST_QK + 4):
                low_part(n, n % 2)

            def relu(i, o):
                b = ORDER[o]
                u = unit(i, o)
                pool.wait_ge(s_z, u + 1 + CREDIT_Z)
                pool.wait_ge(s_scan, u + 1)
                pool.nop(nofuse=True)
                nc.gpsimd.tensor_scalar(R[:, b % 2, :, 0:W[b]], Z[:, b % 2, :, 0:W[b]], 0.0, None,
                                        ALU.max).then_inc(s_relu, 1)

            with pool.Fori(0, PAIRS_SB) as i:
                relu(i, 0)
                relu(i, 1)
                relu(i, 2)
                low_part(FIRST_QK + 4 + 2 * i, 0)
                relu(i, 3)
                low_part(FIRST_QK + 5 + 2 * i, 1)
            for n in range(FIRST_QK + 4 + 2 * PAIRS_SB, CHUNKS):
                low_part(n, n % 2)

            def shifted(n):
                t = n % T
                pool.wait_ge(s_gain, n + 1)
                nc.gpsimd.tensor_tensor(hx[:, t, :], hx[:, t, :], shift[:, :], ALU.add).then_inc(s_h, 1)

            pool.wait_ge(s_vec, 32)
            for n in range(T):
                shifted(n)

            pool.wait_ge(s_logit, 1)
            pool.memset(xe[:, :, :], 0.0).then_inc(s_xe0, 1)
            pool.wait_ge(s_rows, 1)
            pool.wait_ge(s_blank, 16)
            for k in range(2):
                for t in range(T):
                    pool.indirect_dma_start(
                        out=table, out_offset=bass.IndirectOffsetOnAxis(ap=row_i[:, k, t:t + 1], axis=0),
                        in_=pair_ids[:, k, t, :], in_offset=None, bounds_check=S * E - 1,
                        oob_is_err=False).then_inc(s_table, 16)
                    pool.wait_ge(s_table, 16 * (T * k + t + 1))
            pool.wait_ge(s_hst, 16 * T)
            pool.wait_ge(s_idx, 16)
            pool.wait_ge(s_xe0, 1)

            def get(q, n, e):
                nc.gpsimd.tensor_copy(idx_get[:, q, :], idx_all[:, e, :] if isinstance(e, int)
                                      else idx_all[:, ds(e, 1), :].rearrange("r e c -> r (e c)")).then_inc(s_gidx, 1)
                pool.wait_ge(s_gidx, n + 1)
                pool.nop(nofuse=True)
                pool.indirect_dma_start(
                    out=xe[:, q, :], out_offset=None, in_=h_dram,
                    in_offset=bass.IndirectOffsetOnAxis(ap=idx_get[:, q, 0:1], axis=0), bounds_check=S - 1,
                    oob_is_err=False).then_inc(s_get[q], 16)

            def put(q, n, e):
                nc.gpsimd.tensor_copy(idx_put[:, q, :], idx_all[:, e, :] if isinstance(e, int)
                                      else idx_all[:, ds(e, 1), :].rearrange("r e c -> r (e c)")).then_inc(s_pidx, 1)
                pool.wait_ge(s_pidx, n + 1)
                pool.wait_ge(s_ya, n + 1)
                pool.wait_ge(s_yd, n + 1)
                pool.nop(nofuse=True)
                pool.indirect_dma_start(
                    out=y_dram, out_offset=bass.IndirectOffsetOnAxis(ap=idx_put[:, q, 1:2], axis=0),
                    in_=y_rows[0:SLOTS, q, :], in_offset=None, bounds_check=2 * S - 1,
                    oob_is_err=False).then_inc(s_put, 16)

            get(0, 0, 0)
            get(1, 1, 1)

            def step(q, n, last=False):
                if isinstance(n, int):
                    if n > 0:
                        pool.wait_ge(s_put, 16 * n)
                else:
                    pool.wait_ge(s_put, 16 * n)
                    pool.nop(nofuse=True)
                put(q, n, n)
                if not last:
                    pool.wait_ge(s_xeT, n + 1)
                    pool.nop(nofuse=True)
                    get(q, n + 2, n + 2)

            step(0, 0)
            step(1, 1)
            with pool.Fori(1, E // 2 - 1) as m:
                step(0, 2 * m)
                step(1, 2 * m + 1)
            step(0, E - 2, last=True)
            step(1, E - 1, last=True)
            pool.wait_ge(s_put, 16 * E)

            pool.wait_ge(s_passes, 1)
            n_passes = pool.value_load(passes_i[0:1, 0:1], min_val=0, max_val=S // SLOTS)
            with pool.If(n_passes > 1):
                with pool.Fori(1, n_passes) as ps:
                    pool.dma_start(idx_all[:, :, :].rearrange("r e c -> r (e c)"),
                                   table_v[ds(SLOTS * ps, SLOTS)].rearrange("r e c -> r (e c)")).then_inc(s_oidx, 16)
                    pool.wait_ge(s_oidx, 16 * ps)
                    pool.nop(nofuse=True)
                    with pool.Fori(0, E) as e:
                        n = E * ps + e
                        get(0, n, e)
                        put(0, n, e)
                        pool.wait_ge(s_put, 16 * n + 16)
                        pool.nop(nofuse=True)
            with pool.Else():
                pool.nop(nofuse=True)
            pool.sem_inc(s_all, 1)
            pool.wait_ge(s_vec2, 32)
            for n in range(T, 2 * T):
                shifted(n)

        @block.scalar
        def _(act):
            nc.scalar.preload_act_table_set("natural_log_exp_and_others")
            act.sem_inc(s_wlog, CREDIT_WLOG)
            act.sem_inc(s_scan, CREDIT_SCAN)
            for h in range(2):
                act.sem_inc(s_tr[h], CREDIT_TR)
                act.sem_inc(s_wT[h], CREDIT_WT)
                act.sem_inc(s_pv[h], CREDIT_PV)
            act.sem_inc(s_y, CREDIT_Y)
            act.sem_inc(s_z, CREDIT_Z)
            act.sem_inc(s_yt, 1)
            act.sem_inc(s_yTl, 1)

            def high_part(n, slot, use, used=None):
                act.wait_ge(s_raw[slot], 16 * use + 16)
                if used is not None:
                    act.wait_ge(*used)
                    act.wait_ge(s_lo, n - 1)
                nc.scalar.activation(w_hi[:, slot, :], raw[:, slot, :], ACT.Copy).then_inc(s_hi, 1)

            high_part(0, 0, 0)
            high_part(1, 1, 0)
            for c in range(KD):
                act.wait_ge(s_xT, c + 1)
                nc.scalar.activation(xT_hi[:, c, :], bank[:, c, :], ACT.Copy).then_inc(s_xTh, 1)
            for n in range(2, CHUNKS_V):
                high_part(n, n % 2, n // 2, (s_vused, n - 1))
            act.wait_ge(s_vused, CHUNKS_V)
            for b in (4, 0, 2, 6):
                nc.scalar.activation(values[:, b % 4, (b // 4) * D_SB:(b // 4 + 1) * D_SB], bank[:, b, :],
                                     ACT.Copy).then_inc(s_vout_a, 1)
            for n in range(CHUNKS_V, FIRST_QK + 2):
                high_part(n, n % 2, n // 2, (s_vused, n - 1))
            high_part(FIRST_QK + 2, 0, FIRST_QK // 2 + 1, (s_pq, 1))
            high_part(FIRST_QK + 3, 1, FIRST_QK // 2 + 1, (s_pk, 1))

            def weights_out(i, o, h=0):
                b, u = ORDER[o], unit(i, o)
                act.wait_ge(s_tr[h], u + 1 + CREDIT_TR)
                act.wait_ge(s_pv[h], u + CREDIT_PV)
                nc.scalar.activation(wT[:, h, 0:W[b]], TR[h][:, 0:W[b]], ACT.Copy).then_inc(s_wT[h], 1)

            def softplus(i, o):
                b, u = ORDER[o], unit(i, o)
                z, l = Z[:, b % 2, :, 0:W[b]], L[:, b % 2, :, 0:W[b]]
                act.wait_ge(s_z, u + 1 + CREDIT_Z)
                act.wait_ge(s_wlog, u + 1)
                nc.scalar.activation(l, z, ACT.Abs).then_inc(s_abs, 1)
                act.wait_ge(s_abs, u + 1)
                nc.scalar.activation(l, l, ACT.Exp, scale=-1.0).then_inc(s_exp, 1)
                act.wait_ge(s_exp, u + 1)
                nc.scalar.activation(l, l, ACT.Ln, bias=1.0).then_inc(s_ln, 1)

            def weights(i, o):
                b, u = ORDER[o], unit(i, o)
                z = Z[:, b % 2, :, 0:W[b]]
                act.wait_ge(s_wlog, u + 1 + CREDIT_WLOG)
                nc.scalar.activation(z, z, ACT.Exp).then_inc(s_p, 1)

            with act.Fori(0, PAIRS_SB) as i:
                softplus(i, 0)
                softplus(i, 1)
                weights(i, 0)
                weights_out(i, 0)
                softplus(i, 2)
                weights(i, 1)
                weights_out(i, 1)
                high_part(FIRST_QK + 4 + 2 * i, 0, FIRST_QK // 2 + 2 + i, (s_pq, i + 2))
                softplus(i, 3)
                weights(i, 2)
                weights_out(i, 2)
                weights(i, 3)
                high_part(FIRST_QK + 5 + 2 * i, 1, FIRST_QK // 2 + 2 + i, (s_pk, i + 2))
                weights_out(i, 3)

            def soft_weights(i, o):
                b, u = ORDER[o], unit(i, o)
                act.wait_ge(s_nmx, u - UNITS * PAIRS_SB + 1)
                for h in range(2):
                    z = Z[:, b % 2, h, 0:W[b]]
                    ins = nc.scalar.activation(z, z, ACT.Exp, bias=nnear[:, b % 2, h:h + 1],
                                               accum_out=psumd[:, b % 2, h:h + 1])
                ins.then_inc(s_p, 1)

            def softmax_pair(i, ahead):
                soft_weights(i, 0)
                soft_weights(i, 1)
                weights_out(i, 0)
                soft_weights(i, 2)
                weights_out(i, 1)
                if ahead:
                    high_part(FIRST_QK + 4 + 2 * i, 0, FIRST_QK // 2 + 2 + i, (s_pq, i + 2))
                soft_weights(i, 3)
                weights_out(i, 2)
                if ahead:
                    high_part(FIRST_QK + 5 + 2 * i, 1, FIRST_QK // 2 + 2 + i, (s_pk, i + 2))
                weights_out(i, 3)

            with act.Fori(PAIRS_SB, PAIRS - 1) as i:
                softmax_pair(i, True)
            softmax_pair(PAIRS - 1, False)
            for n in range(FIRST_OUT + 2, CHUNKS):
                high_part(n, n % 2, n // 2, (s_oused, n - 1 - FIRST_OUT))

            def normalise(n):
                t = n % T
                act.wait_ge(s_mom, n + 1)
                nc.scalar.activation(rstd[:, t, 0:1], moments[:, t, 1:2], ACT.Sqrt, bias=eps[:, 0:1]
                                     ).then_inc(s_sqrt, 1)

            for n in range(T):
                normalise(n)
            for c in range(0, KD, 2):
                act.wait_ge(s_hT, c + 1)
                nc.scalar.activation(hT[:, c, :], bank[:, c, :], ACT.Copy).then_inc(s_hTe, 1)
            act.wait_ge(s_route, 3)
            nc.scalar.activation(gexp[:, :, :], gdif[:, :, :], ACT.Exp).then_inc(s_gexp, 1)
            act.wait_ge(s_eexp, 1)
            nc.scalar.activation(eexp[:, :], edif[:, :], ACT.Exp).then_inc(s_eexp, 1)

            act.wait_ge(s_hst, 16 * T)
            act.wait_ge(s_hT, KD)
            for t in range(T):
                nc.scalar.activation(hx[:, t, :], hx[:, t, :], ACT.Copy, scale=ALPHA).then_inc(s_scaled, 1)

            def step(q, n):
                act.wait_ge(s_gu, n + 1)
                nc.scalar.activation(silu_g[:, q, :, :], GU[q][:, 0:FB, :], ACT.Silu).then_inc(s_silu, 1)
                act.wait_ge(s_dn, n + 1)
                wait_put(act, n)
                nc.scalar.activation(y_rows[0:SLOTS, q, 0:512], DN[q][:, 0, :], ACT.Copy).then_inc(s_ya, 1)

            def wait_put(eng, n):
                if not isinstance(n, int) or n >= 2:
                    eng.wait_ge(s_put, 16 * n - 16)

            act.wait_ge(s_scaled, T)
            step(0, 0)
            step(1, 1)
            with act.Fori(1, E // 2) as m:
                step(0, 2 * m)
                step(1, 2 * m + 1)
            act.wait_ge(s_passes, 1)
            n_passes = act.value_load(passes_i[0:1, 0:1], min_val=0, max_val=S // SLOTS)
            with act.If(n_passes > 1):
                with act.Fori(1, n_passes) as ps:
                    with act.Fori(0, E) as e:
                        step(0, E * ps + e)
            with act.Else():
                act.nop(nofuse=True)
            for n in range(T, 2 * T):
                normalise(n)

        @block.vector
        def _(dve):
            dve.wait_ge(s_rb, 16)
            dve.wait_ge(s_far, 1)
            nc.vector.tensor_copy(line[:, 0:S - 1 - CLIP], rb[:, REL - 1:REL].to_broadcast([HEADS_CA, S - 1 - CLIP])
                                  ).then_inc(s_line, 1)
            nc.vector.tensor_copy(line[:, S - 1 - CLIP:LINE], rb[:, REL - 1:REL - 1 - (LINE - (S - 1 - CLIP)):-1]
                                  ).then_inc(s_line, 1)
            for c in range(KD):
                dve.wait_ge(s_xTh, c + 1)
                nc.vector.tensor_tensor(xT_lo[:, c, :], bank[:, c, :], xT_hi[:, c, :].bitcast(F32),
                                        ALU.subtract).then_inc(s_xTl, 1)
            dve.wait_ge(s_bias, 16)
            nc.vector.memset(bias[0:P // 2, :, S - P // 2:], NEG).then_inc(s_bmask, 1)
            dve.wait_ge(s_const, 2)
            nc.vector.tensor_copy(iota_f[:, :], iota_i[:, :]).then_inc(s_bmask, 1)
            dve.wait_ge(s_bmask, 2)
            nc.vector.tensor_scalar(iota_big[:, :], iota_f[:, 0:EG], BIG, None, ALU.add).then_inc(s_bmask, 1)
            dve.wait_ge(s_vused, CHUNKS_V)
            for b in (5, 1, 3, 7):
                nc.vector.tensor_copy(values[:, b % 4, (b // 4) * D_SB:(b // 4 + 1) * D_SB], bank[:, b, :]
                                      ).then_inc(s_vout_d, 1)

            def q_out(i):
                dve.wait_ge(s_pq, i + 1)
                nc.vector.tensor_scalar(qT[:, :], PQ, SCALE, None, ALU.mult).then_inc(s_q, 1)

            def k_out(i):
                dve.wait_ge(s_pk, i + 1)
                nc.vector.tensor_copy(kT[:, :], PK).then_inc(s_k, 1)

            q_out(0)
            k_out(0)

            def weights_out(i, o, h=1):
                b, u = ORDER[o], unit(i, o)
                dve.wait_ge(s_tr[h], u + 1 + CREDIT_TR)
                dve.wait_ge(s_pv[h], u + CREDIT_PV)
                nc.vector.tensor_copy(wT[:, h, 0:W[b]], TR[h][:, 0:W[b]]).then_inc(s_wT[h], 1)

            def z_free(u):
                dve.wait_ge(s_tr[1], u + 1)

            def masked(i, o):
                b, u = ORDER[o], unit(i, o)
                dve.wait_ge(s_sc, u + 1)
                z_free(u)
                nc.vector.tensor_tensor(Z[:, b % 2, :, 0:W[b]], SC[:, :, 0:W[b]],
                                        causal[:, S - W[b]:].unsqueeze(1).broadcast_to([P, 2, W[b]]),
                                        ALU.add).then_inc(s_z, 1)

            def later_sum(i, o):
                b, u = ORDER[o], unit(i, o)
                dve.wait_ge(s_ln, u + 1)
                dve.wait_ge(s_relu, u + 1)
                for h in range(2):
                    l, r = L[:, b % 2, h, 0:W[b]][:, ::-1], R[:, b % 2, h, 0:W[b]][:, ::-1]
                    ins = nc.vector.tensor_tensor_scan(l, l, r, 0.0, ALU.add, ALU.add)
                ins.then_inc(s_scan, 1)
                dve.wait_ge(s_scan, u + 1 + CREDIT_SCAN)
                z = Z[:, b % 2, :, 0:W[b]]
                nc.vector.tensor_tensor(z, z, L[:, b % 2, :, 0:W[b]], ALU.subtract).then_inc(s_wlog, 1)

            def y_free(i):
                dve.wait_ge(s_yt, i + 1)

            def y_out(i, o):
                b, u = ORDER[o], unit(i, o)
                dve.wait_ge(s_pv[1], u + 1 + CREDIT_PV)
                if o == 0:
                    y_free(i)
                nc.vector.tensor_copy(y_pair[:, b, :], PV).then_inc(s_y, 1)

            def pair_out(i):
                dve.wait_ge(s_yt, i + 2)
                nc.vector.tensor_scalar(yT_hi[:, ds(i, 1), :].rearrange("p c s -> p (c s)"), YT, 1.0, None,
                                        ALU.mult).then_inc(s_yTh, 1)
                dve.wait_ge(s_yTh, i + 1)
                nc.vector.tensor_tensor(yT_lo[:, ds(i, 1), :].rearrange("p c s -> p (c s)"), YT,
                                        yT_hi[:, ds(i, 1), :].rearrange("p c s -> p (c s)").bitcast(F32),
                                        ALU.subtract).then_inc(s_yTl, 1)

            dve.wait_ge(s_mask, 2)
            dve.wait_ge(s_line_out, 16)
            dve.wait_ge(s_blank, 16)
            with dve.Fori(0, PAIRS_SB) as i:
                masked(i, 0)
                masked(i, 1)
                later_sum(i, 0)
                weights_out(i, 0)
                y_out(i, 0)
                masked(i, 2)
                later_sum(i, 1)
                weights_out(i, 1)
                y_out(i, 1)
                masked(i, 3)
                q_out(i + 1)
                later_sum(i, 2)
                later_sum(i, 3)
                k_out(i + 1)
                weights_out(i, 2)
                y_out(i, 2)
                weights_out(i, 3)
                y_out(i, 3)
                pair_out(i)

            first_u = UNITS * PAIRS_SB

            def biased(i, o):
                b, u = ORDER[o], unit(i, o)
                dve.wait_ge(s_sc, u + 1)
                z_free(u)
                heads = bias[:, ds(2 * i - 2 * PAIRS_SB, 2), S - W[b]:]
                nc.vector.tensor_tensor(Z[:, b % 2, :, 0:W[b]], SC[:, :, 0:W[b]], heads, ALU.add).then_inc(s_z, 1)
                dve.wait_ge(s_z, u + 1 + CREDIT_Z)
                nc.vector.tensor_reduce(near[:, b % 2, :], Z[:, b % 2, :, 0:W[b]], AX.X, ALU.max).then_inc(s_mx, 1)
                dve.wait_ge(s_mx, u - first_u + 1)
                nc.vector.tensor_scalar(nnear[:, b % 2, :], near[:, b % 2, :], -1.0, None, ALU.mult
                                        ).then_inc(s_nmx, 1)

            def inverse(i, o):
                b, u = ORDER[o], unit(i, o)
                dve.wait_ge(s_p, u + 1)
                nc.vector.reciprocal(pinv[:, b % 2, :], psumd[:, b % 2, :]).then_inc(s_inv, 1)

            def soft_y_out(i, o):
                b, u = ORDER[o], unit(i, o)
                dve.wait_ge(s_pv[1], u + 1 + CREDIT_PV)
                dve.wait_ge(s_inv, u - first_u + 1)
                if o == 0:
                    y_free(i)
                nc.vector.tensor_tensor(y_pair[:, b, :].rearrange("p (h d) -> p h d", h=2),
                                        PV.rearrange("p (h d) -> p h d", h=2),
                                        pinv[:, b % 2, :].unsqueeze(2).broadcast_to([P, 2, DH]),
                                        ALU.mult).then_inc(s_y, 1)

            def softmax_pair(i, ahead):
                biased(i, 0)
                biased(i, 1)
                inverse(i, 0)
                weights_out(i, 0)
                soft_y_out(i, 0)
                biased(i, 2)
                inverse(i, 1)
                weights_out(i, 1)
                soft_y_out(i, 1)
                biased(i, 3)
                if ahead:
                    q_out(i + 1)
                inverse(i, 2)
                if ahead:
                    k_out(i + 1)
                weights_out(i, 2)
                soft_y_out(i, 2)
                inverse(i, 3)
                weights_out(i, 3)
                soft_y_out(i, 3)
                pair_out(i)

            dve.wait_ge(s_bmask, 3)
            with dve.Fori(PAIRS_SB, PAIRS - 1) as i:
                softmax_pair(i, True)
            softmax_pair(PAIRS - 1, False)

            def layer_norm(t, n):
                for j in range(2):
                    ins = nc.vector.bn_stats(stats[:, t, j, :], hx[:, t, j * 512:(j + 1) * 512])
                ins.then_inc(s_stat, 1)
                dve.wait_ge(s_stat, n + 1)
                nc.vector.bn_aggr(moments[:, t, :], stats[:, t, :, :].rearrange("p a b -> p (a b)")
                                  ).then_inc(s_mom, 1)

            def scaled(t, n):
                dve.wait_ge(s_sqrt, n + 1)
                nc.vector.reciprocal(rstd[:, t, 1:2], rstd[:, t, 0:1]).then_inc(s_rstd, 1)
                dve.wait_ge(s_rstd, n + 1)
                nc.vector.tensor_scalar(hx[:, t, :], hx[:, t, :], moments[:, t, 0:1], rstd[:, t, 1:2],
                                        ALU.subtract, ALU.mult).then_inc(s_nrm, 1)
                dve.wait_ge(s_nrm, n + 1)
                nc.vector.tensor_tensor(hx[:, t, :], hx[:, t, :], gain[:, :], ALU.mult).then_inc(s_gain, 1)

            dve.wait_ge(s_mix, 1)
            dve.wait_ge(s_vec, 32)
            for t in range(T):
                nc.vector.scalar_tensor_tensor(out=hx[:, t, :], in0=hx[:, t, :], scalar=ALPHA,
                                               in1=bank[:, 2 * t:2 * t + 2, :].rearrange("p b n -> p (b n)"),
                                               op0=ALU.mult, op1=ALU.add).then_inc(s_res, 1)
            for t in range(T):
                dve.wait_ge(s_res, t + 1)
                layer_norm(t, t)
            for t in range(T):
                scaled(t, t)

            for c in range(1, KD, 2):
                dve.wait_ge(s_hT, c + 1)
                nc.vector.tensor_copy(hT[:, c, :], bank[:, c, :]).then_inc(s_hTe, 1)

            steps = [0]

            def then(ins):
                steps[0] += 1
                ins.then_inc(s_route, 1)
                dve.wait_ge(s_route, steps[0])

            def across(a, n):
                return a.unsqueeze(2).broadcast_to([P, T, n])

            def iota(n):
                return iota_f[:, 0:n].unsqueeze(1).broadcast_to([P, T, n])

            def first_max(values_, best, index, n):
                then(nc.vector.tensor_tensor(same[:, :, 0:n], values_, across(best, n), ALU.is_equal))
                then(nc.vector.scalar_tensor_tensor(
                    out=cand[:, :, 0:n], in0=same[:, :, 0:n], scalar=-BIG,
                    in1=iota_big[:, 0:n].unsqueeze(1).broadcast_to([P, T, n]), op0=ALU.mult, op1=ALU.add))
                then(nc.vector.tensor_reduce(index, cand[:, :, 0:n], AX.X, ALU.min))

            dve.wait_ge(s_logit, 1)
            dve.wait_ge(s_rw, 16 * (3 + G))
            LG = bank[:, 0, 0:T * (G + E)].rearrange("p (t n) -> p t n", t=T)
            then(nc.vector.tensor_tensor(logit[:, :, :], LG, b_route[:, :].unsqueeze(1).broadcast_to([P, T, G + E]),
                                         ALU.add))
            glog = logit[:, :, 0:G]
            then(nc.vector.tensor_reduce(gmax[:, :], glog, AX.X, ALU.max))
            then(nc.vector.tensor_tensor(gdif[:, :, :], glog, across(gmax[:, :], G), ALU.subtract))
            first_max(glog, gmax[:, :], gidx[:, :], G)
            then(nc.vector.tensor_tensor(gone[:, :, :], iota(G), across(gidx[:, :], G), ALU.is_equal))
            then(nc.vector.tensor_tensor(picked[:, :, :, :],
                                         logit[:, :, G:].rearrange("p t (g e) -> p t g e", g=G),
                                         gone[:, :, :].unsqueeze(3).broadcast_to([P, T, G, EG]), ALU.mult))
            then(nc.vector.tensor_reduce(elog[:, :, :], picked[:, :, :, :].rearrange("p t g e -> p t e g"),
                                         AX.X, ALU.add))
            then(nc.vector.tensor_reduce(emax[:, 0, :], elog[:, :, :], AX.X, ALU.max))
            first_max(elog[:, :, :], emax[:, 0, :], eidx[:, 0, :], EG)
            then(nc.vector.tensor_tensor(eone[:, :, :], iota(EG), across(eidx[:, 0, :], EG), ALU.is_equal))
            then(nc.vector.scalar_tensor_tensor(out=elog[:, :, :], in0=eone[:, :, :], scalar=NEG, in1=elog[:, :, :],
                                                op0=ALU.mult, op1=ALU.add))
            then(nc.vector.tensor_reduce(emax[:, 1, :], elog[:, :, :], AX.X, ALU.max))
            first_max(elog[:, :, :], emax[:, 1, :], eidx[:, 1, :], EG)
            nc.vector.tensor_tensor(edif[:, :], emax[:, 1, :], emax[:, 0, :], ALU.subtract).then_inc(s_eexp, 1)
            then(nc.vector.scalar_tensor_tensor(
                out=expert[:, :, :], in0=gidx[:, :].unsqueeze(1).broadcast_to([P, 2, T]), scalar=float(EG),
                in1=eidx[:, :, :], op0=ALU.mult, op1=ALU.add))
            for k in range(2):
                ins = nc.vector.tensor_tensor(chosen[:, k, :, :], iota(E), across(expert[:, k, :], E), ALU.is_equal)
            then(ins)
            nc.vector.tensor_tensor(chosen_b[:, :, :], chosen[:, 0, :, :], chosen[:, 1, :, :], ALU.add
                                    ).then_inc(s_onehot, 1)
            dve.wait_ge(s_gexp, 1)
            then(nc.vector.tensor_reduce(gsum[:, :], gexp[:, :, :], AX.X, ALU.add))
            then(nc.vector.reciprocal(gprob[:, :], gsum[:, :]))
            dve.wait_ge(s_eexp, 2)
            then(nc.vector.tensor_scalar(esum[:, :], eexp[:, :], 1.0, None, ALU.add))
            then(nc.vector.reciprocal(einv[:, :], esum[:, :]))
            then(nc.vector.tensor_tensor(gate[:, 0, :], einv[:, :], gprob[:, :], ALU.mult))
            then(nc.vector.tensor_tensor(gate[:, 1, :], eexp[:, :], gate[:, 0, :], ALU.mult))
            dve.wait_ge(s_rank, 1)
            RK = bank[:, 1, 0:T * E].rearrange("p (t e) -> p t e", t=T)
            for k in range(2):
                ins = nc.vector.tensor_tensor(ranked[:, k, :, :], chosen[:, k, :, :], RK, ALU.mult)
            then(ins)
            then(nc.vector.tensor_reduce(rank[:, :, :], ranked[:, :, :, :], AX.X, ALU.add))
            nc.vector.scalar_tensor_tensor(out=row_i[:, :, :], in0=rank[:, :, :], scalar=float(E),
                                           in1=expert[:, :, :], op0=ALU.mult, op1=ALU.add).then_inc(s_rows, 1)
            then(nc.vector.tensor_reduce(count_f[:, :], bank[:, 2, 0:E], AX.X, ALU.max))
            then(nc.vector.tensor_scalar(count_i[:, :], count_f[:, :], float(SLOTS - 1), None, ALU.add))
            nc.vector.tensor_single_scalar(passes_i[:, :], count_i[:, :], SLOTS.bit_length() - 1,
                                           ALU.logical_shift_right).then_inc(s_passes, 1)

            def step(q, n):
                dve.wait_ge(s_xeT, n + 1)
                wait_gu(n)
                nc.vector.tensor_copy(xeT[:, q, :, :], XE).then_inc(s_xeTs, 1)

            def wait_gu(n):
                if not isinstance(n, int) or n >= 2:
                    dve.wait_ge(s_gu, n - 1)

            def finish(q, n):
                dve.wait_ge(s_silu, n + 1)
                nc.vector.tensor_tensor(hid[:, q, :, :], silu_g[:, q, :, :], GU[q][:, FB:, :], ALU.mult
                                        ).then_inc(s_hid, 1)

            def rows_out(q, n):
                dve.wait_ge(s_dn, n + 1)
                if not isinstance(n, int) or n >= 2:
                    dve.wait_ge(s_put, 16 * n - 16)
                nc.vector.tensor_copy(y_rows[0:SLOTS, q, 512:], DN[q][:, 1, :]).then_inc(s_yd, 1)

            step(0, 0)
            for n in range(2):
                finish(n, n)
                step(1 - n, n + 1)
                rows_out(n, n)
            with dve.Fori(1, E // 2 - 1) as m:
                for q in range(2):
                    finish(q, 2 * m + q)
                    step(1 - q, 2 * m + (q + 1))
                    rows_out(q, 2 * m + q)
            finish(0, E - 2)
            step(1, E - 1)
            rows_out(0, E - 2)
            finish(1, E - 1)
            rows_out(1, E - 1)
            n_passes = dve.value_load(passes_i[0:1, 0:1], min_val=0, max_val=S // SLOTS)
            with dve.If(n_passes > 1):
                with dve.Fori(1, n_passes) as ps:
                    with dve.Fori(0, E) as e:
                        step(0, E * ps + e)
                        finish(0, E * ps + e)
                        rows_out(0, E * ps + e)
            with dve.Else():
                dve.nop(nofuse=True)

            dve.wait_ge(s_scaled, T)
            dve.wait_ge(s_vec2, 32)
            for t in range(T):
                dve.wait_ge(s_first[t], 32)
                for k, rows in enumerate((first_y, second_y)):
                    nc.vector.scalar_tensor_tensor(out=hx[:, t, :], in0=rows[:, t, :], scalar=gate[:, k, t:t + 1],
                                                   in1=hx[:, t, :], op0=ALU.mult, op1=ALU.add).then_inc(s_res2, 1)
                    dve.wait_ge(s_res2, 2 * t + k + 1)
                layer_norm(t, T + t)
                if t >= 1:
                    scaled(t - 1, T + t - 1)
            scaled(T - 1, 2 * T - 1)

        @block.tensor
        def _(pe):
            pe.wait_ge(s_ident, 2)
            for c in range(KD):
                for t in range(T):
                    if c == 0:
                        pe.wait_ge(s_x[t], 16)
                    mm = nc.tensor.transpose(bank[:, c, t * P:(t + 1) * P], hx[:, t, c * P:(c + 1) * P], ident[:, :])
                mm.then_inc(s_xT, 1)

            def split_products(dst, a_hi, a_lo, b_hi, b_lo, start, stop):
                nc.tensor.matmul(dst, a_hi, b_hi, start=start, stop=False)
                nc.tensor.matmul(dst, a_lo, b_hi, start=False, stop=False)
                return nc.tensor.matmul(dst, a_hi, b_lo, start=False, stop=stop)

            for c in range(KD):
                pe.wait_ge(s_lo, c + 1)
                if c == 0:
                    pe.wait_ge(s_xTl, KD)
                for g in range(2):
                    for t in range(T):
                        a = slice(t * P, (t + 1) * P)
                        n = slice(g * D_SB, (g + 1) * D_SB)
                        mm = split_products(bank[:, 4 * g + t, :], xT_hi[:, c, a], xT_lo[:, c, a],
                                            w_hi[:, c % 2, n], w_lo[:, c % 2, n], c == 0, c == KD - 1)
                mm.then_inc(s_vused, 1)

            def project(dst, n, slot, cs, done):
                if cs.start == 0:
                    pe.wait_ge(s_lo, n + 1)
                for c in range(KD)[cs]:
                    w = slice(c * P, (c + 1) * P)
                    mm = split_products(dst, w_hi[:, slot, w], w_lo[:, slot, w], xT_hi[:, c, :], xT_lo[:, c, :],
                                        c == 0, c == KD - 1)
                if cs.stop == KD:
                    mm.then_inc(done, 1)

            HALF = (slice(0, KD // 2), slice(KD // 2, KD))

            def project_q(i, half):
                if half == 0 and not (isinstance(i, int) and i == 0):
                    pe.wait_ge(s_q, i)
                project(PQ, FIRST_QK + 2 * i, 0, HALF[half], s_pq)

            def project_k(i, half):
                if half == 0 and not (isinstance(i, int) and i == 0):
                    pe.wait_ge(s_k, i)
                project(PK, FIRST_QK + 1 + 2 * i, 1, HALF[half], s_pk)

            def scores(i, o):
                b, u = ORDER[o], unit(i, o)
                if o == 0:
                    pe.wait_ge(s_q, i + 1)
                    pe.wait_ge(s_k, i + 1)
                pe.wait_ge(s_z, u + CREDIT_Z)
                for h in range(2):
                    a = slice(h * DH, (h + 1) * DH)
                    mm = nc.tensor.matmul(SC[:, h, 0:W[b]], qT[a, b * P:(b + 1) * P], kT[a, 0:W[b]],
                                          start=True, stop=True)
                mm.then_inc(s_sc, 1)

            def turn(i, o):
                b, u = ORDER[o], unit(i, o)
                pe.wait_ge(s_p, u + 1)
                for h in range(2):
                    pe.wait_ge(s_wT[h], u + CREDIT_WT)
                    for j in range(b + 1):
                        mm = nc.tensor.transpose(TR[h][:, j * P:(j + 1) * P], Z[:, b % 2, h, j * P:(j + 1) * P],
                                                 ident[:, :])
                    mm.then_inc(s_tr[h], 1)

            def combine(i, o):
                b, u = ORDER[o], unit(i, o)
                pe.wait_ge(s_y, u + CREDIT_Y)
                for h in range(2):
                    pe.wait_ge(s_wT[h], u + 1 + CREDIT_WT)
                    for j in range(b + 1):
                        v = values[:, j, ds(i * P + h * DH, DH)] if not isinstance(i, int) else \
                            values[:, j, i * P + h * DH:i * P + (h + 1) * DH]
                        mm = nc.tensor.matmul(PV[:, h * DH:(h + 1) * DH], wT[:, h, j * P:(j + 1) * P], v,
                                              start=(j == 0), stop=(j == b))
                    mm.then_inc(s_pv[h], 1)

            def turn_y(i):
                pe.wait_ge(s_y, unit(i + 1, 0) + CREDIT_Y)
                pe.wait_ge(s_yTl, i + 1)
                for t in range(T):
                    mm = nc.tensor.transpose(YT[:, t * P:(t + 1) * P], y_pair[:, t, :], ident[:, :])
                mm.then_inc(s_yt, 1)

            pe.wait_ge(s_vout_a, 1)
            pe.wait_ge(s_vout_d, 1)
            for half in range(2):
                project_q(0, half)
            for half in range(2):
                project_k(0, half)
            pe.wait_ge(s_vout_a, 4)
            pe.wait_ge(s_vout_d, 4)

            def pair(i, ahead):
                scores(i, 0)
                if ahead:
                    project_q(i + 1, 0)
                scores(i, 1)
                if ahead:
                    project_q(i + 1, 1)
                turn(i, 0)
                combine(i, 0)
                scores(i, 2)
                if ahead:
                    project_k(i + 1, 0)
                turn(i, 1)
                combine(i, 1)
                scores(i, 3)
                if ahead:
                    project_k(i + 1, 1)
                turn(i, 2)
                combine(i, 2)
                turn(i, 3)
                combine(i, 3)
                turn_y(i)

            with pe.Fori(0, PAIRS - 1) as i:
                pair(i, True)
            pair(PAIRS - 1, False)

            for c in range(KD):
                pe.wait_ge(s_lo, FIRST_OUT + c + 1)
                if c == 0:
                    pe.wait_ge(s_yTl, PAIRS + 1)
                for t in range(T):
                    for j in range(2):
                        a = slice(t * P, (t + 1) * P)
                        n = slice(j * 512, (j + 1) * 512)
                        mm = split_products(bank[:, 2 * t + j, :], yT_hi[:, c, a], yT_lo[:, c, a],
                                            w_hi[:, c % 2, n], w_lo[:, c % 2, n], c == 0, c == KD - 1)
                if c < KD - 1:
                    mm.then_inc(s_oused, 1)
                else:
                    mm.then_inc(s_mix, 1)

            pe.wait_ge(s_res, T)
            for c in range(KD):
                for t in range(T):
                    if c == 0:
                        pe.wait_ge(s_h, t + 1)
                    mm = nc.tensor.transpose(bank[:, c, t * P:(t + 1) * P], hx[:, t, c::KD], ident[:, :])
                mm.then_inc(s_hT, 1)
            pe.wait_ge(s_hTe, KD)
            pe.wait_ge(s_rw, 16 * (3 + G))
            for t in range(T):
                for c in range(KD):
                    mm = nc.tensor.matmul(bank[:, 0, t * (G + E):(t + 1) * (G + E)], hT[:, c, t * P:(t + 1) * P],
                                          w_route[:, c, :], start=(c == 0), stop=(c == KD - 1))
            mm.then_inc(s_logit, 1)
            pe.wait_ge(s_onehot, 1)
            pe.wait_ge(s_const, 6)
            for t in range(T):
                for j in range(t + 1):
                    nc.tensor.matmul(bank[:, 1, t * E:(t + 1) * E], before[:, :] if j == t else ones[:, :],
                                     chosen_b[:, j, :], start=(j == 0), stop=(j == t))
            for t in range(T):
                mm = nc.tensor.matmul(bank[:, 2, 0:E], ones[:, :], chosen_b[:, t, :], start=(t == 0),
                                      stop=(t == T - 1))
            mm.then_inc(s_rank, 1)

            def turn_x(q, n, use):
                pe.wait_ge(s_get[q], 16 * use + 16)
                if not isinstance(n, int) or n > 0:
                    pe.wait_ge(s_xeTs, n)
                    pe.nop(nofuse=True)
                for c in range(KD):
                    mm = nc.tensor.transpose(XE[:, c, :], xe[:, q, c::KD], ident[0:SLOTS, 0:SLOTS])
                mm.then_inc(s_xeT, 1)

            def gate_up(q, n, r, use):
                pe.wait_ge(s_w[r], 48 * use + 48)
                pe.wait_ge(s_xeTs, n + 1)
                if not isinstance(n, int) or n >= 2:
                    pe.wait_ge(s_hid, n - 1)
                for w, first in ((gate_w[r], 0), (up_w[r], FB)):
                    for b in range(FB):
                        for c in range(KD):
                            mm = nc.tensor.matmul(GU[q][:, first + b, :], w[:, c, b * P:(b + 1) * P],
                                                  xeT[:, q, c, :], start=(c == 0), stop=(c == KD - 1))
                mm.then_inc(s_gu, 1)

            def down(q, n, r):
                pe.wait_ge(s_hid, n + 1)
                if not isinstance(n, int) or n >= 2:
                    pe.wait_ge(s_ya, n - 1)
                    pe.wait_ge(s_yd, n - 1)
                for j in range(2):
                    for b in range(FB):
                        mm = nc.tensor.matmul(DN[q][:, j, :], hid[:, q, b, :], down_w[r][:, b, j * 512:(j + 1) * 512],
                                              start=(b == 0), stop=(b == FB - 1))
                mm.then_inc(s_dn, 1)
                return mm

            pe.wait_ge(s_passes, 1)
            turn_x(0, 0, 0)

            def expert_step(r, n, q, use, round_, more):
                gate_up(q, n, r, round_)
                if more:
                    turn_x(1 - q, n + 1, use)
                down(q, n, r)

            for r in range(RING):
                expert_step(r, r, r % 2, (r + 1) // 2, 0, True)
            with pe.Fori(1, EXPERT_ROUNDS) as rd:
                for r in range(RING):
                    expert_step(r, rd * RING + r, r % 2, rd * (RING // 2) + (r + 1) // 2, rd, True)
            for n in range(RING * EXPERT_ROUNDS, E):
                expert_step(n % RING, n, n % 2, (n + 1) // 2, n // RING, n + 1 < E)

            n_passes = pe.value_load(passes_i[0:1, 0:1], min_val=0, max_val=S // SLOTS)
            slot0_uses = (E + RING - 1) // RING
            with pe.If(n_passes > 1):
                with pe.Fori(1, n_passes) as ps:
                    with pe.Fori(0, E) as e:
                        n = E * ps + e
                        turn_x(0, n, n - E + E // 2)
                        gate_up(0, n, 0, n - E + slot0_uses)
                        down(0, n, 0)
            with pe.Else():
                pe.nop(nofuse=True)


_INS = ["x", "w_in", "w_out", "rel_bias", "ln1_g", "ln1_b", "w_group", "b_group", "w_expert", "b_expert",
        "w_gate", "w_up", "w_down", "ln2_g", "ln2_b"]


def kernel(**inputs):
    import numpy as np
    import concourse.bacc as bacc
    from concourse.bass_utils import run_bass_kernel_spmd as run

    nc = bacc.Bacc("TRN2", target_bir_lowering=False, num_devices=1)
    arrays, args = {}, []
    for name in _INS:
        a = np.ascontiguousarray(inputs[name])
        arrays[f"in_{name}"] = a
        args.append(nc.dram_tensor(f"in_{name}", a.shape, F32, kind="ExternalInput").ap())
    out = nc.dram_tensor("out", arrays["in_x"].shape, F32, kind="ExternalOutput").ap()
    build(nc, *args, out)
    return run(nc, [arrays], core_ids=[0]).results[0]["out"]
```

```python
from contextlib import ExitStack

import concourse.bass as bass
from concourse import mybir

F32 = mybir.dt.float32
F32R = mybir.dt.float32r
BF16 = mybir.dt.bfloat16
I32 = mybir.dt.int32
ALU = mybir.AluOpType
ACT = mybir.ActivationFunctionType
AX = mybir.AxisListType

P = 128
NEG = -1e30
BIG = 64.0
FAR = 1 << 20
LN_EPS = 1e-5
ds = bass.ds


def build(nc, x, w_in, w_out, rel_bias, ln1_g, ln1_b, w_group, b_group, w_expert, b_expert,
          w_gate, w_up, w_down, ln2_g, ln2_b, out):
    DEPTH, D, _ = w_in.shape
    S = x.shape[1]
    T = S // P
    KD = D // P
    DH = 64
    D_SB = D // 2
    PAIRS_SB = D_SB // P
    PAIRS = D // P
    HEADS_CA = rel_bias.shape[1]
    REL = rel_bias.shape[2]
    CLIP = REL // 2
    G = w_group.shape[2]
    EG = w_expert.shape[3]
    E = G * EG
    F = w_gate.shape[4]
    FB = F // P
    ALPHA = (2.0 * DEPTH) ** 0.25
    SCALE = DH ** -0.5
    SLOTS = 64
    RING = 6
    EXPERT_ROUNDS = E // RING
    assert DEPTH == 1 and T == 4 and KD == 8 and E == 32 and FB == 2 and PAIRS_SB == 4

    CHUNKS_V = KD
    FIRST_QK = CHUNKS_V
    FIRST_OUT = FIRST_QK + 2 * PAIRS
    CHUNKS = FIRST_OUT + KD
    UNITS = T
    W = [(b + 1) * P for b in range(T)]

    h_dram = nc.dram_tensor("h_rows", [S, D], F32).ap()
    y_dram = nc.dram_tensor("expert_rows", [2 * S, D], F32).ap()
    LINE = S + P - 1
    line_dram = nc.dram_tensor("bias_lines", [HEADS_CA, P, LINE], F32).ap()

    with ExitStack() as ctx:
        base = (nc.sbuf_base + 63) // 64 * 64
        top = [base]

        def at(name, shape, dt, offset):
            return nc.alloc_sbuf_tensor_at(name, shape, dt, offset=offset)

        def size(shape, dt):
            n = 2 if dt == BF16 else 4
            for d in shape[1:]:
                n *= d
            return (n + 31) // 32 * 32

        def sb(name, shape, dt=F32):
            t = at(name, shape, dt, top[0])
            top[0] += size(shape, dt)
            return t

        def sem(name):
            return ctx.enter_context(nc.semaphore(name))

        hx = sb("hx", [P, T, D])
        gain = sb("gain", [P, D])
        shift = sb("shift", [P, D])
        w_route = sb("w_route", [P, KD, G + E])
        b_route = sb("b_route", [P, G + E])
        ident = sb("ident", [P, P])
        eps = sb("eps", [P, 1])
        row_sum = sb("row_sum", [P, 2 * T])
        nmean = sb("nmean", [P, 2 * T])
        row_sq = sb("row_sq", [P, 2 * T])
        std = sb("std", [P, 2 * T])
        rstd = sb("rstd", [P, 2 * T])
        y_rows_off = top[0]
        y_rows = sb("y_rows", [P, 2, D])
        squares = at("squares", [P, 2, D], F32, y_rows_off)
        xeT = sb("xeT", [P, 2, KD, SLOTS])
        silu_g = sb("silu_g", [P, 2, FB, SLOTS])
        hid = sb("hid", [P, 2, FB, SLOTS])
        idx_all = sb("idx_all", [SLOTS, 2, E], I32)
        empty = sb("empty", [SLOTS, 2, E])
        idx_get = sb("idx_get", [SLOTS, 2], I32)
        idx_put = sb("idx_put", [SLOTS, 2], I32)
        iota_i = sb("iota_i", [P, SLOTS], I32)
        iota_f = sb("iota_f", [P, SLOTS])
        iota_big = sb("iota_big", [P, EG])
        before = sb("before", [P, P], BF16)
        ones = sb("ones", [P, P], BF16)
        ids_i = sb("ids_i", [P, 2, T, 2], I32)
        ids_f = sb("ids_f", [P, 2, T, 2])
        ids_at = sb("ids_at", [P, 2 * T, 2, E])
        logit = sb("logit", [P, T, G + E])
        gmax = sb("gmax", [P, T])
        gdif = sb("gdif", [P, T, G])
        gexp = sb("gexp", [P, T, G])
        gsum = sb("gsum", [P, T])
        gprob = sb("gprob", [P, T])
        same = sb("same", [P, T, EG])
        cand = sb("cand", [P, T, EG])
        gidx = sb("gidx", [P, T])
        gone = sb("gone", [P, T, G])
        picked = sb("picked", [P, T, G, EG])
        elog = sb("elog", [P, T, EG])
        emax = sb("emax", [P, 2, T])
        eidx = sb("eidx", [P, 2, T])
        eone = sb("eone", [P, T, EG])
        edif = sb("edif", [P, T])
        eexp = sb("eexp", [P, T])
        esum = sb("esum", [P, T])
        einv = sb("einv", [P, T])
        gate = sb("gate", [P, 2, T])
        expert = sb("expert", [P, 2, T])
        chosen = sb("chosen", [P, 2, T, E])
        chosen_b = sb("chosen_b", [P, T, E], BF16)
        ranked = at("ranked", [P, 2, T, E], F32, y_rows_off)
        rank = sb("rank", [P, 2, T])
        count_i = sb("count_i", [P, 1], I32)
        count_f = sb("count_f", [P, 1])
        passes_i = sb("passes_i", [P, 1], I32)
        near = sb("near", [P, 2, 2])
        nnear = sb("nnear", [P, 2, 2])
        psumd = sb("psumd", [P, 2, 2])
        pinv = sb("pinv", [P, UNITS, 2])
        arena = (top[0] + 63) // 64 * 64

        top[0] = arena
        xT_hi = sb("xT_hi", [P, KD, S], F32R)
        xT_lo = sb("xT_lo", [P, KD, S], F32R)
        values = sb("values", [P, T, D])
        bias = sb("bias", [P, HEADS_CA, S])
        Z = sb("Z", [P, 2, 2, S])
        L = sb("L", [P, 2, 2, S])
        R = sb("R", [P, 2, S])
        wT = sb("wT", [P, 2, S])
        q_both = sb("q_both", [P, 2, S], F32R)
        k_hi = sb("k_hi", [P, 2, S], F32R)
        k_lo = sb("k_lo", [P, 2, S], F32R)
        y_pair = sb("y_pair", [P, T, P])
        raw = sb("raw", [P, 2, D])
        w_hi = sb("w_hi", [P, 2, D], F32R)
        w_lo = sb("w_lo", [P, 2, D], F32R)
        mask_off = top[0]
        yT_hi = sb("yT_hi", [P, KD, S], F32R)
        yT_lo = sb("yT_lo", [P, KD, S], F32R)
        arena_end = top[0]
        causal_off = top[0]
        causal = sb("causal", [P, S])
        at_rank = at("at_rank", [P, 2 * T, SLOTS], F32, causal_off)
        line = at("line", [HEADS_CA, LINE], F32, mask_off)
        rb = at("rb", [HEADS_CA, REL], F32, mask_off + 4096)
        assert top[0] <= nc.sbuf_usable_end, (top[0], nc.sbuf_usable_end)

        SLOT = (2 * KD * F + FB * D) * 4
        gate_w, up_w, down_w = [], [], []
        for r in range(RING):
            o = arena + r * SLOT
            gate_w.append(at(f"gate_w{r}", [P, KD, F], F32, o))
            up_w.append(at(f"up_w{r}", [P, KD, F], F32, o + KD * F * 4))
            down_w.append(at(f"down_w{r}", [P, FB, D], F32, o + 2 * KD * F * 4))
        xe_off = arena + RING * SLOT
        xe = at("xe", [SLOTS, 2, D], F32, xe_off)
        assert xe_off + 2 * D * 4 <= arena_end
        hT = at("hT", [P, KD, S], F32, arena_end - KD * S * 4)
        first_y = at("first_y", [P, T, D], F32, arena)
        second_y = at("second_y", [P, T, D], F32, arena + T * D * 4)

        bank = ctx.enter_context(nc.psum_tensor("bank", [P, 8, 512], F32))
        SC = bank[:, 0:2, :]
        TR = [bank[:, 2, :], bank[:, 3, :]]
        PQ, PK = bank[:, 4, :], bank[:, 5, :]
        PV = bank[:, 6, 0:P]
        YT = bank[:, 7, :]
        XE = bank[:, 6, :].rearrange("p (c s) -> p c s", c=KD)
        GU = [bank[:, 4 + i, 0:2 * FB * SLOTS].rearrange("p (j s) -> p j s", s=SLOTS) for i in range(2)]
        DN = [bank[0:SLOTS, 2 * i:2 * i + 2, :] for i in range(2)]

        s_x = [sem(f"s_x{t}") for t in range(T)]
        s_ident = sem("s_ident")
        s_const = sem("s_const")
        s_mask = sem("s_mask")
        s_rb = sem("s_rb"); s_line = sem("s_line"); s_line_out = sem("s_line_out"); s_bias = sem("s_bias")
        s_bmask = sem("s_bmask")
        s_xT = sem("s_xT"); s_xTh = sem("s_xTh"); s_xTl = sem("s_xTl")
        s_raw = [sem("s_raw0"), sem("s_raw1")]
        s_hi = sem("s_hi"); s_lo = sem("s_lo"); s_vused = sem("s_vused"); s_oused = sem("s_oused")
        s_vout_d = sem("s_vout_d"); s_vout_a = sem("s_vout_a")
        s_pq = sem("s_pq"); s_pk = sem("s_pk"); s_q = sem("s_q"); s_k = sem("s_k")
        s_qhi = sem("s_qhi"); s_khi = sem("s_khi")
        s_sc = sem("s_sc")
        s_z = sem("s_z")
        s_abs = sem("s_abs"); s_exp = sem("s_exp"); s_ln = sem("s_ln"); s_relu = sem("s_relu")
        s_scan = sem("s_scan"); s_wlog = sem("s_wlog")
        s_p = sem("s_p")
        s_mx = sem("s_mx"); s_nmx = sem("s_nmx"); s_inv = sem("s_inv")
        s_tr = [sem("s_tr0"), sem("s_tr1")]
        s_wT = [sem("s_wT0"), sem("s_wT1")]
        s_pv = [sem("s_pv0"), sem("s_pv1")]
        s_y = sem("s_y"); s_yt = sem("s_yt"); s_yTh = sem("s_yTh"); s_yTl = sem("s_yTl")
        s_mix = sem("s_mix")
        s_vec = sem("s_vec"); s_vec2 = sem("s_vec2")
        s_res = sem("s_res"); s_mean = sem("s_mean"); s_centred = sem("s_centred"); s_sq = sem("s_sq")
        s_sqrt = sem("s_sqrt"); s_rstd = sem("s_rstd"); s_gain = sem("s_gain"); s_h = sem("s_h")
        s_hst = sem("s_hst"); s_hT = sem("s_hT"); s_hTe_act = sem("s_hTe_act"); s_hTe_dve = sem("s_hTe_dve"); s_logit = sem("s_logit")
        s_rw = sem("s_rw")
        s_route = sem("s_route"); s_gexp = sem("s_gexp"); s_eexp = sem("s_eexp")
        s_onehot = sem("s_onehot"); s_rank = sem("s_rank"); s_passes = sem("s_passes")
        s_slots = sem("s_slots"); s_empty = sem("s_empty"); s_lower = sem("s_lower"); s_slotted = sem("s_slotted"); s_idx = sem("s_idx")
        s_xe0 = sem("s_xe0")
        s_w = [sem(f"s_w{r}") for r in range(RING)]
        s_gidx = sem("s_gidx"); s_pidx = sem("s_pidx")
        s_get = [sem("s_get0"), sem("s_get1")]
        s_xeT = sem("s_xeT"); s_xeTs = sem("s_xeTs")
        s_gu = sem("s_gu"); s_silu = sem("s_silu"); s_hid = sem("s_hid")
        s_dn = sem("s_dn"); s_ya = sem("s_ya"); s_yd = sem("s_yd")
        s_put = [sem("s_put0"), sem("s_put1")]; s_all = sem("s_all")
        s_first = [sem(f"s_first{t}") for t in range(T)]
        s_scaled = sem("s_scaled")
        s_res1 = sem("s_res1"); s_out = sem("s_out")

        x_v = x.rearrange("a (t p) d -> p (a t) d", p=P)
        out_v = out.rearrange("a (t p) d -> p (a t) d", p=P)
        h_v = h_dram.rearrange("(t p) d -> p t d", p=P)
        w_in_v = w_in[0].rearrange("(c p) n -> p c n", p=P)
        w_out_v = w_out[0].rearrange("(c p) n -> p c n", p=P)
        w_gate_v = w_gate.rearrange("l g e (p c) f -> p (l g e) (c f)", p=P)
        w_up_v = w_up.rearrange("l g e (p c) f -> p (l g e) (c f)", p=P)
        w_down_v = w_down.rearrange("l g e (b p) d -> p (l g e) b d", p=P)
        y_v = y_dram.rearrange("(k t p) d -> p k t d", k=2, p=P)

        def everywhere(row, n):
            return bass.AP(row.tensor, row.offset, [[0, P], [1, n]])

        def unit(i, o):
            return UNITS * i + o

        ORDER = list(range(T - 1, -1, -1))
        CREDIT_TR, CREDIT_WT, CREDIT_PV, CREDIT_Y = 2, 1, 1, 1
        CREDIT_WLOG, CREDIT_SCAN, CREDIT_Z = 2, 1, 1

        block = ctx.enter_context(nc.Block())

        @block.sync
        def _(sp):
            for t in range(T):
                sp.dma_start(hx[:, t, :], x_v[:, t, :]).then_inc(s_x[t], 16)

            def chunk_free(n):
                if not isinstance(n, int) or n >= 2:
                    sp.wait_ge(s_hi, n - 1)
                    sp.wait_ge(s_lo, n - 1)

            for n in range(CHUNKS_V):
                chunk_free(n)
                src = bass.AP(w_in_v.tensor, w_in_v[:, n, 2 * D_SB:2 * D_SB + 1].offset,
                              [[3 * D, P], [3 * D_SB, 2], [1, D_SB]])
                sp.dma_start(raw[:, n % 2, :].rearrange("p (g j) -> p g j", g=2), src).then_inc(s_raw[n % 2], 16)
                if n == 1:
                    sp.dma_start(rb[:, :], rel_bias[0]).then_inc(s_rb, 16)
                if n == 4:
                    sp.wait_ge(s_line, 2)
                    sp.dma_start(line_dram, line[:, :].unsqueeze(1).broadcast_to([HEADS_CA, P, LINE])).then_inc(s_line_out, 16)
                if n == 6:
                    sp.wait_ge(s_line_out, 16)
                    sp.dma_start(bias[:, :, :], bass.AP(line_dram.tensor, P - 1, [[LINE - 1, P], [P * LINE, HEADS_CA], [1, S]])
                                 ).then_inc(s_bias, 16)
            for first_col, first_pair, pairs in ((0, 0, PAIRS_SB), (3 * D_SB, PAIRS_SB, PAIRS - PAIRS_SB)):
                with sp.Fori(0, pairs) as i:
                    for j in range(2):
                        chunk_free(FIRST_QK + 2 * first_pair + j + 2 * i)
                        sp.nop(nofuse=True)
                        src = w_in_v[:, :, ds(first_col + j * D_SB + P * i, P)]
                        sp.dma_start(raw[:, j, :].rearrange("p (c m) -> p c m", c=KD), src).then_inc(s_raw[j], 16)
                if first_pair == 0:
                    sp.dma_start(gain[:, :], everywhere(ln1_g[0], D)).then_inc(s_vec, 16)
                    sp.dma_start(shift[:, :], everywhere(ln1_b[0], D)).then_inc(s_vec, 16)
                    sp.dma_start(b_route[:, 0:G], everywhere(b_group[0], G)).then_inc(s_rw, 16)
                    sp.dma_start(b_route[:, G:], everywhere(b_expert[0], E)).then_inc(s_rw, 16)
                    with nc.allow_non_contiguous_dma(reason="router weights, once, short rows"):
                        sp.dma_start(w_route[:, :, 0:G], w_group[0].rearrange("(p c) g -> p c g", p=P)
                                     ).then_inc(s_rw, 16)
                        for g in range(G):
                            sp.dma_start(w_route[:, :, G + g * EG:G + (g + 1) * EG],
                                         w_expert[0, g].rearrange("(p c) e -> p c e", p=P)).then_inc(s_rw, 16)
            for n in range(FIRST_OUT, CHUNKS):
                chunk_free(n)
                sp.dma_start(raw[:, n % 2, :], w_out_v[:, n - FIRST_OUT, :]).then_inc(s_raw[n % 2], 16)

            def expert_weights(r, e):
                one = slice(e, e + 1) if isinstance(e, int) else ds(e, 1)
                sp.dma_start(gate_w[r][:, :, :].rearrange("p c f -> p (c f)"),
                             w_gate_v[:, one, :].rearrange("p e n -> p (e n)")).then_inc(s_w[r], 16)
                sp.dma_start(up_w[r][:, :, :].rearrange("p c f -> p (c f)"),
                             w_up_v[:, one, :].rearrange("p e n -> p (e n)")).then_inc(s_w[r], 16)
                sp.dma_start(down_w[r][:, :, :],
                             w_down_v[:, one, :, :].rearrange("p e b d -> p (e b) d")).then_inc(s_w[r], 16)

            sp.wait_ge(s_pk, PAIRS)
            sp.wait_ge(s_pv[1], PAIRS * UNITS + CREDIT_PV)
            sp.wait_ge(s_y, PAIRS * UNITS + CREDIT_Y)
            for r in range(4):
                expert_weights(r, r)
            sp.wait_ge(s_mix, T)
            expert_weights(4, 4)
            for t in range(T):
                sp.wait_ge(s_h, t + 1)
                sp.dma_start(h_v[:, t, :], hx[:, t, :]).then_inc(s_hst, 16)
            sp.wait_ge(s_logit, T)
            expert_weights(5, 5)
            sp.dma_start(gain[:, :], everywhere(ln2_g[0], D)).then_inc(s_vec2, 16)
            sp.dma_start(shift[:, :], everywhere(ln2_b[0], D)).then_inc(s_vec2, 16)
            with sp.Fori(1, EXPERT_ROUNDS) as rd:
                for r in range(RING):
                    sp.wait_ge(s_dn, rd * RING + (r - RING + 1))
                    sp.nop(nofuse=True)
                    expert_weights(r, rd * RING + r)
            for e in range(RING * EXPERT_ROUNDS, E):
                sp.wait_ge(s_dn, e - RING + 1)
                expert_weights(e % RING, e)

            sp.wait_ge(s_passes, 1)
            n_passes = sp.value_load(passes_i[0:1, 0:1], min_val=0, max_val=S // SLOTS)
            with sp.If(n_passes > 1):
                with sp.Fori(1, n_passes) as ps:
                    with sp.Fori(0, E) as e:
                        sp.wait_ge(s_dn, E * ps + e)
                        sp.nop(nofuse=True)
                        expert_weights(0, e)
            with sp.Else():
                sp.nop(nofuse=True)

            sp.wait_ge(s_all, 1)
            for t in range(T):
                sp.dma_start(first_y[:, t, :], y_v[:, 0, t, :]).then_inc(s_first[t], 16)
                sp.dma_start(second_y[:, t, :], y_v[:, 1, t, :]).then_inc(s_first[t], 16)
            for t in range(T):
                sp.wait_ge(s_h, T + t + 1)
                sp.dma_start(out_v[:, t, :], hx[:, t, :]).then_inc(s_out, 16)
            sp.wait_ge(s_out, 16 * T)

        @block.gpsimd
        def _(pool):
            pool.memset(ident[:, :], 0.0).then_inc(s_ident, 1)
            pool.wait_ge(s_ident, 1)
            pool.affine_select(out=ident[:, :], in_=ident[:, :], compare_op=ALU.not_equal, fill=1.0, base=0,
                               pattern=[[-1, P]], channel_multiplier=1).then_inc(s_ident, 1)
            pool.memset(causal[:, :], 0.0).then_inc(s_mask, 1)
            pool.wait_ge(s_mask, 1)
            pool.affine_select(out=causal[:, (T - 1) * P:], in_=causal[:, (T - 1) * P:], compare_op=ALU.is_gt,
                               fill=NEG, base=0, pattern=[[-1, P]], channel_multiplier=1).then_inc(s_mask, 1)
            pool.memset(ones[:, :], 1.0).then_inc(s_const, 1)
            pool.iota(iota_i[:, :], pattern=[[1, SLOTS]], base=0, channel_multiplier=0).then_inc(s_const, 1)
            pool.iota(ids_i[:, :, :, 0], pattern=[[0, 2], [P, T]], base=1, channel_multiplier=1).then_inc(s_const, 1)
            pool.iota(ids_i[:, :, :, 1], pattern=[[S, 2], [P, T]], base=1, channel_multiplier=1).then_inc(s_const, 1)
            pool.memset(eps[:, :], LN_EPS).then_inc(s_const, 1)
            pool.wait_ge(s_const, 5)
            pool.affine_select(out=before[:, :], in_=ones[:, :], compare_op=ALU.is_gt, fill=0.0, base=0,
                               pattern=[[1, P]], channel_multiplier=-1).then_inc(s_const, 1)

            def low_part(n, slot):
                pool.wait_ge(s_hi, n + 1)
                nc.gpsimd.tensor_tensor(w_lo[:, slot, :], raw[:, slot, :], w_hi[:, slot, :].bitcast(F32),
                                        ALU.subtract).then_inc(s_lo, 1)

            for n in range(FIRST_QK + 4):
                low_part(n, n % 2)

            def relu(i, o):
                b = ORDER[o]
                u = unit(i, o)
                pool.wait_ge(s_z, u + 1 + CREDIT_Z)
                pool.wait_ge(s_scan, u + CREDIT_SCAN)
                pool.nop(nofuse=True)
                nc.gpsimd.tensor_scalar(R[:, :, 0:W[b]], Z[:, b % 2, :, 0:W[b]], 0.0, None,
                                        ALU.max).then_inc(s_relu, 1)

            with pool.Fori(0, PAIRS_SB) as i:
                relu(i, 0)
                relu(i, 1)
                relu(i, 2)
                low_part(FIRST_QK + 4 + 2 * i, 0)
                relu(i, 3)
                low_part(FIRST_QK + 5 + 2 * i, 1)
            for n in range(FIRST_QK + 4 + 2 * PAIRS_SB, CHUNKS):
                low_part(n, n % 2)

            def shifted(n):
                t = n % T
                pool.wait_ge(s_gain, n + 1)
                nc.gpsimd.tensor_tensor(hx[:, t, :], hx[:, t, :], shift[:, :], ALU.add).then_inc(s_h, 1)

            pool.wait_ge(s_vec, 32)
            for n in range(T):
                shifted(n)

            pool.wait_ge(s_logit, T)
            pool.memset(xe[:, :, :], 0.0).then_inc(s_xe0, 1)
            pool.wait_ge(s_hst, 16 * T)
            pool.wait_ge(s_idx, 1)
            pool.wait_ge(s_xe0, 1)

            def get(q, n, e):
                nc.gpsimd.tensor_copy(idx_get[:, q:q + 1], idx_all[:, 0, ds(e, 1)]).then_inc(s_gidx, 1)
                pool.wait_ge(s_gidx, n + 1)
                pool.nop(nofuse=True)
                pool.indirect_dma_start(
                    out=xe[:, q, :], out_offset=None, in_=h_dram,
                    in_offset=bass.IndirectOffsetOnAxis(ap=idx_get[:, q:q + 1], axis=0), bounds_check=S - 1,
                    oob_is_err=False).then_inc(s_get[q], 16)

            def put(q, n, e):
                nc.gpsimd.tensor_copy(idx_put[:, q:q + 1], idx_all[:, 1, ds(e, 1)]).then_inc(s_pidx, 1)
                pool.wait_ge(s_pidx, n + 1)
                pool.wait_ge(s_ya, n + 1)
                pool.wait_ge(s_yd, n + 1)
                pool.nop(nofuse=True)
                pool.indirect_dma_start(
                    out=y_dram, out_offset=bass.IndirectOffsetOnAxis(ap=idx_put[:, q:q + 1], axis=0),
                    in_=y_rows[0:SLOTS, q, :], in_offset=None, bounds_check=2 * S - 1,
                    oob_is_err=False).then_inc(s_put[q], 16)

            get(0, 0, 0)
            get(1, 1, 1)

            def step(q, n, use, last=False):
                if not last:
                    pool.wait_ge(s_xeT, n + 1)
                    pool.nop(nofuse=True)
                    get(q, n + 2, n + 2)
                if not isinstance(n, int) or n >= 2:
                    pool.wait_ge(s_put[q], 16 * use)
                    pool.nop(nofuse=True)
                put(q, n, n)

            step(0, 0, 0)
            step(1, 1, 0)
            with pool.Fori(1, E // 2 - 1) as m:
                step(0, 2 * m, m)
                step(1, 2 * m + 1, m)
            step(0, E - 2, E // 2 - 1, last=True)
            step(1, E - 1, E // 2 - 1, last=True)
            for q in range(2):
                pool.wait_ge(s_put[q], 16 * (E // 2))

            pool.wait_ge(s_passes, 1)
            n_passes = pool.value_load(passes_i[0:1, 0:1], min_val=0, max_val=S // SLOTS)
            with pool.If(n_passes > 1):
                with pool.Fori(1, n_passes) as ps:
                    pool.wait_ge(s_idx, ps + 1)
                    pool.nop(nofuse=True)
                    with pool.Fori(0, E) as e:
                        n = E * ps + e
                        get(0, n, e)
                        put(0, n, e)
                        pool.wait_ge(s_put[0], 16 * n + (16 - 8 * E))
                        pool.nop(nofuse=True)
            with pool.Else():
                pool.nop(nofuse=True)
            pool.sem_inc(s_all, 1)
            pool.wait_ge(s_vec2, 32)
            for n in range(T, 2 * T):
                shifted(n)

        @block.scalar
        def _(act):
            nc.scalar.preload_act_table_set("natural_log_exp_and_others")
            act.sem_inc(s_wlog, CREDIT_WLOG)
            act.sem_inc(s_scan, CREDIT_SCAN)
            for h in range(2):
                act.sem_inc(s_tr[h], CREDIT_TR)
                act.sem_inc(s_wT[h], CREDIT_WT)
                act.sem_inc(s_pv[h], CREDIT_PV)
            act.sem_inc(s_y, CREDIT_Y)
            act.sem_inc(s_z, CREDIT_Z)
            act.sem_inc(s_yt, 1)
            act.sem_inc(s_yTl, 1)

            def high_part(n, slot, use, used=None):
                act.wait_ge(s_raw[slot], 16 * use + 16)
                if used is not None:
                    act.wait_ge(*used)
                    act.wait_ge(s_lo, n - 1)
                nc.scalar.activation(w_hi[:, slot, :], raw[:, slot, :], ACT.Copy).then_inc(s_hi, 1)

            def turned_x(c):
                act.wait_ge(s_xT, c + 1)
                nc.scalar.activation(xT_hi[:, c, :], bank[:, c, :], ACT.Copy).then_inc(s_xTh, 1)

            for c in range(0, 2):
                turned_x(c)
            high_part(0, 0, 0)
            for c in range(2, 6):
                turned_x(c)
            high_part(1, 1, 0)
            for c in range(6, KD):
                turned_x(c)
            for n in range(2, CHUNKS_V + 1):
                high_part(n, n % 2, n // 2, (s_vused, n - 1))
            act.wait_ge(s_vused, CHUNKS_V)
            for b in (4, 0, 2, 6):
                nc.scalar.activation(values[:, b % 4, (b // 4) * D_SB:(b // 4 + 1) * D_SB], bank[:, b, :],
                                     ACT.Copy).then_inc(s_vout_a, 1)
                if b == 4:
                    high_part(FIRST_QK + 1, 1, FIRST_QK // 2, (s_vused, CHUNKS_V))

            def k_high(i):
                act.wait_ge(s_pk, i + 1)
                if not isinstance(i, int):
                    act.wait_ge(s_sc, unit(i, 0))
                for h in range(2):
                    for half in range(2):
                        ins = nc.scalar.activation(k_hi[half * DH:(half + 1) * DH, h, :],
                                                   PK[h * DH:(h + 1) * DH, :], ACT.Copy)
                ins.then_inc(s_khi, 1)

            high_part(FIRST_QK + 2, 0, FIRST_QK // 2 + 1, (s_pq, 1))
            k_high(0)
            high_part(FIRST_QK + 3, 1, FIRST_QK // 2 + 1, (s_pk, 1))

            def weights_out(i, o, h=0):
                b, u = ORDER[o], unit(i, o)
                act.wait_ge(s_tr[h], u + 1 + CREDIT_TR)
                act.wait_ge(s_pv[h], u + CREDIT_PV)
                nc.scalar.activation(wT[:, h, 0:W[b]], TR[h][:, 0:W[b]], ACT.Copy).then_inc(s_wT[h], 1)

            def softplus(i, o):
                b, u = ORDER[o], unit(i, o)
                z, l = Z[:, b % 2, :, 0:W[b]], L[:, b % 2, :, 0:W[b]]
                act.wait_ge(s_z, u + 1 + CREDIT_Z)
                act.wait_ge(s_wlog, u + 1)
                nc.scalar.activation(l, z, ACT.Abs).then_inc(s_abs, 1)
                act.wait_ge(s_abs, u + 1)
                nc.scalar.activation(l, l, ACT.Exp, scale=-1.0).then_inc(s_exp, 1)
                act.wait_ge(s_exp, u + 1)
                nc.scalar.activation(l, l, ACT.Ln, bias=1.0).then_inc(s_ln, 1)

            def weights(i, o):
                b, u = ORDER[o], unit(i, o)
                z = Z[:, b % 2, :, 0:W[b]]
                act.wait_ge(s_wlog, u + 1 + CREDIT_WLOG)
                nc.scalar.activation(z, z, ACT.Exp).then_inc(s_p, 1)

            with act.Fori(0, PAIRS_SB) as i:
                softplus(i, 0)
                softplus(i, 1)
                weights(i, 0)
                weights_out(i, 0)
                weights(i, 1)
                softplus(i, 2)
                weights_out(i, 1)
                high_part(FIRST_QK + 4 + 2 * i, 0, FIRST_QK // 2 + 2 + i, (s_pq, i + 2))
                softplus(i, 3)
                weights(i, 2)
                k_high(i + 1)
                weights(i, 3)
                weights_out(i, 2)
                weights_out(i, 3)
                high_part(FIRST_QK + 5 + 2 * i, 1, FIRST_QK // 2 + 2 + i, (s_pk, i + 2))

            def soft_weights(i, o):
                b, u = ORDER[o], unit(i, o)
                act.wait_ge(s_nmx, u - UNITS * PAIRS_SB + 1)
                for h in range(2):
                    z = Z[:, b % 2, h, 0:W[b]]
                    ins = nc.scalar.activation(z, z, ACT.Exp, bias=nnear[:, b % 2, h:h + 1],
                                               accum_out=psumd[:, b % 2, h:h + 1])
                ins.then_inc(s_p, 1)

            def softmax_pair(i, ahead):
                soft_weights(i, 0)
                soft_weights(i, 1)
                weights_out(i, 0)
                soft_weights(i, 2)
                weights_out(i, 1)
                if ahead:
                    high_part(FIRST_QK + 4 + 2 * i, 0, FIRST_QK // 2 + 2 + i, (s_pq, i + 2))
                soft_weights(i, 3)
                if ahead:
                    k_high(i + 1)
                weights_out(i, 2)
                weights_out(i, 3)
                if ahead:
                    high_part(FIRST_QK + 5 + 2 * i, 1, FIRST_QK // 2 + 2 + i, (s_pk, i + 2))

            with act.Fori(PAIRS_SB, PAIRS - 1) as i:
                softmax_pair(i, True)
            softmax_pair(PAIRS - 1, False)
            for n in range(FIRST_OUT + 2, CHUNKS):
                high_part(n, n % 2, n // 2, (s_oused, n - 1 - FIRST_OUT))

            def centre(n):
                t = n % T
                act.wait_ge(s_mean, n + 1)
                nc.scalar.activation(hx[:, t, :], hx[:, t, :], ACT.Identity, bias=nmean[:, n:n + 1]
                                     ).then_inc(s_centred, 1)
                act.wait_ge(s_centred, n + 1)
                if n % T >= 2:
                    act.wait_ge(s_sq, n - 1)
                nc.scalar.activation(squares[:, t % 2, :], hx[:, t, :], ACT.Square,
                                     accum_out=row_sq[:, n:n + 1]).then_inc(s_sq, 1)

            def root(n):
                act.wait_ge(s_sq, n + 1)
                nc.scalar.activation(std[:, n:n + 1], row_sq[:, n:n + 1], ACT.Sqrt, bias=eps[:, 0:1], scale=1.0 / D
                                     ).then_inc(s_sqrt, 1)

            def centre_and_root(first):
                for n in range(first, first + T):
                    centre(n)
                    root(n)

            centre_and_root(0)
            for t in range(T):
                act.wait_ge(s_hT, t + 1)
                nc.scalar.activation(hT[:, 0:KD // 2, t * P:(t + 1) * P],
                                     bank[:, 2 * t, :].rearrange("p (c s) -> p c s", c=KD // 2), ACT.Copy
                                     ).then_inc(s_hTe_act, 1)
            act.wait_ge(s_route, 3)
            nc.scalar.activation(gexp[:, :, :], gdif[:, :, :], ACT.Exp).then_inc(s_gexp, 1)
            act.wait_ge(s_eexp, 1)
            nc.scalar.activation(eexp[:, :], edif[:, :], ACT.Exp).then_inc(s_eexp, 1)

            act.wait_ge(s_hst, 16 * T)
            act.wait_ge(s_hT, T)
            for t in range(T):
                nc.scalar.activation(hx[:, t, :], hx[:, t, :], ACT.Copy, scale=ALPHA).then_inc(s_scaled, 1)

            def step(q, n, put_uses):
                act.wait_ge(s_gu, n + 1)
                nc.scalar.activation(silu_g[:, q, :, :], GU[q][:, 0:FB, :], ACT.Silu).then_inc(s_silu, 1)
                act.wait_ge(s_dn, n + 1)
                if not isinstance(n, int) or n >= 2:
                    act.wait_ge(s_put[q], 16 * put_uses)
                nc.scalar.activation(y_rows[0:SLOTS, q, 0:512], DN[q][:, 0, :], ACT.Copy).then_inc(s_ya, 1)

            act.wait_ge(s_scaled, T)
            step(0, 0, 0)
            step(1, 1, 0)
            with act.Fori(1, E // 2) as m:
                step(0, 2 * m, m)
                step(1, 2 * m + 1, m)
            act.wait_ge(s_passes, 1)
            n_passes = act.value_load(passes_i[0:1, 0:1], min_val=0, max_val=S // SLOTS)
            with act.If(n_passes > 1):
                with act.Fori(1, n_passes) as ps:
                    with act.Fori(0, E) as e:
                        step(0, E * ps + e, E * ps + e + (-E // 2))
            with act.Else():
                act.nop(nofuse=True)
            centre_and_root(T)

        @block.vector
        def _(dve):
            dve.wait_ge(s_rb, 16)
            nc.vector.tensor_copy(line[:, 0:S - 1 - CLIP], rb[:, REL - 1:REL].to_broadcast([HEADS_CA, S - 1 - CLIP])
                                  ).then_inc(s_line, 1)
            nc.vector.tensor_copy(line[:, S - 1 - CLIP:LINE], rb[:, REL - 1:REL - 1 - (LINE - (S - 1 - CLIP)):-1]
                                  ).then_inc(s_line, 1)
            for c in range(KD):
                dve.wait_ge(s_xTh, c + 1)
                nc.vector.tensor_tensor(xT_lo[:, c, :], bank[:, c, :], xT_hi[:, c, :].bitcast(F32),
                                        ALU.subtract).then_inc(s_xTl, 1)
            dve.wait_ge(s_bias, 16)
            nc.vector.memset(bias[0:P // 2, :, S - P // 2:], NEG).then_inc(s_bmask, 1)
            dve.wait_ge(s_const, 2)
            nc.vector.tensor_copy(iota_f[:, :], iota_i[:, :]).then_inc(s_bmask, 1)
            dve.wait_ge(s_bmask, 2)
            nc.vector.tensor_scalar(iota_big[:, :], iota_f[:, 0:EG], BIG, None, ALU.add).then_inc(s_bmask, 1)
            dve.wait_ge(s_const, 4)
            nc.vector.tensor_copy(ids_f[:, :, :, :], ids_i[:, :, :, :]).then_inc(s_bmask, 1)
            dve.wait_ge(s_vused, CHUNKS_V)
            for b in (5, 1, 3, 7):
                nc.vector.tensor_copy(values[:, b % 4, (b // 4) * D_SB:(b // 4 + 1) * D_SB], bank[:, b, :]
                                      ).then_inc(s_vout_d, 1)

            def q_out(i):
                dve.wait_ge(s_pq, i + 1)
                for h in range(2):
                    own = slice(h * DH, (h + 1) * DH)
                    ins = nc.vector.tensor_scalar(q_both[own, h, :], PQ[own, :], SCALE, None, ALU.mult)
                ins.then_inc(s_qhi, 1)
                dve.wait_ge(s_qhi, i + 1)
                for h in range(2):
                    own, other = slice(h * DH, (h + 1) * DH), slice((1 - h) * DH, (2 - h) * DH)
                    ins = nc.vector.scalar_tensor_tensor(out=q_both[other, h, :], in0=PQ[own, :], scalar=SCALE,
                                                         in1=q_both[own, h, :].bitcast(F32), op0=ALU.mult,
                                                         op1=ALU.subtract)
                ins.then_inc(s_q, 1)

            def k_out(i):
                dve.wait_ge(s_khi, i + 1)
                for h in range(2):
                    own = slice(h * DH, (h + 1) * DH)
                    for half in range(2):
                        ins = nc.vector.tensor_tensor(k_lo[half * DH:(half + 1) * DH, h, :], PK[own, :],
                                                      k_hi[own, h, :].bitcast(F32), ALU.subtract)
                ins.then_inc(s_k, 1)

            q_out(0)
            k_out(0)

            def weights_out(i, o, h=1):
                b, u = ORDER[o], unit(i, o)
                dve.wait_ge(s_tr[h], u + 1 + CREDIT_TR)
                dve.wait_ge(s_pv[h], u + CREDIT_PV)
                nc.vector.tensor_copy(wT[:, h, 0:W[b]], TR[h][:, 0:W[b]]).then_inc(s_wT[h], 1)

            def z_free(u):
                dve.wait_ge(s_tr[1], u + 1)

            def masked(i, o):
                b, u = ORDER[o], unit(i, o)
                dve.wait_ge(s_sc, u + 1)
                z_free(u)
                nc.vector.tensor_tensor(Z[:, b % 2, :, 0:W[b]], SC[:, :, 0:W[b]],
                                        causal[:, S - W[b]:].unsqueeze(1).broadcast_to([P, 2, W[b]]),
                                        ALU.add).then_inc(s_z, 1)

            def later_sum(i, o):
                b, u = ORDER[o], unit(i, o)
                dve.wait_ge(s_ln, u + 1)
                dve.wait_ge(s_relu, u + 1)
                for h in range(2):
                    l, r = L[:, b % 2, h, 0:W[b]][:, ::-1], R[:, h, 0:W[b]][:, ::-1]
                    ins = nc.vector.tensor_tensor_scan(l, l, r, 0.0, ALU.add, ALU.add)
                ins.then_inc(s_scan, 1)
                dve.wait_ge(s_scan, u + 1 + CREDIT_SCAN)
                z = Z[:, b % 2, :, 0:W[b]]
                nc.vector.tensor_tensor(z, z, L[:, b % 2, :, 0:W[b]], ALU.subtract).then_inc(s_wlog, 1)

            def y_free(i):
                dve.wait_ge(s_yt, i + 1)

            def y_out(i, o):
                b, u = ORDER[o], unit(i, o)
                dve.wait_ge(s_pv[1], u + 1 + CREDIT_PV)
                if o == 0:
                    y_free(i)
                nc.vector.tensor_copy(y_pair[:, b, :], PV).then_inc(s_y, 1)

            def pair_out(i):
                dve.wait_ge(s_yt, i + 2)
                nc.vector.tensor_scalar(yT_hi[:, ds(i, 1), :].rearrange("p c s -> p (c s)"), YT, 1.0, None,
                                        ALU.mult).then_inc(s_yTh, 1)
                dve.wait_ge(s_yTh, i + 1)
                nc.vector.tensor_tensor(yT_lo[:, ds(i, 1), :].rearrange("p c s -> p (c s)"), YT,
                                        yT_hi[:, ds(i, 1), :].rearrange("p c s -> p (c s)").bitcast(F32),
                                        ALU.subtract).then_inc(s_yTl, 1)

            dve.wait_ge(s_mask, 2)
            dve.wait_ge(s_line_out, 16)
            with dve.Fori(0, PAIRS_SB) as i:
                masked(i, 0)
                masked(i, 1)
                later_sum(i, 0)
                later_sum(i, 1)
                weights_out(i, 0)
                masked(i, 2)
                y_out(i, 0)
                weights_out(i, 1)
                masked(i, 3)
                q_out(i + 1)
                later_sum(i, 2)
                later_sum(i, 3)
                y_out(i, 1)
                weights_out(i, 2)
                weights_out(i, 3)
                k_out(i + 1)
                y_out(i, 2)
                y_out(i, 3)
                pair_out(i)

            first_u = UNITS * PAIRS_SB

            def biased(i, o):
                b, u = ORDER[o], unit(i, o)
                dve.wait_ge(s_sc, u + 1)
                z_free(u)
                heads = bias[:, ds(2 * i - 2 * PAIRS_SB, 2), S - W[b]:]
                nc.vector.tensor_tensor(Z[:, b % 2, :, 0:W[b]], SC[:, :, 0:W[b]], heads, ALU.add).then_inc(s_z, 1)
                dve.wait_ge(s_z, u + 1 + CREDIT_Z)
                nc.vector.tensor_reduce(near[:, b % 2, :], Z[:, b % 2, :, 0:W[b]], AX.X, ALU.max).then_inc(s_mx, 1)
                dve.wait_ge(s_mx, u - first_u + 1)
                nc.vector.tensor_scalar(nnear[:, b % 2, :], near[:, b % 2, :], -1.0, None, ALU.mult
                                        ).then_inc(s_nmx, 1)

            def inverse(i, o):
                b, u = ORDER[o], unit(i, o)
                dve.wait_ge(s_p, u + 1)
                nc.vector.reciprocal(pinv[:, o, :], psumd[:, b % 2, :]).then_inc(s_inv, 1)

            def soft_y_out(i, o):
                b, u = ORDER[o], unit(i, o)
                dve.wait_ge(s_pv[1], u + 1 + CREDIT_PV)
                dve.wait_ge(s_inv, u - first_u + 1)
                if o == 0:
                    y_free(i)
                nc.vector.tensor_tensor(y_pair[:, b, :].rearrange("p (h d) -> p h d", h=2),
                                        PV.rearrange("p (h d) -> p h d", h=2),
                                        pinv[:, o, :].unsqueeze(2).broadcast_to([P, 2, DH]),
                                        ALU.mult).then_inc(s_y, 1)

            def softmax_pair(i, ahead):
                biased(i, 0)
                biased(i, 1)
                inverse(i, 0)
                weights_out(i, 0)
                biased(i, 2)
                soft_y_out(i, 0)
                inverse(i, 1)
                weights_out(i, 1)
                biased(i, 3)
                if ahead:
                    q_out(i + 1)
                soft_y_out(i, 1)
                inverse(i, 2)
                inverse(i, 3)
                weights_out(i, 2)
                weights_out(i, 3)
                if ahead:
                    k_out(i + 1)
                soft_y_out(i, 2)
                soft_y_out(i, 3)
                pair_out(i)

            dve.wait_ge(s_bmask, 4)
            with dve.Fori(PAIRS_SB, PAIRS - 1) as i:
                softmax_pair(i, True)
            softmax_pair(PAIRS - 1, False)

            def mean(n):
                dve.wait_ge(s_res, n + 1)
                nc.vector.tensor_scalar(nmean[:, n:n + 1], row_sum[:, n:n + 1], -1.0 / D, None, ALU.mult
                                        ).then_inc(s_mean, 1)

            def scaled(n):
                t = n % T
                dve.wait_ge(s_sqrt, n + 1)
                nc.vector.reciprocal(rstd[:, n:n + 1], std[:, n:n + 1]).then_inc(s_rstd, 1)
                dve.wait_ge(s_rstd, n + 1)
                nc.vector.scalar_tensor_tensor(out=hx[:, t, :], in0=hx[:, t, :], scalar=rstd[:, n:n + 1],
                                               in1=gain[:, :], op0=ALU.mult, op1=ALU.mult).then_inc(s_gain, 1)

            dve.wait_ge(s_vec, 32)
            for t in range(T):
                dve.wait_ge(s_mix, t + 1)
                nc.vector.scalar_tensor_tensor(out=hx[:, t, :], in0=hx[:, t, :], scalar=ALPHA,
                                               in1=bank[:, 2 * t:2 * t + 2, :].rearrange("p b n -> p (b n)"),
                                               op0=ALU.mult, op1=ALU.add, accum_out=row_sum[:, t:t + 1]
                                               ).then_inc(s_res, 1)
                mean(t)
                if t >= 2:
                    scaled(t - 2)
            scaled(T - 2)
            scaled(T - 1)

            for t in range(T):
                dve.wait_ge(s_hT, t + 1)
                nc.vector.tensor_copy(hT[:, KD // 2:, t * P:(t + 1) * P],
                                      bank[:, 2 * t + 1, :].rearrange("p (c s) -> p c s", c=KD // 2)
                                      ).then_inc(s_hTe_dve, 1)

            steps = [0]

            def then(ins):
                steps[0] += 1
                ins.then_inc(s_route, 1)
                dve.wait_ge(s_route, steps[0])

            def across(a, n):
                return a.unsqueeze(2).broadcast_to([P, T, n])

            def iota(n):
                return iota_f[:, 0:n].unsqueeze(1).broadcast_to([P, T, n])

            def first_max(values_, best, index, n):
                then(nc.vector.tensor_tensor(same[:, :, 0:n], values_, across(best, n), ALU.is_equal))
                then(nc.vector.scalar_tensor_tensor(
                    out=cand[:, :, 0:n], in0=same[:, :, 0:n], scalar=-BIG,
                    in1=iota_big[:, 0:n].unsqueeze(1).broadcast_to([P, T, n]), op0=ALU.mult, op1=ALU.add))
                then(nc.vector.tensor_reduce(index, cand[:, :, 0:n], AX.X, ALU.min))

            dve.wait_ge(s_logit, T)
            dve.wait_ge(s_rw, 16 * (3 + G))
            LG = bank[:, 0, 0:T * (G + E)].rearrange("p (t n) -> p t n", t=T)
            then(nc.vector.tensor_tensor(logit[:, :, :], LG, b_route[:, :].unsqueeze(1).broadcast_to([P, T, G + E]),
                                         ALU.add))
            glog = logit[:, :, 0:G]
            then(nc.vector.tensor_reduce(gmax[:, :], glog, AX.X, ALU.max))
            then(nc.vector.tensor_tensor(gdif[:, :, :], glog, across(gmax[:, :], G), ALU.subtract))
            first_max(glog, gmax[:, :], gidx[:, :], G)
            then(nc.vector.tensor_tensor(gone[:, :, :], iota(G), across(gidx[:, :], G), ALU.is_equal))
            then(nc.vector.tensor_tensor(picked[:, :, :, :],
                                         logit[:, :, G:].rearrange("p t (g e) -> p t g e", g=G),
                                         gone[:, :, :].unsqueeze(3).broadcast_to([P, T, G, EG]), ALU.mult))
            then(nc.vector.tensor_reduce(elog[:, :, :], picked[:, :, :, :].rearrange("p t g e -> p t e g"),
                                         AX.X, ALU.add))
            then(nc.vector.tensor_reduce(emax[:, 0, :], elog[:, :, :], AX.X, ALU.max))
            first_max(elog[:, :, :], emax[:, 0, :], eidx[:, 0, :], EG)
            then(nc.vector.tensor_tensor(eone[:, :, :], iota(EG), across(eidx[:, 0, :], EG), ALU.is_equal))
            then(nc.vector.scalar_tensor_tensor(out=elog[:, :, :], in0=eone[:, :, :], scalar=NEG, in1=elog[:, :, :],
                                                op0=ALU.mult, op1=ALU.add))
            then(nc.vector.tensor_reduce(emax[:, 1, :], elog[:, :, :], AX.X, ALU.max))
            first_max(elog[:, :, :], emax[:, 1, :], eidx[:, 1, :], EG)
            nc.vector.tensor_tensor(edif[:, :], emax[:, 1, :], emax[:, 0, :], ALU.subtract).then_inc(s_eexp, 1)
            then(nc.vector.scalar_tensor_tensor(
                out=expert[:, :, :], in0=gidx[:, :].unsqueeze(1).broadcast_to([P, 2, T]), scalar=float(EG),
                in1=eidx[:, :, :], op0=ALU.mult, op1=ALU.add))
            for k in range(2):
                ins = nc.vector.tensor_tensor(chosen[:, k, :, :], iota(E), across(expert[:, k, :], E), ALU.is_equal)
            then(ins)
            nc.vector.tensor_tensor(chosen_b[:, :, :], chosen[:, 0, :, :], chosen[:, 1, :, :], ALU.add
                                    ).then_inc(s_onehot, 1)
            then(nc.vector.tensor_tensor(
                ids_at[:, :, :, :],
                chosen[:, :, :, :].rearrange("p k t e -> p (k t) e").unsqueeze(2).broadcast_to([P, 2 * T, 2, E]),
                ids_f[:, :, :, :].rearrange("p k t c -> p (k t) c").unsqueeze(3).broadcast_to([P, 2 * T, 2, E]),
                ALU.mult))
            dve.wait_ge(s_rank, 1)
            RK = bank[:, 1, 0:T * E].rearrange("p (t e) -> p t e", t=T)
            for k in range(2):
                ins = nc.vector.tensor_tensor(ranked[:, k, :, :], chosen[:, k, :, :], RK, ALU.mult)
            then(ins)
            then(nc.vector.tensor_reduce(rank[:, :, :], ranked[:, :, :, :], AX.X, ALU.add))

            def fill_slots(ps):
                nc.vector.tensor_tensor(
                    at_rank[:, :, :], iota_f[:, :].unsqueeze(1).broadcast_to([P, 2 * T, SLOTS]),
                    rank[:, :, :].rearrange("p k t -> p (k t)").unsqueeze(2).broadcast_to([P, 2 * T, SLOTS]),
                    ALU.is_equal).then_inc(s_slots, 1)
                dve.wait_ge(s_slotted, ps + 1)
                found = bank[0:SLOTS, 7, 0:2 * E].rearrange("p (c e) -> p c e", c=2)
                nc.vector.tensor_scalar(empty[:, :, :], found, 0.0, float(FAR), ALU.is_equal, ALU.mult
                                        ).then_inc(s_empty, 1)
                dve.wait_ge(s_empty, ps + 1)
                nc.vector.scalar_tensor_tensor(out=idx_all[:, :, :], in0=found, scalar=-1.0, in1=empty[:, :, :],
                                               op0=ALU.add, op1=ALU.add).then_inc(s_idx, 1)

            fill_slots(0)
            then(nc.vector.tensor_reduce(count_f[:, :], bank[:, 2, 0:E], AX.X, ALU.max))
            then(nc.vector.tensor_scalar(count_i[:, :], count_f[:, :], float(SLOTS - 1), None, ALU.add))
            nc.vector.tensor_single_scalar(passes_i[:, :], count_i[:, :], SLOTS.bit_length() - 1,
                                           ALU.logical_shift_right).then_inc(s_passes, 1)
            dve.wait_ge(s_gexp, 1)
            then(nc.vector.tensor_reduce(gsum[:, :], gexp[:, :, :], AX.X, ALU.add))
            then(nc.vector.reciprocal(gprob[:, :], gsum[:, :]))
            dve.wait_ge(s_eexp, 2)
            then(nc.vector.tensor_scalar(esum[:, :], eexp[:, :], 1.0, None, ALU.add))
            then(nc.vector.reciprocal(einv[:, :], esum[:, :]))
            then(nc.vector.tensor_tensor(gate[:, 0, :], einv[:, :], gprob[:, :], ALU.mult))
            then(nc.vector.tensor_tensor(gate[:, 1, :], eexp[:, :], gate[:, 0, :], ALU.mult))

            def step(q, n):
                dve.wait_ge(s_xeT, n + 1)
                wait_gu(n)
                nc.vector.tensor_copy(xeT[:, q, :, :], XE).then_inc(s_xeTs, 1)

            def wait_gu(n):
                if not isinstance(n, int) or n >= 2:
                    dve.wait_ge(s_gu, n - 1)

            def finish(q, n):
                dve.wait_ge(s_silu, n + 1)
                nc.vector.tensor_tensor(hid[:, q, :, :], silu_g[:, q, :, :], GU[q][:, FB:, :], ALU.mult
                                        ).then_inc(s_hid, 1)

            def rows_out(q, n, put_uses):
                dve.wait_ge(s_dn, n + 1)
                if not isinstance(n, int) or n >= 2:
                    dve.wait_ge(s_put[q], 16 * put_uses)
                nc.vector.tensor_copy(y_rows[0:SLOTS, q, 512:], DN[q][:, 1, :]).then_inc(s_yd, 1)

            step(0, 0)
            for n in range(2):
                finish(n, n)
                step(1 - n, n + 1)
                rows_out(n, n, 0)
            with dve.Fori(1, E // 2 - 1) as m:
                for q in range(2):
                    finish(q, 2 * m + q)
                    step(1 - q, 2 * m + (q + 1))
                    rows_out(q, 2 * m + q, m)
            finish(0, E - 2)
            step(1, E - 1)
            rows_out(0, E - 2, E // 2 - 1)
            finish(1, E - 1)
            rows_out(1, E - 1, E // 2 - 1)
            n_passes = dve.value_load(passes_i[0:1, 0:1], min_val=0, max_val=S // SLOTS)
            with dve.If(n_passes > 1):
                with dve.Fori(1, n_passes) as ps:
                    dve.wait_ge(s_put[0], 16 * E * ps + (-8 * E))
                    nc.vector.tensor_scalar(rank[:, :, :], rank[:, :, :], float(-SLOTS), None, ALU.add
                                            ).then_inc(s_lower, 1)
                    dve.wait_ge(s_lower, ps)
                    fill_slots(ps)
                    with dve.Fori(0, E) as e:
                        n = E * ps + e
                        step(0, n)
                        finish(0, n)
                        rows_out(0, n, n + (-E // 2))
            with dve.Else():
                dve.nop(nofuse=True)

            dve.wait_ge(s_scaled, T)
            dve.wait_ge(s_vec2, 32)
            for t in range(T):
                dve.wait_ge(s_first[t], 32)
                n = T + t
                nc.vector.scalar_tensor_tensor(out=hx[:, t, :], in0=first_y[:, t, :], scalar=gate[:, 0, t:t + 1],
                                               in1=hx[:, t, :], op0=ALU.mult, op1=ALU.add).then_inc(s_res1, 1)
                dve.wait_ge(s_res1, t + 1)
                nc.vector.scalar_tensor_tensor(out=hx[:, t, :], in0=second_y[:, t, :], scalar=gate[:, 1, t:t + 1],
                                               in1=hx[:, t, :], op0=ALU.mult, op1=ALU.add,
                                               accum_out=row_sum[:, n:n + 1]).then_inc(s_res, 1)
                mean(n)
                if t >= 1:
                    scaled(n - 1)
            scaled(2 * T - 1)

        @block.tensor
        def _(pe):
            pe.wait_ge(s_ident, 2)
            for c in range(KD):
                for t in range(T):
                    if c == 0:
                        pe.wait_ge(s_x[t], 16)
                    mm = nc.tensor.transpose(bank[:, c, t * P:(t + 1) * P], hx[:, t, c * P:(c + 1) * P], ident[:, :])
                mm.then_inc(s_xT, 1)

            def split_products(dst, a_hi, a_lo, b_hi, b_lo, start, stop):
                nc.tensor.matmul(dst, a_hi, b_hi, start=start, stop=False)
                nc.tensor.matmul(dst, a_lo, b_hi, start=False, stop=False)
                return nc.tensor.matmul(dst, a_hi, b_lo, start=False, stop=stop)

            for c in range(KD):
                pe.wait_ge(s_lo, c + 1)
                for g in range(2):
                    for t in range(T):
                        if c == 0:
                            pe.wait_ge(s_xTl, 4 * g + t + 1)
                        a = slice(t * P, (t + 1) * P)
                        n = slice(g * D_SB, (g + 1) * D_SB)
                        mm = split_products(bank[:, 4 * g + t, :], xT_hi[:, c, a], xT_lo[:, c, a],
                                            w_hi[:, c % 2, n], w_lo[:, c % 2, n], c == 0, c == KD - 1)
                mm.then_inc(s_vused, 1)

            def project(dst, n, slot, cs, done):
                if cs.start == 0:
                    pe.wait_ge(s_lo, n + 1)
                for c in range(KD)[cs]:
                    w = slice(c * P, (c + 1) * P)
                    mm = split_products(dst, w_hi[:, slot, w], w_lo[:, slot, w], xT_hi[:, c, :], xT_lo[:, c, :],
                                        c == 0, c == KD - 1)
                if cs.stop == KD:
                    mm.then_inc(done, 1)

            def project_q(i, part):
                if part == 0 and not (isinstance(i, int) and i == 0):
                    pe.wait_ge(s_q, i)
                project(PQ, FIRST_QK + 2 * i, 0, slice(2 * part, 2 * part + 2), s_pq)

            def project_k(i, part):
                if part == 0 and not (isinstance(i, int) and i == 0):
                    pe.wait_ge(s_k, i)
                project(PK, FIRST_QK + 1 + 2 * i, 1, slice(2 * part, 2 * part + 2), s_pk)

            def scores(i, o):
                b, u = ORDER[o], unit(i, o)
                if o == 0:
                    pe.wait_ge(s_q, i + 1)
                    pe.wait_ge(s_k, i + 1)
                pe.wait_ge(s_z, u + CREDIT_Z)
                for h in range(2):
                    q = q_both[:, h, b * P:(b + 1) * P]
                    nc.tensor.matmul(SC[:, h, 0:W[b]], q, k_hi[:, h, 0:W[b]], start=True, stop=False)
                    mm = nc.tensor.matmul(SC[:, h, 0:W[b]], q, k_lo[:, h, 0:W[b]], start=False, stop=True)
                mm.then_inc(s_sc, 1)

            def turn(i, o):
                b, u = ORDER[o], unit(i, o)
                pe.wait_ge(s_p, u + 1)
                for h in range(2):
                    pe.wait_ge(s_wT[h], u + CREDIT_WT)
                    for j in range(b + 1):
                        mm = nc.tensor.transpose(TR[h][:, j * P:(j + 1) * P], Z[:, b % 2, h, j * P:(j + 1) * P],
                                                 ident[:, :])
                    mm.then_inc(s_tr[h], 1)

            def combine(i, o):
                b, u = ORDER[o], unit(i, o)
                pe.wait_ge(s_y, u + CREDIT_Y)
                for h in range(2):
                    pe.wait_ge(s_wT[h], u + 1 + CREDIT_WT)
                    for j in range(b + 1):
                        v = values[:, j, ds(i * P + h * DH, DH)] if not isinstance(i, int) else \
                            values[:, j, i * P + h * DH:i * P + (h + 1) * DH]
                        mm = nc.tensor.matmul(PV[:, h * DH:(h + 1) * DH], wT[:, h, j * P:(j + 1) * P], v,
                                              start=(j == 0), stop=(j == b))
                    mm.then_inc(s_pv[h], 1)

            def turn_y(i):
                pe.wait_ge(s_y, unit(i + 1, 0) + CREDIT_Y)
                pe.wait_ge(s_yTl, i + 1)
                for t in range(T):
                    mm = nc.tensor.transpose(YT[:, t * P:(t + 1) * P], y_pair[:, t, :], ident[:, :])
                mm.then_inc(s_yt, 1)

            pe.wait_ge(s_vout_a, 1)
            pe.wait_ge(s_vout_d, 1)
            for part in range(4):
                project_q(0, part)
            for part in range(4):
                project_k(0, part)
            pe.wait_ge(s_vout_a, 4)
            pe.wait_ge(s_vout_d, 4)

            def pair(i, ahead):
                def fill(project_, *parts):
                    for part in parts if ahead else ():
                        project_(i + 1, part)

                scores(i, 0)
                fill(project_q, 0, 1)
                scores(i, 1)
                fill(project_q, 2, 3)
                fill(project_k, 0)
                turn(i, 0)
                scores(i, 2)
                fill(project_k, 1)
                combine(i, 0)
                turn(i, 1)
                scores(i, 3)
                fill(project_k, 2, 3)
                combine(i, 1)
                turn(i, 2)
                turn(i, 3)
                combine(i, 2)
                combine(i, 3)
                turn_y(i)

            with pe.Fori(0, PAIRS - 1) as i:
                pair(i, True)
            pair(PAIRS - 1, False)

            for c in range(KD):
                pe.wait_ge(s_lo, FIRST_OUT + c + 1)
                if c == 0:
                    pe.wait_ge(s_yTl, PAIRS + 1)
                for t in range(T):
                    for j in range(2):
                        a = slice(t * P, (t + 1) * P)
                        n = slice(j * 512, (j + 1) * 512)
                        mm = split_products(bank[:, 2 * t + j, :], yT_hi[:, c, a], yT_lo[:, c, a],
                                            w_hi[:, c % 2, n], w_lo[:, c % 2, n], c == 0, c == KD - 1)
                    if c == KD - 1:
                        mm.then_inc(s_mix, 1)
                if c < KD - 1:
                    mm.then_inc(s_oused, 1)

            for t in range(T):
                pe.wait_ge(s_h, t + 1)
                for c in range(KD):
                    mm = nc.tensor.transpose(bank[:, 2 * t + c // 4, c % 4 * P:(c % 4 + 1) * P], hx[:, t, c::KD],
                                             ident[:, :])
                mm.then_inc(s_hT, 1)
            pe.wait_ge(s_rw, 16 * (3 + G))
            for t in range(T):
                pe.wait_ge(s_hTe_act, t + 1)
                pe.wait_ge(s_hTe_dve, t + 1)
                for c in range(KD):
                    mm = nc.tensor.matmul(bank[:, 0, t * (G + E):(t + 1) * (G + E)], hT[:, c, t * P:(t + 1) * P],
                                          w_route[:, c, :], start=(c == 0), stop=(c == KD - 1))
                mm.then_inc(s_logit, 1)
            pe.wait_ge(s_onehot, 1)
            pe.wait_ge(s_const, 6)
            for t in range(T):
                for j in range(t + 1):
                    nc.tensor.matmul(bank[:, 1, t * E:(t + 1) * E], before[:, :] if j == t else ones[:, :],
                                     chosen_b[:, j, :], start=(j == 0), stop=(j == t))
            for t in range(T):
                mm = nc.tensor.matmul(bank[:, 2, 0:E], ones[:, :], chosen_b[:, t, :], start=(t == 0),
                                      stop=(t == T - 1))
            mm.then_inc(s_rank, 1)

            def slots(ps):
                pe.wait_ge(s_slots, ps + 1)
                for j in range(2 * T):
                    mm = nc.tensor.matmul(bank[0:SLOTS, 7, 0:2 * E], at_rank[:, j, :],
                                          ids_at[:, j, :, :].rearrange("p c e -> p (c e)"),
                                          start=(j == 0), stop=(j == 2 * T - 1))
                mm.then_inc(s_slotted, 1)

            slots(0)

            def turn_x(q, n, use):
                pe.wait_ge(s_get[q], 16 * use + 16)
                if not isinstance(n, int) or n > 0:
                    pe.wait_ge(s_xeTs, n)
                    pe.nop(nofuse=True)
                for c in range(KD):
                    mm = nc.tensor.transpose(XE[:, c, :], xe[:, q, c::KD], ident[0:SLOTS, 0:SLOTS])
                mm.then_inc(s_xeT, 1)

            def gate_up(q, n, r, use):
                pe.wait_ge(s_w[r], 48 * use + 48)
                pe.wait_ge(s_xeTs, n + 1)
                if not isinstance(n, int) or n >= 2:
                    pe.wait_ge(s_hid, n - 1)
                for w, first in ((gate_w[r], 0), (up_w[r], FB)):
                    for b in range(FB):
                        for c in range(KD):
                            mm = nc.tensor.matmul(GU[q][:, first + b, :], w[:, c, b * P:(b + 1) * P],
                                                  xeT[:, q, c, :], start=(c == 0), stop=(c == KD - 1))
                mm.then_inc(s_gu, 1)

            def down(q, n, r):
                pe.wait_ge(s_hid, n + 1)
                if not isinstance(n, int) or n >= 2:
                    pe.wait_ge(s_ya, n - 1)
                    pe.wait_ge(s_yd, n - 1)
                for j in range(2):
                    for b in range(FB):
                        mm = nc.tensor.matmul(DN[q][:, j, :], hid[:, q, b, :], down_w[r][:, b, j * 512:(j + 1) * 512],
                                              start=(b == 0), stop=(b == FB - 1))
                mm.then_inc(s_dn, 1)
                return mm

            pe.wait_ge(s_passes, 1)
            turn_x(0, 0, 0)

            def expert_step(r, n, q, use, round_, more):
                gate_up(q, n, r, round_)
                if more:
                    turn_x(1 - q, n + 1, use)
                down(q, n, r)

            for r in range(RING):
                expert_step(r, r, r % 2, (r + 1) // 2, 0, True)
            with pe.Fori(1, EXPERT_ROUNDS) as rd:
                for r in range(RING):
                    expert_step(r, rd * RING + r, r % 2, rd * (RING // 2) + (r + 1) // 2, rd, True)
            for n in range(RING * EXPERT_ROUNDS, E):
                expert_step(n % RING, n, n % 2, (n + 1) // 2, n // RING, n + 1 < E)

            n_passes = pe.value_load(passes_i[0:1, 0:1], min_val=0, max_val=S // SLOTS)
            slot0_uses = (E + RING - 1) // RING
            with pe.If(n_passes > 1):
                with pe.Fori(1, n_passes) as ps:
                    slots(ps)
                    with pe.Fori(0, E) as e:
                        n = E * ps + e
                        turn_x(0, n, n - E + E // 2)
                        gate_up(0, n, 0, n - E + slot0_uses)
                        down(0, n, 0)
            with pe.Else():
                pe.nop(nofuse=True)


_INS = ["x", "w_in", "w_out", "rel_bias", "ln1_g", "ln1_b", "w_group", "b_group", "w_expert", "b_expert",
        "w_gate", "w_up", "w_down", "ln2_g", "ln2_b"]


def kernel(**inputs):
    import numpy as np
    import concourse.bacc as bacc
    from concourse.bass_utils import run_bass_kernel_spmd as run

    nc = bacc.Bacc("TRN2", target_bir_lowering=False, num_devices=1)
    arrays, args = {}, []
    for name in _INS:
        a = np.ascontiguousarray(inputs[name])
        arrays[f"in_{name}"] = a
        args.append(nc.dram_tensor(f"in_{name}", a.shape, F32, kind="ExternalInput").ap())
    out = nc.dram_tensor("out", arrays["in_x"].shape, F32, kind="ExternalOutput").ap()
    build(nc, *args, out)
    return run(nc, [arrays], core_ids=[0]).results[0]["out"]
```

```python
from contextlib import ExitStack

import concourse.bass as bass
from concourse import mybir

F32 = mybir.dt.float32
F32R = mybir.dt.float32r
BF16 = mybir.dt.bfloat16
I32 = mybir.dt.int32
ALU = mybir.AluOpType
ACT = mybir.ActivationFunctionType
AX = mybir.AxisListType

P = 128
NEG = -1e30
BIG = 64.0
FAR = 1 << 20
LN_EPS = 1e-5
ds = bass.ds


def build(nc, x, w_in, w_out, rel_bias, ln1_g, ln1_b, w_group, b_group, w_expert, b_expert,
          w_gate, w_up, w_down, ln2_g, ln2_b, out):
    DEPTH, D, _ = w_in.shape
    S = x.shape[1]
    T = S // P
    KD = D // P
    DH = 64
    D_SB = D // 2
    PAIRS_SB = D_SB // P
    PAIRS = D // P
    HEADS_CA = rel_bias.shape[1]
    REL = rel_bias.shape[2]
    CLIP = REL // 2
    G = w_group.shape[2]
    EG = w_expert.shape[3]
    E = G * EG
    F = w_gate.shape[4]
    FB = F // P
    ALPHA = (2.0 * DEPTH) ** 0.25
    SCALE = DH ** -0.5
    SLOTS = 64
    RING = 6
    EXPERT_ROUNDS = E // RING
    XES = 3
    assert RING % XES == 0 and RING % 2 == 0
    assert DEPTH == 1 and T == 4 and KD == 8 and E == 32 and FB == 2 and PAIRS_SB == 4

    CHUNKS_V = KD
    FIRST_QK = CHUNKS_V
    FIRST_OUT = FIRST_QK + 2 * PAIRS
    CHUNKS = FIRST_OUT + KD
    UNITS = T
    W = [(b + 1) * P for b in range(T)]

    h_dram = nc.dram_tensor("h_rows", [S, D], F32).ap()
    y_dram = nc.dram_tensor("expert_rows", [2 * S, D], F32).ap()
    LINE = S + P - 1
    line_dram = nc.dram_tensor("bias_lines", [HEADS_CA, P, LINE], F32).ap()

    with ExitStack() as ctx:
        base = (nc.sbuf_base + 63) // 64 * 64
        top = [base]

        def at(name, shape, dt, offset):
            return nc.alloc_sbuf_tensor_at(name, shape, dt, offset=offset)

        def size(shape, dt):
            n = 2 if dt == BF16 else 4
            for d in shape[1:]:
                n *= d
            return (n + 31) // 32 * 32

        def sb(name, shape, dt=F32):
            t = at(name, shape, dt, top[0])
            top[0] += size(shape, dt)
            return t

        def sem(name):
            return ctx.enter_context(nc.semaphore(name))

        hx = sb("hx", [P, T, D])
        gain_off = top[0]
        gain = sb("gain", [P, D])
        shift = sb("shift", [P, D])
        down_hi = at("down_hi", [P, FB, D], F32R, gain_off)
        w_route = sb("w_route", [P, KD, G + E])
        b_route = sb("b_route", [P, G + E])
        ident = sb("ident", [P, P])
        eps = sb("eps", [P, 1])
        row_sum = sb("row_sum", [P, 2 * T])
        nmean = sb("nmean", [P, 2 * T])
        row_sq = sb("row_sq", [P, 2 * T])
        std = sb("std", [P, 2 * T])
        rstd = sb("rstd", [P, 2 * T])
        y_rows_off = top[0]
        y_rows = sb("y_rows", [P, 2, D])
        squares = at("squares", [P, 2, D], F32, y_rows_off)
        xeT = sb("xeT", [P, 2, KD, SLOTS])
        silu_g = sb("silu_g", [P, 2, FB, SLOTS])
        hid = sb("hid", [P, 2, FB, SLOTS])
        idx_all = sb("idx_all", [SLOTS, 2, E], I32)
        empty = sb("empty", [SLOTS, 2, E])
        idx_get = sb("idx_get", [SLOTS, XES], I32)
        idx_put = sb("idx_put", [SLOTS, 2], I32)
        iota_i = sb("iota_i", [P, SLOTS], I32)
        iota_f = sb("iota_f", [P, SLOTS])
        iota_big = sb("iota_big", [P, EG])
        before = sb("before", [P, P], BF16)
        ones = sb("ones", [P, P], BF16)
        ids_i = sb("ids_i", [P, 2, T, 2], I32)
        ids_f = sb("ids_f", [P, 2, T, 2])
        ids_at = sb("ids_at", [P, 2 * T, 2, E])
        logit = sb("logit", [P, T, G + E])
        gmax = sb("gmax", [P, T])
        gdif = sb("gdif", [P, T, G])
        gexp = sb("gexp", [P, T, G])
        gsum = sb("gsum", [P, T])
        gprob = sb("gprob", [P, T])
        same = sb("same", [P, T, EG])
        cand = sb("cand", [P, T, EG])
        gidx = sb("gidx", [P, T])
        gone = sb("gone", [P, T, G])
        picked = sb("picked", [P, T, G, EG])
        elog = sb("elog", [P, T, EG])
        emax = sb("emax", [P, 2, T])
        eidx = sb("eidx", [P, 2, T])
        eone = sb("eone", [P, T, EG])
        edif = sb("edif", [P, T])
        eexp = sb("eexp", [P, T])
        esum = sb("esum", [P, T])
        einv = sb("einv", [P, T])
        gate = sb("gate", [P, 2, T])
        expert = sb("expert", [P, 2, T])
        chosen = sb("chosen", [P, 2, T, E])
        chosen_b = sb("chosen_b", [P, T, E], BF16)
        ranked = at("ranked", [P, 2, T, E], F32, y_rows_off)
        rank = sb("rank", [P, 2, T])
        count_i = sb("count_i", [P, 1], I32)
        count_f = sb("count_f", [P, 1])
        passes_i = sb("passes_i", [P, 1], I32)
        near = sb("near", [P, 2, 2])
        nnear = sb("nnear", [P, 2, 2])
        psumd = sb("psumd", [P, 2, 2])
        pinv = sb("pinv", [P, UNITS, 2])
        arena = (top[0] + 63) // 64 * 64

        top[0] = arena
        xT_hi = sb("xT_hi", [P, KD, S], F32R)
        xT_lo = sb("xT_lo", [P, KD, S], F32R)
        values = sb("values", [P, T, D])
        bias = sb("bias", [P, HEADS_CA, S])
        Z = sb("Z", [P, 2, 2, S])
        L = sb("L", [P, 2, 2, S])
        R = sb("R", [P, 2, S])
        wT = sb("wT", [P, 2, S])
        q_both = sb("q_both", [P, 2, S], F32R)
        k_hi = sb("k_hi", [P, 2, S], F32R)
        k_lo = sb("k_lo", [P, 2, S], F32R)
        y_pair = sb("y_pair", [P, T, P])
        raw = sb("raw", [P, 2, D])
        w_hi = sb("w_hi", [P, 2, D], F32R)
        w_lo = sb("w_lo", [P, 2, D], F32R)
        mask_off = top[0]
        yT_hi = sb("yT_hi", [P, KD, S], F32R)
        yT_lo = sb("yT_lo", [P, KD, S], F32R)
        arena_end = top[0]
        causal_off = top[0]
        causal = sb("causal", [P, S])
        at_rank = at("at_rank", [P, 2 * T, SLOTS], F32, causal_off)
        line = at("line", [HEADS_CA, LINE], F32, mask_off)
        rb = at("rb", [HEADS_CA, REL], F32, mask_off + 4096)
        assert top[0] <= nc.sbuf_usable_end, (top[0], nc.sbuf_usable_end)

        SLOT = (2 * KD * F + FB * D) * 4
        gate_w, up_w, down_w, down_lo = [], [], [], []
        for r in range(RING):
            o = arena + r * SLOT
            gate_w.append(at(f"gate_w{r}", [P, KD, F], F32, o))
            up_w.append(at(f"up_w{r}", [P, KD, F], F32, o + KD * F * 4))
            down_w.append(at(f"down_w{r}", [P, FB, D], F32, o + 2 * KD * F * 4))
            down_lo.append(at(f"down_lo{r}", [P, FB, D], F32R, o + 2 * KD * F * 4))
        last_slot = arena + (RING - 1) * SLOT
        gain2 = at("gain2", [P, D], F32, last_slot)
        shift2 = at("shift2", [P, D], F32, last_slot + D * 4)
        xe_off = arena + RING * SLOT
        xe = at("xe", [SLOTS, XES, D], F32, xe_off)
        hid_both_off = xe_off + XES * D * 4
        hid_both = at("hid_both", [P, 2, FB, 2 * SLOTS], F32R, hid_both_off)
        assert hid_both_off + 4 * FB * SLOTS * 4 <= arena_end
        hT = at("hT", [P, KD, S], F32, arena_end - KD * S * 4)
        first_y = at("first_y", [P, T, D], F32, arena)
        second_y = at("second_y", [P, T, D], F32, arena + T * D * 4)

        bank = ctx.enter_context(nc.psum_tensor("bank", [P, 8, 512], F32))
        SC = bank[:, 0:2, :]
        TR = [bank[:, 2, :], bank[:, 3, :]]
        PQ, PK = bank[:, 4, :], bank[:, 5, :]
        PV = bank[:, 6, :]
        YT = bank[:, 7, :]
        XE = bank[:, 6, :].rearrange("p (c s) -> p c s", c=KD)
        GU = [bank[:, 4 + i, 0:2 * FB * SLOTS].rearrange("p (j s) -> p j s", s=SLOTS) for i in range(2)]
        DN = [bank[:, 2 * i:2 * i + 2, :] for i in range(2)]

        s_x = [sem(f"s_x{t}") for t in range(T)]
        s_ident = sem("s_ident")
        s_const = sem("s_const")
        s_mask = sem("s_mask")
        s_rb = sem("s_rb"); s_line = sem("s_line"); s_line_out = sem("s_line_out"); s_bias = sem("s_bias")
        s_bmask = sem("s_bmask")
        s_xT = sem("s_xT"); s_xTh = sem("s_xTh"); s_xTl = sem("s_xTl")
        s_raw = [sem("s_raw0"), sem("s_raw1")]
        s_hi = sem("s_hi"); s_lo = sem("s_lo"); s_vused = sem("s_vused"); s_oused = sem("s_oused")
        s_vout_d = sem("s_vout_d"); s_vout_a = sem("s_vout_a")
        s_pq = sem("s_pq"); s_pk = sem("s_pk"); s_q = sem("s_q"); s_k = sem("s_k")
        s_qhi = sem("s_qhi"); s_khi = sem("s_khi")
        s_sc = sem("s_sc")
        s_z = sem("s_z")
        s_abs = sem("s_abs"); s_exp = sem("s_exp"); s_ln = sem("s_ln"); s_relu = sem("s_relu")
        s_scan = sem("s_scan"); s_wlog = sem("s_wlog")
        s_p = sem("s_p")
        s_mx = sem("s_mx"); s_nmx = sem("s_nmx"); s_inv = sem("s_inv")
        s_tr = [sem("s_tr0"), sem("s_tr1")]
        s_wT = [sem("s_wT0"), sem("s_wT1")]
        s_pv = [sem("s_pv0"), sem("s_pv1")]
        s_y = sem("s_y"); s_yt = sem("s_yt"); s_yTh = sem("s_yTh"); s_yTl = sem("s_yTl")
        s_mix = sem("s_mix")
        s_vec = sem("s_vec"); s_vec2 = sem("s_vec2")
        s_res = sem("s_res"); s_mean = sem("s_mean"); s_centred = sem("s_centred"); s_sq = sem("s_sq")
        s_sqrt = sem("s_sqrt"); s_rstd = sem("s_rstd"); s_gain = sem("s_gain"); s_h = sem("s_h")
        s_hst = sem("s_hst"); s_hT = sem("s_hT"); s_hTe_act = sem("s_hTe_act"); s_hTe_dve = sem("s_hTe_dve")
        s_logit = sem("s_logit")
        s_rw = sem("s_rw"); s_last = sem("s_last")
        s_route = sem("s_route"); s_gexp = sem("s_gexp"); s_eexp = sem("s_eexp")
        s_onehot = sem("s_onehot"); s_rank = sem("s_rank"); s_passes = sem("s_passes")
        s_slots = sem("s_slots"); s_empty = sem("s_empty"); s_lower = sem("s_lower")
        s_slotted = sem("s_slotted"); s_idx = sem("s_idx")
        s_xe0 = sem("s_xe0")
        s_gate_w = [sem(f"s_gate_w{r}") for r in range(RING)]
        s_up_w = [sem(f"s_up_w{r}") for r in range(RING)]
        s_down_w = [sem(f"s_down_w{r}") for r in range(RING)]
        s_gidx = sem("s_gidx"); s_pidx = sem("s_pidx")
        s_get = [sem(f"s_get{a}") for a in range(XES)]
        s_xeT = sem("s_xeT"); s_xeTs = sem("s_xeTs")
        s_gu = sem("s_gu"); s_silu = sem("s_silu"); s_prod = sem("s_prod")
        s_hid_hi = sem("s_hid_hi"); s_hid = sem("s_hid"); s_dhi = sem("s_dhi"); s_dlo = sem("s_dlo")
        s_dn = sem("s_dn"); s_ya = sem("s_ya"); s_yd = sem("s_yd")
        s_put = [sem("s_put0"), sem("s_put1")]; s_all = sem("s_all")
        s_first = [sem(f"s_first{t}") for t in range(T)]
        s_scaled = sem("s_scaled")
        s_res1 = sem("s_res1"); s_out = sem("s_out")

        x_v = x.rearrange("a (t p) d -> p (a t) d", p=P)
        out_v = out.rearrange("a (t p) d -> p (a t) d", p=P)
        h_v = h_dram.rearrange("(t p) d -> p t d", p=P)
        w_in_v = w_in[0].rearrange("(c p) n -> p c n", p=P)
        w_out_v = w_out[0].rearrange("(c p) n -> p c n", p=P)
        w_gate_v = w_gate.rearrange("l g e (p c) f -> p (l g e) (c f)", p=P)
        w_up_v = w_up.rearrange("l g e (p c) f -> p (l g e) (c f)", p=P)
        w_down_v = w_down.rearrange("l g e (b p) d -> p (l g e) b d", p=P)
        y_v = y_dram.rearrange("(k t p) d -> p k t d", k=2, p=P)

        def everywhere(row, n):
            return bass.AP(row.tensor, row.offset, [[0, P], [1, n]])

        def unit(i, o):
            return UNITS * i + o

        slot0_uses = (E + RING - 1) // RING
        STICK, SOFT = "stick-breaking", "softmax"
        ORDER = list(range(T - 1, -1, -1))
        CREDIT_TR, CREDIT_WT, CREDIT_PV = 2, 1, 1
        CREDIT_WLOG, CREDIT_SCAN, CREDIT_Z = 2, 1, 1

        block = ctx.enter_context(nc.Block())

        @block.sync
        def _(sp):
            for t in range(T):
                sp.dma_start(hx[:, t, :], x_v[:, t, :]).then_inc(s_x[t], 16)

            def chunk_free(n):
                if not isinstance(n, int) or n >= 2:
                    sp.wait_ge(s_hi, n - 1)
                    sp.wait_ge(s_lo, n - 1)

            for n in range(CHUNKS_V):
                chunk_free(n)
                src = bass.AP(w_in_v.tensor, w_in_v[:, n, 2 * D_SB:2 * D_SB + 1].offset,
                              [[3 * D, P], [3 * D_SB, 2], [1, D_SB]])
                sp.dma_start(raw[:, n % 2, :].rearrange("p (g j) -> p g j", g=2), src).then_inc(s_raw[n % 2], 16)
                if n == 1:
                    sp.dma_start(rb[:, :], rel_bias[0]).then_inc(s_rb, 16)
                if n == 4:
                    sp.wait_ge(s_line, 2)
                    sp.dma_start(line_dram, line[:, :].unsqueeze(1).broadcast_to([HEADS_CA, P, LINE])).then_inc(s_line_out, 16)
                if n == 6:
                    sp.wait_ge(s_line_out, 16)
                    sp.dma_start(bias[:, :, :], bass.AP(line_dram.tensor, P - 1, [[LINE - 1, P], [P * LINE, HEADS_CA], [1, S]])
                                 ).then_inc(s_bias, 16)
            for first_col, first_pair, pairs in ((0, 0, PAIRS_SB), (3 * D_SB, PAIRS_SB, PAIRS - PAIRS_SB)):
                with sp.Fori(0, pairs) as i:
                    for j in range(2):
                        chunk_free(FIRST_QK + 2 * first_pair + j + 2 * i)
                        sp.nop(nofuse=True)
                        src = w_in_v[:, :, ds(first_col + (1 - j) * D_SB + P * i, P)]
                        sp.dma_start(raw[:, j, :].rearrange("p (c m) -> p c m", c=KD), src).then_inc(s_raw[j], 16)
                if first_pair == 0:
                    sp.dma_start(gain[:, :], everywhere(ln1_g[0], D)).then_inc(s_vec, 16)
                    sp.dma_start(shift[:, :], everywhere(ln1_b[0], D)).then_inc(s_vec, 16)
                    sp.dma_start(b_route[:, 0:G], everywhere(b_group[0], G)).then_inc(s_rw, 16)
                    sp.dma_start(b_route[:, G:], everywhere(b_expert[0], E)).then_inc(s_rw, 16)
                    with nc.allow_non_contiguous_dma(reason="router weights, once, short rows"):
                        sp.dma_start(w_route[:, :, 0:G], w_group[0].rearrange("(p c) g -> p c g", p=P)
                                     ).then_inc(s_rw, 16)
                        for g in range(G):
                            sp.dma_start(w_route[:, :, G + g * EG:G + (g + 1) * EG],
                                         w_expert[0, g].rearrange("(p c) e -> p c e", p=P)).then_inc(s_rw, 16)

            def expert_matrix(r, e, which):
                one = slice(e, e + 1) if isinstance(e, int) else ds(e, 1)
                if which == 0:
                    sp.dma_start(gate_w[r][:, :, :].rearrange("p c f -> p (c f)"),
                                 w_gate_v[:, one, :].rearrange("p e n -> p (e n)")).then_inc(s_gate_w[r], 16)
                elif which == 1:
                    sp.dma_start(up_w[r][:, :, :].rearrange("p c f -> p (c f)"),
                                 w_up_v[:, one, :].rearrange("p e n -> p (e n)")).then_inc(s_up_w[r], 16)
                else:
                    sp.dma_start(down_w[r][:, :, :],
                                 w_down_v[:, one, :, :].rearrange("p e b d -> p (e b) d")).then_inc(s_down_w[r], 16)

            def expert_weights(r, e):
                for which in range(3):
                    expert_matrix(r, e, which)

            for n in range(FIRST_OUT, CHUNKS):
                chunk_free(n)
                sp.dma_start(raw[:, n % 2, :], w_out_v[:, n - FIRST_OUT, :]).then_inc(s_raw[n % 2], 16)
                done = n - FIRST_OUT - 1
                if done == 0:
                    sp.wait_ge(s_pk, PAIRS)
                    sp.wait_ge(s_pv[1], PAIRS * UNITS + CREDIT_PV)
                    sp.wait_ge(s_yt, PAIRS + 1)
                if done >= 0:
                    expert_matrix(done // 3, done // 3, done % 3)
            for m in range(KD - 1, 3 * 4):
                expert_matrix(m // 3, m // 3, m % 3)
            sp.wait_ge(s_mix, T)
            expert_weights(4, 4)
            for t in range(T):
                sp.wait_ge(s_h, t + 1)
                sp.dma_start(h_v[:, t, :], hx[:, t, :]).then_inc(s_hst, 16)
            sp.wait_ge(s_logit, T)
            expert_weights(5, 5)
            def one_before(r, round_):
                sp.wait_ge(s_gate_w[(r - 1) % RING], 16 * round_ + (16 if r >= 1 else 0))
                sp.nop(nofuse=True)

            def refill(r, e):
                sp.wait_ge(s_gu, e + (1 - RING))
                sp.nop(nofuse=True)
                expert_matrix(r, e, 0)
                expert_matrix(r, e, 1)
                sp.wait_ge(s_dn, e + (1 - RING))
                sp.nop(nofuse=True)
                expert_matrix(r, e, 2)

            with sp.Fori(1, EXPERT_ROUNDS) as rd:
                for r in range(RING):
                    one_before(r, rd)
                    refill(r, rd * RING + r)
            for e in range(RING * EXPERT_ROUNDS, E):
                one_before(e % RING, e // RING)
                refill(e % RING, e)
            sp.wait_ge(s_dn, (E // RING - 1) * RING + RING)
            sp.dma_start(gain2[:, :], everywhere(ln2_g[0], D)).then_inc(s_vec2, 16)
            sp.dma_start(shift2[:, :], everywhere(ln2_b[0], D)).then_inc(s_vec2, 16)

            sp.wait_ge(s_passes, 1)
            n_passes = sp.value_load(passes_i[0:1, 0:1], min_val=0, max_val=S // SLOTS)
            with sp.If(n_passes > 1):
                with sp.Fori(1, n_passes) as ps:
                    with sp.Fori(0, E) as e:
                        sp.wait_ge(s_dn, E * ps + e)
                        sp.nop(nofuse=True)
                        expert_weights(0, e)
            with sp.Else():
                sp.nop(nofuse=True)

            sp.wait_ge(s_all, 1)
            for t in range(T):
                sp.dma_start(first_y[:, t, :], y_v[:, 0, t, :]).then_inc(s_first[t], 16)
                sp.dma_start(second_y[:, t, :], y_v[:, 1, t, :]).then_inc(s_first[t], 16)
            for t in range(T):
                if t < T - 1:
                    sp.wait_ge(s_h, T + t + 1)
                else:
                    sp.wait_ge(s_last, 1)
                sp.dma_start(out_v[:, t, :], hx[:, t, :]).then_inc(s_out, 16)
            sp.wait_ge(s_out, 16 * T)

        @block.gpsimd
        def _(pool):
            pool.memset(ident[:, :], 0.0).then_inc(s_ident, 1)
            pool.wait_ge(s_ident, 1)
            pool.affine_select(out=ident[:, :], in_=ident[:, :], compare_op=ALU.not_equal, fill=1.0, base=0,
                               pattern=[[-1, P]], channel_multiplier=1).then_inc(s_ident, 1)
            pool.memset(causal[:, :], 0.0).then_inc(s_mask, 1)
            pool.wait_ge(s_mask, 1)
            pool.affine_select(out=causal[:, (T - 1) * P:], in_=causal[:, (T - 1) * P:], compare_op=ALU.is_gt,
                               fill=NEG, base=0, pattern=[[-1, P]], channel_multiplier=1).then_inc(s_mask, 1)
            pool.memset(ones[:, :], 1.0).then_inc(s_const, 1)
            pool.iota(iota_i[:, :], pattern=[[1, SLOTS]], base=0, channel_multiplier=0).then_inc(s_const, 1)
            pool.iota(ids_i[:, :, :, 0], pattern=[[0, 2], [P, T]], base=1, channel_multiplier=1).then_inc(s_const, 1)
            pool.iota(ids_i[:, :, :, 1], pattern=[[S, 2], [P, T]], base=1, channel_multiplier=1).then_inc(s_const, 1)
            pool.memset(eps[:, :], LN_EPS).then_inc(s_const, 1)
            pool.wait_ge(s_const, 5)
            pool.affine_select(out=before[:, :], in_=ones[:, :], compare_op=ALU.is_gt, fill=0.0, base=0,
                               pattern=[[1, P]], channel_multiplier=-1).then_inc(s_const, 1)

            def low_part(n, slot):
                pool.wait_ge(s_hi, n + 1)
                nc.gpsimd.tensor_tensor(w_lo[:, slot, :], raw[:, slot, :], w_hi[:, slot, :].bitcast(F32),
                                        ALU.subtract).then_inc(s_lo, 1)

            for n in range(FIRST_QK + 4):
                low_part(n, n % 2)

            def relu(i, o):
                b = ORDER[o]
                u = unit(i, o)
                pool.wait_ge(s_z, u + 1 + CREDIT_Z)
                pool.wait_ge(s_scan, u + CREDIT_SCAN)
                pool.nop(nofuse=True)
                nc.gpsimd.tensor_scalar(R[:, :, 0:W[b]], Z[:, b % 2, :, 0:W[b]], 0.0, None,
                                        ALU.max).then_inc(s_relu, 1)

            with pool.Fori(0, PAIRS_SB) as i:
                relu(i, 0)
                relu(i, 1)
                low_part(FIRST_QK + 4 + 2 * i, 0)
                relu(i, 2)
                relu(i, 3)
                low_part(FIRST_QK + 5 + 2 * i, 1)
            for n in range(FIRST_QK + 4 + 2 * PAIRS_SB, CHUNKS):
                low_part(n, n % 2)

            def shifted(n, vector=shift):
                t = n % T
                pool.wait_ge(s_gain, n + 1)
                nc.gpsimd.tensor_tensor(hx[:, t, :], hx[:, t, :], vector[:, :], ALU.add).then_inc(s_h, 1)

            pool.wait_ge(s_vec, 32)
            for n in range(T):
                shifted(n)

            pool.wait_ge(s_logit, T)
            pool.memset(xe[:, :, :], 0.0).then_inc(s_xe0, 1)
            pool.wait_ge(s_hst, 16 * T)
            pool.wait_ge(s_idx, 1)
            pool.wait_ge(s_xe0, 1)

            def get(a, n, e):
                nc.gpsimd.tensor_copy(idx_get[:, a:a + 1], idx_all[:, 0, ds(e, 1)]).then_inc(s_gidx, 1)
                pool.wait_ge(s_gidx, n + 1)
                pool.nop(nofuse=True)
                pool.indirect_dma_start(
                    out=xe[:, a, :], out_offset=None, in_=h_dram,
                    in_offset=bass.IndirectOffsetOnAxis(ap=idx_get[:, a:a + 1], axis=0), bounds_check=S - 1,
                    oob_is_err=False).then_inc(s_get[a], 16)

            def put(q, n, e):
                nc.gpsimd.tensor_copy(idx_put[:, q:q + 1], idx_all[:, 1, ds(e, 1)]).then_inc(s_pidx, 1)
                pool.wait_ge(s_pidx, n + 1)
                pool.wait_ge(s_yd, n + 1)
                pool.nop(nofuse=True)
                pool.indirect_dma_start(
                    out=y_dram, out_offset=bass.IndirectOffsetOnAxis(ap=idx_put[:, q:q + 1], axis=0),
                    in_=y_rows[0:SLOTS, q, :], in_offset=None, bounds_check=2 * S - 1,
                    oob_is_err=False).then_inc(s_put[q], 16)

            for n in range(XES):
                get(n, n, n)

            def get_again(a, n):
                pool.wait_ge(s_xeT, n - XES + 1)
                pool.nop(nofuse=True)
                get(a, n, n)

            def step(n, r, use, more=True):
                if more:
                    get_again((r + 1) % XES, n + XES + 1)
                if not isinstance(n, int) or n >= 2:
                    pool.wait_ge(s_put[r % 2], 16 * use)
                    pool.nop(nofuse=True)
                put(r % 2, n, n)

            get_again(0, XES)
            for n in range(RING):
                step(n, n, n // 2)
            with pool.Fori(1, EXPERT_ROUNDS - 1) as rd:
                for r in range(RING):
                    step(rd * RING + r, r, rd * (RING // 2) + r // 2)
            for n in range(RING * (EXPERT_ROUNDS - 1), E):
                step(n, n % RING, n // 2, more=n + XES + 1 < E)
            for q in range(2):
                pool.wait_ge(s_put[q], 16 * (E // 2))

            pool.wait_ge(s_passes, 1)
            n_passes = pool.value_load(passes_i[0:1, 0:1], min_val=0, max_val=S // SLOTS)
            with pool.If(n_passes > 1):
                with pool.Fori(1, n_passes) as ps:
                    pool.wait_ge(s_idx, ps + 1)
                    pool.nop(nofuse=True)
                    with pool.Fori(0, E) as e:
                        n = E * ps + e
                        get(0, n, e)
                        put(0, n, e)
                        pool.wait_ge(s_put[0], 16 * n + (16 - 8 * E))
                        pool.nop(nofuse=True)
            with pool.Else():
                pool.nop(nofuse=True)
            pool.sem_inc(s_all, 1)
            pool.wait_ge(s_vec2, 32)
            for n in range(T, 2 * T - 1):
                shifted(n, shift2)

        @block.scalar
        def _(act):
            nc.scalar.preload_act_table_set("natural_log_exp_and_others")
            act.sem_inc(s_wlog, CREDIT_WLOG)
            act.sem_inc(s_scan, CREDIT_SCAN)
            for h in range(2):
                act.sem_inc(s_tr[h], CREDIT_TR)
                act.sem_inc(s_wT[h], CREDIT_WT)
                act.sem_inc(s_pv[h], CREDIT_PV)
            act.sem_inc(s_y, 1)
            act.sem_inc(s_z, CREDIT_Z)
            act.sem_inc(s_yt, 1)
            act.sem_inc(s_yTl, 1)

            def high_part(n, slot, use, used=None):
                act.wait_ge(s_raw[slot], 16 * use + 16)
                if used is not None:
                    act.wait_ge(*used)
                    act.wait_ge(s_lo, n - 1)
                nc.scalar.activation(w_hi[:, slot, :], raw[:, slot, :], ACT.Copy).then_inc(s_hi, 1)

            def turned_x(c):
                act.wait_ge(s_xT, c + 1)
                nc.scalar.activation(xT_hi[:, c, :], bank[:, c, :], ACT.Copy).then_inc(s_xTh, 1)

            for c in range(0, 2):
                turned_x(c)
            high_part(0, 0, 0)
            for c in range(2, 6):
                turned_x(c)
            high_part(1, 1, 0)
            for c in range(6, KD):
                turned_x(c)
            for n in range(2, CHUNKS_V + 1):
                high_part(n, n % 2, n // 2, (s_vused, n - 1))
            act.wait_ge(s_vused, CHUNKS_V)
            for b in (4, 0, 2, 6):
                nc.scalar.activation(values[:, b % 4, (b // 4) * D_SB:(b // 4 + 1) * D_SB], bank[:, b, :],
                                     ACT.Copy).then_inc(s_vout_a, 1)
                if b == 4:
                    high_part(FIRST_QK + 1, 1, FIRST_QK // 2, (s_vused, CHUNKS_V))

            def k_high(i):
                act.wait_ge(s_pk, i + 1)
                if not isinstance(i, int) or i > 0:
                    act.wait_ge(s_sc, unit(i, 0))
                for h in range(2):
                    for half in range(2):
                        ins = nc.scalar.activation(k_hi[half * DH:(half + 1) * DH, h, :],
                                                   PK[h * DH:(h + 1) * DH, :], ACT.Copy)
                    ins.then_inc(s_khi, 1)

            def q_high(i):
                act.wait_ge(s_pq, i + 1)
                for h in range(2):
                    own = slice(h * DH, (h + 1) * DH)
                    ins = nc.scalar.activation(q_both[own, h, :], PQ[own, :], ACT.Copy, scale=SCALE)
                ins.then_inc(s_qhi, 1)

            k_high(0)
            high_part(FIRST_QK + 2, 0, FIRST_QK // 2 + 1, (s_pk, 1))
            q_high(0)
            high_part(FIRST_QK + 3, 1, FIRST_QK // 2 + 1, (s_pq, 1))

            def weights_out(i, o, h=0):
                b, u = ORDER[o], unit(i, o)
                act.wait_ge(s_tr[h], u + 1 + CREDIT_TR)
                act.wait_ge(s_pv[h], u + CREDIT_PV)
                nc.scalar.activation(wT[:, h, 0:W[b]], TR[h][:, 0:W[b]], ACT.Copy).then_inc(s_wT[h], 1)

            def softplus(i, o):
                b, u = ORDER[o], unit(i, o)
                z, l = Z[:, b % 2, :, 0:W[b]], L[:, b % 2, :, 0:W[b]]
                act.wait_ge(s_z, u + 1 + CREDIT_Z)
                act.wait_ge(s_wlog, u + 1)
                nc.scalar.activation(l, z, ACT.Abs).then_inc(s_abs, 1)
                act.wait_ge(s_abs, u + 1)
                nc.scalar.activation(l, l, ACT.Exp, scale=-1.0).then_inc(s_exp, 1)
                act.wait_ge(s_exp, u + 1)
                nc.scalar.activation(l, l, ACT.Ln, bias=1.0).then_inc(s_ln, 1)

            def weights(i, o):
                b, u = ORDER[o], unit(i, o)
                z = Z[:, b % 2, :, 0:W[b]]
                act.wait_ge(s_wlog, u + 1 + CREDIT_WLOG)
                nc.scalar.activation(z, z, ACT.Exp).then_inc(s_p, 1)

            def soft_weights(i, o):
                b, u = ORDER[o], unit(i, o)
                act.wait_ge(s_nmx, u - UNITS * PAIRS_SB + 1)
                for h in range(2):
                    z = Z[:, b % 2, h, 0:W[b]]
                    ins = nc.scalar.activation(z, z, ACT.Exp, bias=nnear[:, b % 2, h:h + 1],
                                               accum_out=psumd[:, b % 2, h:h + 1])
                ins.then_inc(s_p, 1)

            def pair(i, kind, before):
                last = i + (-1)
                if before:
                    weights_out(last, 2)
                    (weights if before == STICK else soft_weights)(last, 3)
                if before:
                    weights_out(last, 3)
                if kind == STICK:
                    softplus(i, 0)
                    softplus(i, 1)
                (weights if kind == STICK else soft_weights)(i, 0)
                ahead = not isinstance(i, int) or i + 1 < PAIRS
                if ahead:
                    high_part(FIRST_QK + 4 + 2 * i, 0, FIRST_QK // 2 + 2 + i, (s_pk, i + 2))
                weights_out(i, 0)
                (weights if kind == STICK else soft_weights)(i, 1)
                if kind == STICK:
                    softplus(i, 2)
                if ahead:
                    k_high(i + 1)
                weights_out(i, 1)
                weights_out(i, 1, h=1)
                if ahead:
                    q_high(i + 1)
                if kind == STICK:
                    softplus(i, 3)
                (weights if kind == STICK else soft_weights)(i, 2)
                if ahead:
                    high_part(FIRST_QK + 5 + 2 * i, 1, FIRST_QK // 2 + 2 + i, (s_pq, i + 2))

            pair(0, STICK, None)
            with act.Fori(1, PAIRS_SB) as i:
                pair(i, STICK, STICK)
            pair(PAIRS_SB, SOFT, STICK)
            with act.Fori(PAIRS_SB + 1, PAIRS - 1) as i:
                pair(i, SOFT, SOFT)
            pair(PAIRS - 1, SOFT, SOFT)
            weights_out(PAIRS - 1, 2)
            soft_weights(PAIRS - 1, 3)
            weights_out(PAIRS - 1, 3)
            for n in range(FIRST_OUT + 2, CHUNKS):
                high_part(n, n % 2, n // 2, (s_oused, n - 1 - FIRST_OUT))

            def centre(n):
                t = n % T
                act.wait_ge(s_mean, n + 1)
                nc.scalar.activation(hx[:, t, :], hx[:, t, :], ACT.Identity, bias=nmean[:, n:n + 1]
                                     ).then_inc(s_centred, 1)
                act.wait_ge(s_centred, n + 1)
                if n % T >= 2:
                    act.wait_ge(s_sq, n - 1)
                nc.scalar.activation(squares[:, t % 2, :], hx[:, t, :], ACT.Square,
                                     accum_out=row_sq[:, n:n + 1]).then_inc(s_sq, 1)

            def root(n):
                act.wait_ge(s_sq, n + 1)
                nc.scalar.activation(std[:, n:n + 1], row_sq[:, n:n + 1], ACT.Sqrt, bias=eps[:, 0:1], scale=1.0 / D
                                     ).then_inc(s_sqrt, 1)

            def centre_and_root(first):
                for n in range(first, first + T):
                    centre(n)
                    root(n)

            centre_and_root(0)
            for t in range(T):
                act.wait_ge(s_hT, t + 1)
                nc.scalar.activation(hT[:, 0:KD // 2, t * P:(t + 1) * P],
                                     bank[:, 2 * t, :].rearrange("p (c s) -> p c s", c=KD // 2), ACT.Copy
                                     ).then_inc(s_hTe_act, 1)
            act.wait_ge(s_route, 3)
            nc.scalar.activation(gexp[:, :, :], gdif[:, :, :], ACT.Exp).then_inc(s_gexp, 1)
            act.wait_ge(s_eexp, 1)
            nc.scalar.activation(eexp[:, :], edif[:, :], ACT.Exp).then_inc(s_eexp, 1)

            act.wait_ge(s_hst, 16 * T)
            act.wait_ge(s_hT, T)
            for t in range(T):
                nc.scalar.activation(hx[:, t, :], hx[:, t, :], ACT.Copy, scale=ALPHA).then_inc(s_scaled, 1)

            def down_high(n, r, use):
                act.wait_ge(s_down_w[r], 16 * use + 16)
                if not isinstance(n, int) or n >= 1:
                    act.wait_ge(s_dn, n)
                else:
                    act.wait_ge(s_h, T)
                nc.scalar.activation(down_hi[:, :, :], down_w[r][:, :, :], ACT.Copy).then_inc(s_dhi, 1)

            def silu(q, n):
                act.wait_ge(s_gu, n + 1)
                if not isinstance(n, int) or n >= 2:
                    act.wait_ge(s_prod, n - 1)
                nc.scalar.activation(silu_g[:, q, :, :], GU[q][:, 0:FB, :], ACT.Silu).then_inc(s_silu, 1)

            def rows_low(q, n, put_uses):
                act.wait_ge(s_dn, n + 1)
                if not isinstance(n, int) or n >= 2:
                    act.wait_ge(s_put[q], 16 * put_uses)
                nc.scalar.activation(y_rows[0:SLOTS, q, :].rearrange("p (j n) -> p j n", j=2),
                                     DN[q][SLOTS:2 * SLOTS, :, :], ACT.Copy).then_inc(s_ya, 1)

            def step(n, r, q, use, put_uses, more=True):
                if more:
                    down_high(n + 1, r, use)
                    silu(1 - q, n + 1)
                rows_low(q, n, put_uses)

            act.wait_ge(s_scaled, T)
            down_high(0, 0, 0)
            silu(0, 0)
            for n in range(RING):
                step(n, (n + 1) % RING, n % 2, (n + 1) // RING, n // 2)
            with act.Fori(1, EXPERT_ROUNDS) as rd:
                for r in range(RING):
                    step(rd * RING + r, (r + 1) % RING, r % 2, rd + (r + 1) // RING, rd * (RING // 2) + r // 2)
            for n in range(RING * EXPERT_ROUNDS, E):
                step(n, (n + 1) % RING, n % 2, (n + 1) // RING, n // 2, more=n + 1 < E)
            act.wait_ge(s_passes, 1)
            n_passes = act.value_load(passes_i[0:1, 0:1], min_val=0, max_val=S // SLOTS)
            with act.If(n_passes > 1):
                with act.Fori(1, n_passes) as ps:
                    with act.Fori(0, E) as e:
                        n = E * ps + e
                        down_high(n, 0, n - E + slot0_uses)
                        silu(0, n)
                        rows_low(0, n, n + (-E // 2))
            with act.Else():
                act.nop(nofuse=True)
            centre_and_root(T)

        @block.vector
        def _(dve):
            dve.wait_ge(s_rb, 16)
            nc.vector.tensor_copy(line[:, 0:S - 1 - CLIP], rb[:, REL - 1:REL].to_broadcast([HEADS_CA, S - 1 - CLIP])
                                  ).then_inc(s_line, 1)
            nc.vector.tensor_copy(line[:, S - 1 - CLIP:LINE], rb[:, REL - 1:REL - 1 - (LINE - (S - 1 - CLIP)):-1]
                                  ).then_inc(s_line, 1)
            for c in range(KD):
                dve.wait_ge(s_xTh, c + 1)
                nc.vector.tensor_tensor(xT_lo[:, c, :], bank[:, c, :], xT_hi[:, c, :].bitcast(F32),
                                        ALU.subtract).then_inc(s_xTl, 1)
            dve.wait_ge(s_bias, 16)
            nc.vector.memset(bias[0:P // 2, :, S - P // 2:], NEG).then_inc(s_bmask, 1)
            dve.wait_ge(s_const, 2)
            nc.vector.tensor_copy(iota_f[:, :], iota_i[:, :]).then_inc(s_bmask, 1)
            dve.wait_ge(s_bmask, 2)
            nc.vector.tensor_scalar(iota_big[:, :], iota_f[:, 0:EG], BIG, None, ALU.add).then_inc(s_bmask, 1)
            dve.wait_ge(s_const, 4)
            nc.vector.tensor_copy(ids_f[:, :, :, :], ids_i[:, :, :, :]).then_inc(s_bmask, 1)
            dve.wait_ge(s_vused, CHUNKS_V)
            for b in (5, 1, 3, 7):
                nc.vector.tensor_copy(values[:, b % 4, (b // 4) * D_SB:(b // 4 + 1) * D_SB], bank[:, b, :]
                                      ).then_inc(s_vout_d, 1)

            def q_out(i):
                dve.wait_ge(s_qhi, i + 1)
                for h in range(2):
                    own, other = slice(h * DH, (h + 1) * DH), slice((1 - h) * DH, (2 - h) * DH)
                    ins = nc.vector.scalar_tensor_tensor(out=q_both[other, h, :], in0=PQ[own, :], scalar=SCALE,
                                                         in1=q_both[own, h, :].bitcast(F32), op0=ALU.mult,
                                                         op1=ALU.subtract)
                ins.then_inc(s_q, 1)

            def k_out(i):
                for h in range(2):
                    dve.wait_ge(s_khi, 2 * i + (h + 1))
                    own = slice(h * DH, (h + 1) * DH)
                    for half in range(2):
                        ins = nc.vector.tensor_tensor(k_lo[half * DH:(half + 1) * DH, h, :], PK[own, :],
                                                      k_hi[own, h, :].bitcast(F32), ALU.subtract)
                ins.then_inc(s_k, 1)

            k_out(0)
            q_out(0)

            def weights_out(i, o, h=1):
                b, u = ORDER[o], unit(i, o)
                dve.wait_ge(s_tr[h], u + 1 + CREDIT_TR)
                dve.wait_ge(s_pv[h], u + CREDIT_PV)
                nc.vector.tensor_copy(wT[:, h, 0:W[b]], TR[h][:, 0:W[b]]).then_inc(s_wT[h], 1)

            def z_free(u):
                dve.wait_ge(s_tr[1], u + 1)

            def masked(i, o):
                b, u = ORDER[o], unit(i, o)
                dve.wait_ge(s_sc, u + 1)
                z_free(u)
                nc.vector.tensor_tensor(Z[:, b % 2, :, 0:W[b]], SC[:, :, 0:W[b]],
                                        causal[:, S - W[b]:].unsqueeze(1).broadcast_to([P, 2, W[b]]),
                                        ALU.add).then_inc(s_z, 1)

            def later_sum(i, o):
                b, u = ORDER[o], unit(i, o)
                dve.wait_ge(s_ln, u + 1)
                dve.wait_ge(s_relu, u + 1)
                for h in range(2):
                    l, r = L[:, b % 2, h, 0:W[b]][:, ::-1], R[:, h, 0:W[b]][:, ::-1]
                    ins = nc.vector.tensor_tensor_scan(l, l, r, 0.0, ALU.add, ALU.add)
                ins.then_inc(s_scan, 1)
                dve.wait_ge(s_scan, u + 1 + CREDIT_SCAN)
                z = Z[:, b % 2, :, 0:W[b]]
                nc.vector.tensor_tensor(z, z, L[:, b % 2, :, 0:W[b]], ALU.subtract).then_inc(s_wlog, 1)

            def y_out(i, kind):
                for h in range(2):
                    dve.wait_ge(s_pv[h], unit(i + 1, 0) + CREDIT_PV)
                dve.wait_ge(s_yt, i + 1)
                if kind == STICK:
                    nc.vector.tensor_copy(y_pair[:, :, :].rearrange("p t n -> p (t n)"), PV).then_inc(s_y, 1)
                else:
                    dve.wait_ge(s_inv, unit(i + 1, 0) - first_u)
                    nc.vector.tensor_tensor(y_pair[:, :, :].rearrange("p t (h d) -> p t h d", h=2),
                                            PV.rearrange("p (t h d) -> p t h d", t=T, h=2),
                                            pinv[:, :, :].unsqueeze(3).broadcast_to([P, T, 2, DH]),
                                            ALU.mult).then_inc(s_y, 1)

            def pair_out(i):
                dve.wait_ge(s_yt, i + 2)
                nc.vector.tensor_scalar(yT_hi[:, ds(i, 1), :].rearrange("p c s -> p (c s)"), YT, 1.0, None,
                                        ALU.mult).then_inc(s_yTh, 1)
                dve.wait_ge(s_yTh, i + 1)
                nc.vector.tensor_tensor(yT_lo[:, ds(i, 1), :].rearrange("p c s -> p (c s)"), YT,
                                        yT_hi[:, ds(i, 1), :].rearrange("p c s -> p (c s)").bitcast(F32),
                                        ALU.subtract).then_inc(s_yTl, 1)

            dve.wait_ge(s_mask, 2)
            dve.wait_ge(s_line_out, 16)
            first_u = UNITS * PAIRS_SB

            def biased(i, o):
                b, u = ORDER[o], unit(i, o)
                dve.wait_ge(s_sc, u + 1)
                z_free(u)
                heads = bias[:, ds(2 * i - 2 * PAIRS_SB, 2), S - W[b]:]
                nc.vector.tensor_tensor(Z[:, b % 2, :, 0:W[b]], SC[:, :, 0:W[b]], heads, ALU.add).then_inc(s_z, 1)

            def maximum(i, o):
                b, u = ORDER[o], unit(i, o)
                dve.wait_ge(s_z, u + 1 + CREDIT_Z)
                nc.vector.tensor_reduce(near[:, b % 2, :], Z[:, b % 2, :, 0:W[b]], AX.X, ALU.max).then_inc(s_mx, 1)
                dve.wait_ge(s_mx, u - first_u + 1)
                nc.vector.tensor_scalar(nnear[:, b % 2, :], near[:, b % 2, :], -1.0, None, ALU.mult
                                        ).then_inc(s_nmx, 1)

            def inverse(i, o):
                b, u = ORDER[o], unit(i, o)
                if o == 0:
                    dve.wait_ge(s_y, i + 1)
                dve.wait_ge(s_p, u + 1)
                nc.vector.reciprocal(pinv[:, b, :], psumd[:, b % 2, :]).then_inc(s_inv, 1)

            def pair(i, kind, before):
                def scores_out(i, o, between=None):
                    (masked if kind == STICK else biased)(i, o)
                    if between is not None:
                        q_out(between)
                    if kind == SOFT:
                        maximum(i, o)

                last = i + (-1)
                if before == STICK:
                    later_sum(last, 3)
                if before:
                    weights_out(last, 2)
                scores_out(i, 0)
                if before == SOFT:
                    inverse(last, 3)
                if before:
                    weights_out(last, 3)
                scores_out(i, 1)
                if before:
                    y_out(last, before)
                if kind == STICK:
                    later_sum(i, 0)
                    later_sum(i, 1)
                else:
                    inverse(i, 0)
                if kind == STICK:
                    scores_out(i, 2)
                    weights_out(i, 0)
                else:
                    weights_out(i, 0)
                    scores_out(i, 2)
                if before:
                    pair_out(last)
                if kind == SOFT:
                    inverse(i, 1)
                ahead = not isinstance(i, int) or i + 1 < PAIRS
                if ahead:
                    k_out(i + 1)
                scores_out(i, 3, between=i + 1 if ahead else None)
                (later_sum if kind == STICK else inverse)(i, 2)

            pair(0, STICK, None)
            with dve.Fori(1, PAIRS_SB) as i:
                pair(i, STICK, STICK)
            dve.wait_ge(s_bmask, 4)
            pair(PAIRS_SB, SOFT, STICK)
            with dve.Fori(PAIRS_SB + 1, PAIRS - 1) as i:
                pair(i, SOFT, SOFT)
            pair(PAIRS - 1, SOFT, SOFT)
            weights_out(PAIRS - 1, 2)
            inverse(PAIRS - 1, 3)
            weights_out(PAIRS - 1, 3)
            y_out(PAIRS - 1, SOFT)
            pair_out(PAIRS - 1)

            def mean(n):
                dve.wait_ge(s_res, n + 1)
                nc.vector.tensor_scalar(nmean[:, n:n + 1], row_sum[:, n:n + 1], -1.0 / D, None, ALU.mult
                                        ).then_inc(s_mean, 1)

            def scaled(n, vector=gain):
                t = n % T
                dve.wait_ge(s_sqrt, n + 1)
                nc.vector.reciprocal(rstd[:, n:n + 1], std[:, n:n + 1]).then_inc(s_rstd, 1)
                dve.wait_ge(s_rstd, n + 1)
                nc.vector.scalar_tensor_tensor(out=hx[:, t, :], in0=hx[:, t, :], scalar=rstd[:, n:n + 1],
                                               in1=vector[:, :], op0=ALU.mult, op1=ALU.mult).then_inc(s_gain, 1)

            dve.wait_ge(s_vec, 32)
            for t in range(T):
                dve.wait_ge(s_mix, t + 1)
                nc.vector.scalar_tensor_tensor(out=hx[:, t, :], in0=hx[:, t, :], scalar=ALPHA,
                                               in1=bank[:, 2 * t:2 * t + 2, :].rearrange("p b n -> p (b n)"),
                                               op0=ALU.mult, op1=ALU.add, accum_out=row_sum[:, t:t + 1]
                                               ).then_inc(s_res, 1)
                mean(t)
                if t >= 2:
                    scaled(t - 2)
            def half_hT(t):
                dve.wait_ge(s_hT, t + 1)
                nc.vector.tensor_copy(hT[:, KD // 2:, t * P:(t + 1) * P],
                                      bank[:, 2 * t + 1, :].rearrange("p (c s) -> p c s", c=KD // 2)
                                      ).then_inc(s_hTe_dve, 1)

            scaled(T - 2)
            half_hT(0)
            scaled(T - 1)
            for t in range(1, T):
                half_hT(t)

            steps = [0]

            def then(ins):
                steps[0] += 1
                ins.then_inc(s_route, 1)
                dve.wait_ge(s_route, steps[0])

            def across(a, n):
                return a.unsqueeze(2).broadcast_to([P, T, n])

            def iota(n):
                return iota_f[:, 0:n].unsqueeze(1).broadcast_to([P, T, n])

            def first_max(values_, best, index, n):
                then(nc.vector.tensor_tensor(same[:, :, 0:n], values_, across(best, n), ALU.is_equal))
                then(nc.vector.scalar_tensor_tensor(
                    out=cand[:, :, 0:n], in0=same[:, :, 0:n], scalar=-BIG,
                    in1=iota_big[:, 0:n].unsqueeze(1).broadcast_to([P, T, n]), op0=ALU.mult, op1=ALU.add))
                then(nc.vector.tensor_reduce(index, cand[:, :, 0:n], AX.X, ALU.min))

            dve.wait_ge(s_logit, T)
            dve.wait_ge(s_rw, 16 * (3 + G))
            LG = bank[:, 0, 0:T * (G + E)].rearrange("p (t n) -> p t n", t=T)
            then(nc.vector.tensor_tensor(logit[:, :, :], LG, b_route[:, :].unsqueeze(1).broadcast_to([P, T, G + E]),
                                         ALU.add))
            glog = logit[:, :, 0:G]
            then(nc.vector.tensor_reduce(gmax[:, :], glog, AX.X, ALU.max))
            then(nc.vector.tensor_tensor(gdif[:, :, :], glog, across(gmax[:, :], G), ALU.subtract))
            first_max(glog, gmax[:, :], gidx[:, :], G)
            then(nc.vector.tensor_tensor(gone[:, :, :], iota(G), across(gidx[:, :], G), ALU.is_equal))
            then(nc.vector.tensor_tensor(picked[:, :, :, :],
                                         logit[:, :, G:].rearrange("p t (g e) -> p t g e", g=G),
                                         gone[:, :, :].unsqueeze(3).broadcast_to([P, T, G, EG]), ALU.mult))
            then(nc.vector.tensor_reduce(elog[:, :, :], picked[:, :, :, :].rearrange("p t g e -> p t e g"),
                                         AX.X, ALU.add))
            then(nc.vector.tensor_reduce(emax[:, 0, :], elog[:, :, :], AX.X, ALU.max))
            first_max(elog[:, :, :], emax[:, 0, :], eidx[:, 0, :], EG)
            then(nc.vector.tensor_tensor(eone[:, :, :], iota(EG), across(eidx[:, 0, :], EG), ALU.is_equal))
            then(nc.vector.scalar_tensor_tensor(out=elog[:, :, :], in0=eone[:, :, :], scalar=NEG, in1=elog[:, :, :],
                                                op0=ALU.mult, op1=ALU.add))
            then(nc.vector.tensor_reduce(emax[:, 1, :], elog[:, :, :], AX.X, ALU.max))
            first_max(elog[:, :, :], emax[:, 1, :], eidx[:, 1, :], EG)
            nc.vector.tensor_tensor(edif[:, :], emax[:, 1, :], emax[:, 0, :], ALU.subtract).then_inc(s_eexp, 1)
            then(nc.vector.scalar_tensor_tensor(
                out=expert[:, :, :], in0=gidx[:, :].unsqueeze(1).broadcast_to([P, 2, T]), scalar=float(EG),
                in1=eidx[:, :, :], op0=ALU.mult, op1=ALU.add))
            for k in range(2):
                ins = nc.vector.tensor_tensor(chosen[:, k, :, :], iota(E), across(expert[:, k, :], E), ALU.is_equal)
            then(ins)
            nc.vector.tensor_tensor(chosen_b[:, :, :], chosen[:, 0, :, :], chosen[:, 1, :, :], ALU.add
                                    ).then_inc(s_onehot, 1)
            then(nc.vector.tensor_tensor(
                ids_at[:, :, :, :],
                chosen[:, :, :, :].rearrange("p k t e -> p (k t) e").unsqueeze(2).broadcast_to([P, 2 * T, 2, E]),
                ids_f[:, :, :, :].rearrange("p k t c -> p (k t) c").unsqueeze(3).broadcast_to([P, 2 * T, 2, E]),
                ALU.mult))
            dve.wait_ge(s_rank, 1)
            RK = bank[:, 1, 0:T * E].rearrange("p (t e) -> p t e", t=T)
            for k in range(2):
                ins = nc.vector.tensor_tensor(ranked[:, k, :, :], chosen[:, k, :, :], RK, ALU.mult)
            then(ins)
            then(nc.vector.tensor_reduce(rank[:, :, :], ranked[:, :, :, :], AX.X, ALU.add))

            def fill_slots(ps):
                nc.vector.tensor_tensor(
                    at_rank[:, :, :], iota_f[:, :].unsqueeze(1).broadcast_to([P, 2 * T, SLOTS]),
                    rank[:, :, :].rearrange("p k t -> p (k t)").unsqueeze(2).broadcast_to([P, 2 * T, SLOTS]),
                    ALU.is_equal).then_inc(s_slots, 1)
                dve.wait_ge(s_slotted, ps + 1)
                found = bank[0:SLOTS, 7, 0:2 * E].rearrange("p (c e) -> p c e", c=2)
                nc.vector.tensor_scalar(empty[:, :, :], found, 0.0, float(FAR), ALU.is_equal, ALU.mult
                                        ).then_inc(s_empty, 1)
                dve.wait_ge(s_empty, ps + 1)
                nc.vector.scalar_tensor_tensor(out=idx_all[:, :, :], in0=found, scalar=-1.0, in1=empty[:, :, :],
                                               op0=ALU.add, op1=ALU.add).then_inc(s_idx, 1)

            fill_slots(0)
            then(nc.vector.tensor_reduce(count_f[:, :], bank[:, 2, 0:E], AX.X, ALU.max))
            then(nc.vector.tensor_scalar(count_i[:, :], count_f[:, :], float(SLOTS - 1), None, ALU.add))
            nc.vector.tensor_single_scalar(passes_i[:, :], count_i[:, :], SLOTS.bit_length() - 1,
                                           ALU.logical_shift_right).then_inc(s_passes, 1)
            dve.wait_ge(s_gexp, 1)
            then(nc.vector.tensor_reduce(gsum[:, :], gexp[:, :, :], AX.X, ALU.add))
            then(nc.vector.reciprocal(gprob[:, :], gsum[:, :]))
            dve.wait_ge(s_eexp, 2)
            then(nc.vector.tensor_scalar(esum[:, :], eexp[:, :], 1.0, None, ALU.add))
            then(nc.vector.reciprocal(einv[:, :], esum[:, :]))
            then(nc.vector.tensor_tensor(gate[:, 0, :], einv[:, :], gprob[:, :], ALU.mult))
            then(nc.vector.tensor_tensor(gate[:, 1, :], eexp[:, :], gate[:, 0, :], ALU.mult))

            def step(q, n):
                dve.wait_ge(s_xeT, n + 1)
                wait_gu(n)
                nc.vector.tensor_copy(xeT[:, q, :, :], XE).then_inc(s_xeTs, 1)

            def wait_gu(n):
                if not isinstance(n, int) or n >= 2:
                    dve.wait_ge(s_gu, n - 1)

            def finish(q, n):
                dve.wait_ge(s_silu, n + 1)
                if not isinstance(n, int) or n >= 2:
                    dve.wait_ge(s_dn, n - 1)
                nc.vector.tensor_tensor(hid[:, q, :, :], silu_g[:, q, :, :], GU[q][:, FB:, :], ALU.mult
                                        ).then_inc(s_prod, 1)
                dve.wait_ge(s_prod, n + 1)
                nc.vector.tensor_scalar(hid_both[:, q, :, 0:SLOTS], hid[:, q, :, :], 1.0, None, ALU.mult
                                        ).then_inc(s_hid_hi, 1)
                dve.wait_ge(s_hid_hi, n + 1)
                nc.vector.tensor_tensor(hid_both[:, q, :, SLOTS:], hid[:, q, :, :],
                                        hid_both[:, q, :, 0:SLOTS].bitcast(F32), ALU.subtract).then_inc(s_hid, 1)

            def down_low(n, r):
                dve.wait_ge(s_dhi, n + 1)
                nc.vector.tensor_tensor(down_lo[r][:, :, :], down_w[r][:, :, :], down_hi[:, :, :].bitcast(F32),
                                        ALU.subtract).then_inc(s_dlo, 1)

            def rows_out(q, n):
                dve.wait_ge(s_ya, n + 1)
                rows = y_rows[0:SLOTS, q, :].rearrange("p (j n) -> p j n", j=2)
                nc.vector.tensor_tensor(rows, rows, DN[q][0:SLOTS, :, :], ALU.add).then_inc(s_yd, 1)

            def expert_step(n, r, q, left=2):
                if left >= 2:
                    step(q, n + 2)
                if left >= 1:
                    down_low(n + 1, r)
                    finish(1 - q, n + 1)
                rows_out(q, n)

            step(0, 0)
            down_low(0, 0)
            step(1, 1)
            finish(0, 0)
            for n in range(RING):
                expert_step(n, (n + 1) % RING, n % 2)
            with dve.Fori(1, EXPERT_ROUNDS) as rd:
                for r in range(RING):
                    expert_step(rd * RING + r, (r + 1) % RING, r % 2)
            for n in range(RING * EXPERT_ROUNDS, E):
                expert_step(n, (n + 1) % RING, n % 2, left=E - 1 - n)
            n_passes = dve.value_load(passes_i[0:1, 0:1], min_val=0, max_val=S // SLOTS)
            with dve.If(n_passes > 1):
                with dve.Fori(1, n_passes) as ps:
                    dve.wait_ge(s_put[0], 16 * E * ps + (-8 * E))
                    dve.wait_ge(s_put[1], 16 * (E // 2))
                    nc.vector.tensor_scalar(rank[:, :, :], rank[:, :, :], float(-SLOTS), None, ALU.add
                                            ).then_inc(s_lower, 1)
                    dve.wait_ge(s_lower, ps)
                    fill_slots(ps)
                    with dve.Fori(0, E) as e:
                        n = E * ps + e
                        step(0, n)
                        down_low(n, 0)
                        finish(0, n)
                        rows_out(0, n)
            with dve.Else():
                dve.nop(nofuse=True)

            dve.wait_ge(s_scaled, T)
            dve.wait_ge(s_vec2, 32)

            def add_first(t):
                dve.wait_ge(s_first[t], 32)
                nc.vector.scalar_tensor_tensor(out=hx[:, t, :], in0=first_y[:, t, :], scalar=gate[:, 0, t:t + 1],
                                               in1=hx[:, t, :], op0=ALU.mult, op1=ALU.add).then_inc(s_res1, 1)

            add_first(0)
            for t in range(T):
                n = T + t
                dve.wait_ge(s_res1, t + 1)
                nc.vector.scalar_tensor_tensor(out=hx[:, t, :], in0=second_y[:, t, :], scalar=gate[:, 1, t:t + 1],
                                               in1=hx[:, t, :], op0=ALU.mult, op1=ALU.add,
                                               accum_out=row_sum[:, n:n + 1]).then_inc(s_res, 1)
                mean(n)
                if t + 1 < T:
                    add_first(t + 1)
                if t >= 1:
                    scaled(n - 1, gain2)
            scaled(2 * T - 1, gain2)
            dve.wait_ge(s_gain, 2 * T)
            nc.vector.tensor_tensor(hx[:, T - 1, :], hx[:, T - 1, :], shift2[:, :], ALU.add).then_inc(s_last, 1)

        @block.tensor
        def _(pe):
            pe.wait_ge(s_ident, 2)
            for c in range(KD):
                for t in range(T):
                    if c == 0:
                        pe.wait_ge(s_x[t], 16)
                    mm = nc.tensor.transpose(bank[:, c, t * P:(t + 1) * P], hx[:, t, c * P:(c + 1) * P], ident[:, :])
                mm.then_inc(s_xT, 1)

            def split_products(dst, a_hi, a_lo, b_hi, b_lo, start, stop):
                nc.tensor.matmul(dst, a_hi, b_hi, start=start, stop=False)
                nc.tensor.matmul(dst, a_lo, b_hi, start=False, stop=False)
                return nc.tensor.matmul(dst, a_hi, b_lo, start=False, stop=stop)

            for c in range(KD):
                pe.wait_ge(s_lo, c + 1)
                for g in range(2):
                    for t in range(T):
                        if c == 0:
                            pe.wait_ge(s_xTl, 4 * g + t + 1)
                        a = slice(t * P, (t + 1) * P)
                        n = slice(g * D_SB, (g + 1) * D_SB)
                        mm = split_products(bank[:, 4 * g + t, :], xT_hi[:, c, a], xT_lo[:, c, a],
                                            w_hi[:, c % 2, n], w_lo[:, c % 2, n], c == 0, c == KD - 1)
                mm.then_inc(s_vused, 1)

            def project(dst, n, slot, cs, done):
                if cs.start == 0:
                    pe.wait_ge(s_lo, n + 1)
                for c in range(KD)[cs]:
                    w = slice(c * P, (c + 1) * P)
                    mm = split_products(dst, w_hi[:, slot, w], w_lo[:, slot, w], xT_hi[:, c, :], xT_lo[:, c, :],
                                        c == 0, c == KD - 1)
                if cs.stop == KD:
                    mm.then_inc(done, 1)

            def project_q(i, part):
                if part == 0 and not (isinstance(i, int) and i == 0):
                    pe.wait_ge(s_q, i)
                project(PQ, FIRST_QK + 1 + 2 * i, 1, slice(2 * part, 2 * part + 2), s_pq)

            def project_k(i, part):
                if part == 0 and not (isinstance(i, int) and i == 0):
                    pe.wait_ge(s_k, i)
                project(PK, FIRST_QK + 2 * i, 0, slice(2 * part, 2 * part + 2), s_pk)

            def scores(i, o):
                b, u = ORDER[o], unit(i, o)
                if o == 0:
                    pe.wait_ge(s_q, i + 1)
                    pe.wait_ge(s_k, i + 1)
                pe.wait_ge(s_z, u + CREDIT_Z)
                for h in range(2):
                    q = q_both[:, h, b * P:(b + 1) * P]
                    nc.tensor.matmul(SC[:, h, 0:W[b]], q, k_hi[:, h, 0:W[b]], start=True, stop=False)
                    mm = nc.tensor.matmul(SC[:, h, 0:W[b]], q, k_lo[:, h, 0:W[b]], start=False, stop=True)
                mm.then_inc(s_sc, 1)

            def turn(i, o):
                b, u = ORDER[o], unit(i, o)
                pe.wait_ge(s_p, u + 1)
                for h in range(2):
                    pe.wait_ge(s_wT[h], u + CREDIT_WT)
                    for j in range(b + 1):
                        keys = slice(j * P, (j + 1) * P)
                        mm = nc.tensor.transpose(TR[h][:, keys], Z[:, b % 2, h, keys], ident[:, :])
                    mm.then_inc(s_tr[h], 1)

            def combine(i, o):
                b, u = ORDER[o], unit(i, o)
                if o == 0:
                    pe.wait_ge(s_y, i + 1)
                for h in range(2):
                    pe.wait_ge(s_wT[h], u + 1 + CREDIT_WT)
                    for j in range(b + 1):
                        v = values[:, j, ds(i * P + h * DH, DH)] if not isinstance(i, int) else \
                            values[:, j, i * P + h * DH:i * P + (h + 1) * DH]
                        mm = nc.tensor.matmul(PV[:, b * P + h * DH:b * P + (h + 1) * DH],
                                              wT[:, h, j * P:(j + 1) * P], v, start=(j == 0), stop=(j == b))
                    mm.then_inc(s_pv[h], 1)

            def turn_y(i):
                pe.wait_ge(s_y, i + 2)
                pe.wait_ge(s_yTl, i + 1)
                for t in range(T):
                    mm = nc.tensor.transpose(YT[:, t * P:(t + 1) * P], y_pair[:, t, :], ident[:, :])
                mm.then_inc(s_yt, 1)

            pe.wait_ge(s_vout_a, 1)
            pe.wait_ge(s_vout_d, 1)
            for part in range(4):
                project_k(0, part)
            for part in range(4):
                project_q(0, part)
            pe.wait_ge(s_vout_a, 4)
            pe.wait_ge(s_vout_d, 4)

            EARLY_TILE, EARLY_CHUNKS = 2, 2

            def out_products(t, c):
                for j in range(2):
                    a = slice(t * P, (t + 1) * P)
                    n = slice(j * 512, (j + 1) * 512)
                    mm = split_products(bank[:, 2 * t + j, :], yT_hi[:, c, a], yT_lo[:, c, a],
                                        w_hi[:, c % 2, n], w_lo[:, c % 2, n], c == 0, c == KD - 1)
                return mm

            def early_out(c):
                pe.wait_ge(s_lo, FIRST_OUT + c + 1)
                if c == 0:
                    pe.wait_ge(s_q, PAIRS)
                    pe.wait_ge(s_k, PAIRS)
                out_products(EARLY_TILE, c)

            def pair(i, kind, before):
                last = i + (-1)
                ahead = not isinstance(i, int) or i + 1 < PAIRS

                def fill(project_, *parts):
                    for part in parts if ahead else ():
                        project_(i + 1, part)

                scores(i, 0)
                if not ahead:
                    early_out(0)
                fill(project_k, 0)
                if before:
                    turn(last, 2)
                fill(project_k, 1)
                if before:
                    turn(last, 3)
                    combine(last, 2)
                scores(i, 1)
                if not ahead:
                    early_out(1)
                if before:
                    combine(last, 3)
                fill(project_k, 2, 3)
                if before:
                    turn_y(last)
                fill(project_q, 0, 1)
                turn(i, 0)
                scores(i, 2)
                fill(project_q, 2)
                scores(i, 3)
                combine(i, 0)
                turn(i, 1)
                fill(project_q, 3)
                combine(i, 1)

            pair(0, STICK, None)
            with pe.Fori(1, PAIRS_SB) as i:
                pair(i, STICK, STICK)
            pair(PAIRS_SB, SOFT, STICK)
            with pe.Fori(PAIRS_SB + 1, PAIRS - 1) as i:
                pair(i, SOFT, SOFT)
            pair(PAIRS - 1, SOFT, SOFT)
            turn(PAIRS - 1, 2)
            turn(PAIRS - 1, 3)
            combine(PAIRS - 1, 2)
            combine(PAIRS - 1, 3)
            turn_y(PAIRS - 1)

            for c in range(KD):
                if c >= EARLY_CHUNKS:
                    pe.wait_ge(s_lo, FIRST_OUT + c + 1)
                if c == 0:
                    pe.wait_ge(s_yTl, PAIRS + 1)
                for t in range(T):
                    if t != EARLY_TILE or c >= EARLY_CHUNKS:
                        mm = out_products(t, c)
                    if c == KD - 1:
                        mm.then_inc(s_mix, 1)
                if c < KD - 1:
                    mm.then_inc(s_oused, 1)

            def turn_h(t):
                pe.wait_ge(s_h, t + 1)
                for c in range(KD):
                    mm = nc.tensor.transpose(bank[:, 2 * t + c // 4, c % 4 * P:(c % 4 + 1) * P], hx[:, t, c::KD],
                                             ident[:, :])
                mm.then_inc(s_hT, 1)

            def route(t):
                pe.wait_ge(s_hTe_act, t + 1)
                pe.wait_ge(s_hTe_dve, t + 1)
                for c in range(KD):
                    mm = nc.tensor.matmul(bank[:, 0, t * (G + E):(t + 1) * (G + E)], hT[:, c, t * P:(t + 1) * P],
                                          w_route[:, c, :], start=(c == 0), stop=(c == KD - 1))
                mm.then_inc(s_logit, 1)

            pe.wait_ge(s_rw, 16 * (3 + G))
            for t in range(T):
                turn_h(t)
            for t in range(T):
                route(t)
            pe.wait_ge(s_onehot, 1)
            pe.wait_ge(s_const, 6)
            for t in range(T):
                for j in range(t + 1):
                    nc.tensor.matmul(bank[:, 1, t * E:(t + 1) * E], before[:, :] if j == t else ones[:, :],
                                     chosen_b[:, j, :], start=(j == 0), stop=(j == t))
            for t in range(T):
                mm = nc.tensor.matmul(bank[:, 2, 0:E], ones[:, :], chosen_b[:, t, :], start=(t == 0),
                                      stop=(t == T - 1))
            mm.then_inc(s_rank, 1)

            def slots(ps):
                pe.wait_ge(s_slots, ps + 1)
                for j in range(2 * T):
                    mm = nc.tensor.matmul(bank[0:SLOTS, 7, 0:2 * E], at_rank[:, j, :],
                                          ids_at[:, j, :, :].rearrange("p c e -> p (c e)"),
                                          start=(j == 0), stop=(j == 2 * T - 1))
                mm.then_inc(s_slotted, 1)

            slots(0)

            def turn_x(a, n, use):
                pe.wait_ge(s_get[a], 16 * use + 16)
                if not isinstance(n, int) or n > 0:
                    pe.wait_ge(s_xeTs, n)
                    pe.nop(nofuse=True)
                for c in range(KD):
                    mm = nc.tensor.transpose(XE[:, c, :], xe[:, a, c::KD], ident[0:SLOTS, 0:SLOTS])
                mm.then_inc(s_xeT, 1)

            def gate_products(q, n, r, use):
                pe.wait_ge(s_gate_w[r], 16 * use + 16)
                pe.wait_ge(s_xeTs, n + 1)
                if not isinstance(n, int) or n >= 2:
                    pe.wait_ge(s_prod, n - 1)
                for b in range(FB):
                    for c in range(KD):
                        nc.tensor.matmul(GU[q][:, b, :], gate_w[r][:, c, b * P:(b + 1) * P], xeT[:, q, c, :],
                                         start=(c == 0), stop=(c == KD - 1))

            def up_products(q, n, r, use):
                pe.wait_ge(s_up_w[r], 16 * use + 16)
                for b in range(FB):
                    for c in range(KD):
                        mm = nc.tensor.matmul(GU[q][:, FB + b, :], up_w[r][:, c, b * P:(b + 1) * P],
                                              xeT[:, q, c, :], start=(c == 0), stop=(c == KD - 1))
                mm.then_inc(s_gu, 1)

            def down(q, n, r):
                pe.wait_ge(s_hid, n + 1)
                pe.wait_ge(s_dlo, n + 1)
                if not isinstance(n, int) or n >= 2:
                    pe.wait_ge(s_yd, n - 1)
                for j in range(2):
                    cols = slice(j * 512, (j + 1) * 512)
                    for b in range(FB):
                        nc.tensor.matmul(DN[q][:, j, :], hid_both[:, q, b, :], down_hi[:, b, cols],
                                         start=(b == 0), stop=False)
                        mm = nc.tensor.matmul(DN[q][:, j, :], hid_both[:, q, b, :], down_lo[r][:, b, cols],
                                              start=False, stop=(b == FB - 1))
                mm.then_inc(s_dn, 1)

            pe.wait_ge(s_passes, 1)
            turn_x(0, 0, 0)
            gate_products(0, 0, 0, 0)
            up_products(0, 0, 0, 0)
            turn_x(1, 1, 0)

            def expert_step(n, r, q, use, round_, left=2):
                ahead = (1 - q, n + 1, (r + 1) % RING, round_ + (r + 1) // RING)
                if left >= 1:
                    gate_products(*ahead)
                if left >= 2:
                    turn_x((r + 2) % XES, n + 2, use)
                down(q, n, r)
                if left >= 1:
                    up_products(*ahead)

            for r in range(RING):
                expert_step(r, r, r % 2, (r + 2) // XES, 0)
            with pe.Fori(1, EXPERT_ROUNDS) as rd:
                for r in range(RING):
                    expert_step(rd * RING + r, r, r % 2, rd * (RING // XES) + (r + 2) // XES, rd)
            for n in range(RING * EXPERT_ROUNDS, E):
                expert_step(n, n % RING, n % 2, (n + 2) // XES, n // RING, left=E - 1 - n)

            n_passes = pe.value_load(passes_i[0:1, 0:1], min_val=0, max_val=S // SLOTS)
            with pe.If(n_passes > 1):
                with pe.Fori(1, n_passes) as ps:
                    slots(ps)
                    with pe.Fori(0, E) as e:
                        n = E * ps + e
                        turn_x(0, n, n - E + (E + XES - 1) // XES)
                        gate_products(0, n, 0, n - E + slot0_uses)
                        up_products(0, n, 0, n - E + slot0_uses)
                        down(0, n, 0)
            with pe.Else():
                pe.nop(nofuse=True)


_INS = ["x", "w_in", "w_out", "rel_bias", "ln1_g", "ln1_b", "w_group", "b_group", "w_expert", "b_expert",
        "w_gate", "w_up", "w_down", "ln2_g", "ln2_b"]


def kernel(**inputs):
    import numpy as np
    import concourse.bacc as bacc
    from concourse.bass_utils import run_bass_kernel_spmd as run

    nc = bacc.Bacc("TRN2", target_bir_lowering=False, num_devices=1)
    arrays, args = {}, []
    for name in _INS:
        a = np.ascontiguousarray(inputs[name])
        arrays[f"in_{name}"] = a
        args.append(nc.dram_tensor(f"in_{name}", a.shape, F32, kind="ExternalInput").ap())
    out = nc.dram_tensor("out", arrays["in_x"].shape, F32, kind="ExternalOutput").ap()
    build(nc, *args, out)
    return run(nc, [arrays], core_ids=[0]).results[0]["out"]
```
